# Optimizing a Trainium2 kernel written in Bass

```python
import jax, jax.numpy as jnp
from jax import lax
import numpy as np

D_MODEL = 1024
BATCH = 1
SEQ = 512
DEPTH = 2
DEC_BATCH = 8
DEC_SEQ = 4
PAST_LEN = 4096
PAGE_SIZE = 128

HEAD_DIM = 64
N_HEADS = D_MODEL // HEAD_DIM
D_FF = 4 * D_MODEL
D_DECAY_LORA = max(32, int(round(1.8 * D_MODEL ** 0.5 / 32)) * 32)
D_AAA_LORA = max(32, int(round(1.8 * D_MODEL ** 0.5 / 32)) * 32)
D_MV_LORA = max(32, int(round(1.3 * D_MODEL ** 0.5 / 32)) * 32)
D_GATE_LORA = max(32, int(round(0.6 * D_MODEL ** 0.8 / 32)) * 32)
N_MIXERS = 2
N_RWKV = (DEPTH + 1) // 2
N_POOL = DEPTH // 2
POOL_WINDOWS = (2, 4, 8, 16)
N_POOL_GROUPS = len(POOL_WINDOWS)
POOL_GROUP = D_MODEL // N_POOL_GROUPS
POOL_BUF = max(POOL_WINDOWS) - 1
NORM_EPS = 1e-6
GN_EPS = 64e-5
L2_EPS = 1e-12

kernel_name = 'rwkv7_pool_hybrid_step'

def rmsnorm(x, g):
    xf = x.astype(jnp.float32)
    y = xf * lax.rsqrt(jnp.mean(xf * xf, axis=-1, keepdims=True) + NORM_EPS)
    return (y * g).astype(x.dtype)

def wkv7_scan(S0, r, decay, k, v, a_vec, b_vec):
    def step(S, inp):
        r_t, w_t, k_t, v_t, a_t, b_t = inp
        sa = jnp.einsum('bhvk,bhk->bhv', S, a_t)
        S = S * w_t[:, :, None, :] + sa[..., None] * b_t[:, :, None, :] + v_t[..., None] * k_t[:, :, None, :]
        return S, jnp.einsum('bhvk,bhk->bhv', S, r_t)
    seq = tuple(jnp.moveaxis(t, 1, 0) for t in (r, decay, k, v, a_vec, b_vec))
    S, y = lax.scan(step, S0, seq)
    return S, jnp.moveaxis(y, 0, 1)

def rwkv7_time_mix(x, shift_prev, wkv_prev, v_first, vres, mix, w_rkv, w_o, w0, w1, w2,
                   a0, a1, a2, g1, g2, k_k, k_a, r_k, gn_w, gn_b):
    B, T, D = x.shape
    f32 = jnp.float32
    x_prev = jnp.concatenate([shift_prev[:, None, :].astype(x.dtype), x[:, :-1]], axis=1)
    xs = x[:, :, None, :] + (x_prev - x)[:, :, None, :] * mix
    rkv = jnp.einsum('btjc,jcd->btjd', xs[:, :, :3], w_rkv)
    r, k, v = rkv[:, :, 0], rkv[:, :, 1], rkv[:, :, 2]
    xv, xw, xa, xg = xs[:, :, 2], xs[:, :, 3], xs[:, :, 4], xs[:, :, 5]
    w_pre = (w0 + jnp.tanh(xw @ w1) @ w2).astype(f32)
    decay = jnp.exp(-jnp.exp(-jax.nn.softplus(-w_pre) - 0.5))
    if vres is None:
        v_first = v
    else:
        v0, v1, v2 = vres
        v = v + (v_first - v) * jax.nn.sigmoid(v0 + (xv @ v1) @ v2)
    a = jax.nn.sigmoid(a0 + (xa @ a1) @ a2)
    g = jax.nn.sigmoid(xg @ g1) @ g2
    hd = lambda t: t.reshape(B, T, N_HEADS, HEAD_DIM).astype(f32)
    kk = hd(k * k_k)
    kk = kk / jnp.maximum(jnp.sqrt(jnp.sum(kk * kk, axis=-1, keepdims=True)), L2_EPS)
    k = k * (1 + (a - 1) * k_a)
    r_h, k_h, v_h, a_h = hd(r), hd(k), hd(v), hd(a)
    S, y = wkv7_scan(wkv_prev.astype(f32), r_h, hd(decay), k_h, v_h, -kk, kk * a_h)
    mu = jnp.mean(y, axis=-1, keepdims=True)
    var = jnp.mean(jnp.square(y - mu), axis=-1, keepdims=True)
    y = ((y - mu) * lax.rsqrt(var + GN_EPS)).reshape(B, T, D) * gn_w + gn_b
    bonus = jnp.sum(r_h * k_h * r_k, axis=-1, keepdims=True) * v_h
    y = (y + bonus.reshape(B, T, D)).astype(x.dtype)
    out = (y * g) @ w_o
    return out, x[:, -1], S.astype(wkv_prev.dtype), v_first

def pool_mix(x, buf, start_pos, w_pool, pool_scale):
    B, T, D = x.shape
    f32 = jnp.float32
    ext = jnp.concatenate([buf.astype(x.dtype), x], axis=1)
    cs = jnp.cumsum(ext.astype(f32), axis=1)
    cs = jnp.concatenate([jnp.zeros((B, 1, D), f32), cs], axis=1)
    pos = start_pos + jnp.arange(T)
    means = []
    for gi, w in enumerate(POOL_WINDOWS):
        sl = slice(gi * POOL_GROUP, (gi + 1) * POOL_GROUP)
        s = cs[:, POOL_BUF + 1:, sl] - cs[:, POOL_BUF + 1 - w:POOL_BUF + 1 - w + T, sl]
        cnt = jnp.minimum(pos + 1, w).astype(f32)
        means.append(s / cnt[None, :, None])
    pooled = jnp.concatenate(means, axis=-1)
    diff = (pooled - x.astype(f32)).astype(x.dtype).reshape(B, T, N_POOL_GROUPS, POOL_GROUP)
    y = jnp.einsum('btgc,gcd->btgd', diff, w_pool).reshape(B, T, D) * pool_scale
    return y, ext[:, -POOL_BUF:]

def trunk(x, start_pos, shift_states, wkv_states, pool_bufs, p):
    new_shift, new_wkv, new_pool = [], [], []
    v_first = None
    for i in range(DEPTH):
        h = rmsnorm(x, p['norm_mix'][i])
        j = i // N_MIXERS
        if i % N_MIXERS == 0:
            vres = None if j == 0 else (p['v0'][j - 1], p['v1'][j - 1], p['v2'][j - 1])
            out, s_shift, s_wkv, v_first = rwkv7_time_mix(
                h, shift_states[j], wkv_states[j], v_first, vres,
                p['mix'][j], p['w_rkv'][j], p['w_o'][j], p['w0'][j], p['w1'][j], p['w2'][j],
                p['a0'][j], p['a1'][j], p['a2'][j], p['g1'][j], p['g2'][j],
                p['k_k'][j], p['k_a'][j], p['r_k'][j], p['gn_w'][j], p['gn_b'][j])
            new_shift.append(s_shift)
            new_wkv.append(s_wkv)
        else:
            out, s_buf = pool_mix(h, pool_bufs[j], start_pos, p['pool_w'][j], p['pool_scale'][j])
            new_pool.append(s_buf)
        x = x + out
        h = rmsnorm(x, p['norm_ffn'][i])
        x = x + jnp.square(jax.nn.relu(h @ p['ffn_w1'][i])) @ p['ffn_w2'][i]
    y = rmsnorm(x, p['norm_final'])
    return y, jnp.stack(new_wkv), jnp.stack(new_shift), jnp.stack(new_pool)

def setup_inputs(seed: int = 0) -> dict:
    key = jax.random.key(seed)
    ks = jax.random.split(key, 32)
    nrm = lambda k, shape, s: jax.random.normal(k, shape, jnp.float32) * s
    D, H, K = D_MODEL, N_HEADS, HEAD_DIM
    nv = max(N_RWKV - 1, 0)
    return {
        'x_prompt': nrm(ks[0], (BATCH, SEQ, D), 1.0),
        'x_sample': nrm(ks[1], (DEC_BATCH, DEC_SEQ, D), 1.0),
        'state_wkv': nrm(ks[2], (N_RWKV, DEC_BATCH, H, K, K), 0.3),
        'state_shift': nrm(ks[3], (N_RWKV, DEC_BATCH, D), 1.0),
        'state_pool': nrm(ks[4], (N_POOL, DEC_BATCH, POOL_BUF, D), 1.0),
        'norm_mix': 1.0 + nrm(ks[5], (DEPTH, D), 0.05),
        'norm_ffn': 1.0 + nrm(ks[6], (DEPTH, D), 0.05),
        'norm_final': 1.0 + nrm(ks[7], (D,), 0.05),
        'rwkv_mix': jax.random.uniform(ks[8], (N_RWKV, 6, D), jnp.float32),
        'rwkv_w_rkv': nrm(ks[9], (N_RWKV, 3, D, D), D ** -0.5),
        'rwkv_w_o': nrm(ks[10], (N_RWKV, D, D), D ** -0.5),
        'rwkv_w0': jax.random.uniform(ks[11], (N_RWKV, D), jnp.float32, -6.0, -1.0),
        'rwkv_w1': nrm(ks[12], (N_RWKV, D, D_DECAY_LORA), D ** -0.5),
        'rwkv_w2': nrm(ks[13], (N_RWKV, D_DECAY_LORA, D), 0.5 * D_DECAY_LORA ** -0.5),
        'rwkv_a0': nrm(ks[14], (N_RWKV, D), 0.1),
        'rwkv_a1': nrm(ks[15], (N_RWKV, D, D_AAA_LORA), D ** -0.5),
        'rwkv_a2': nrm(ks[16], (N_RWKV, D_AAA_LORA, D), D_AAA_LORA ** -0.5),
        'rwkv_v0': nrm(ks[17], (nv, D), 0.5),
        'rwkv_v1': nrm(ks[18], (nv, D, D_MV_LORA), D ** -0.5),
        'rwkv_v2': nrm(ks[19], (nv, D_MV_LORA, D), D_MV_LORA ** -0.5),
        'rwkv_g1': nrm(ks[20], (N_RWKV, D, D_GATE_LORA), D ** -0.5),
        'rwkv_g2': nrm(ks[21], (N_RWKV, D_GATE_LORA, D), D_GATE_LORA ** -0.5),
        'rwkv_k_k': 0.85 + nrm(ks[22], (N_RWKV, D), 0.1),
        'rwkv_k_a': 1.0 + nrm(ks[23], (N_RWKV, D), 0.1),
        'rwkv_r_k': nrm(ks[24], (N_RWKV, H, K), 0.1),
        'rwkv_gn_w': 1.0 + nrm(ks[25], (N_RWKV, D), 0.05),
        'rwkv_gn_b': nrm(ks[26], (N_RWKV, D), 0.02),
        'pool_w': nrm(ks[27], (N_POOL, N_POOL_GROUPS, POOL_GROUP, POOL_GROUP), POOL_GROUP ** -0.5),
        'pool_scale': 1.0 + nrm(ks[28], (N_POOL, D), 0.1),
        'ffn_w1': nrm(ks[29], (DEPTH, D, D_FF), D ** -0.5),
        'ffn_w2': nrm(ks[30], (DEPTH, D_FF, D), 0.5 * D_FF ** -0.5),
    }

def reference(x_prompt, x_sample, state_wkv, state_shift, state_pool, norm_mix, norm_ffn, norm_final,
              rwkv_mix, rwkv_w_rkv, rwkv_w_o, rwkv_w0, rwkv_w1, rwkv_w2, rwkv_a0, rwkv_a1, rwkv_a2,
              rwkv_v0, rwkv_v1, rwkv_v2, rwkv_g1, rwkv_g2, rwkv_k_k, rwkv_k_a, rwkv_r_k,
              rwkv_gn_w, rwkv_gn_b, pool_w, pool_scale, ffn_w1, ffn_w2):
    p = {'norm_mix': norm_mix, 'norm_ffn': norm_ffn, 'norm_final': norm_final,
         'mix': rwkv_mix, 'w_rkv': rwkv_w_rkv, 'w_o': rwkv_w_o, 'w0': rwkv_w0, 'w1': rwkv_w1,
         'w2': rwkv_w2, 'a0': rwkv_a0, 'a1': rwkv_a1, 'a2': rwkv_a2, 'v0': rwkv_v0, 'v1': rwkv_v1,
         'v2': rwkv_v2, 'g1': rwkv_g1, 'g2': rwkv_g2, 'k_k': rwkv_k_k, 'k_a': rwkv_k_a,
         'r_k': rwkv_r_k, 'gn_w': rwkv_gn_w, 'gn_b': rwkv_gn_b, 'pool_w': pool_w,
         'pool_scale': pool_scale, 'ffn_w1': ffn_w1, 'ffn_w2': ffn_w2}
    dt = x_prompt.dtype
    z_shift = jnp.zeros((N_RWKV, BATCH, D_MODEL), dt)
    z_wkv = jnp.zeros((N_RWKV, BATCH, N_HEADS, HEAD_DIM, HEAD_DIM), dt)
    z_pool = jnp.zeros((N_POOL, BATCH, POOL_BUF, D_MODEL), dt)
    y_prompt, wkv_prompt, shift_prompt, pool_prompt = trunk(x_prompt, 0, z_shift, z_wkv, z_pool, p)
    y_sample, wkv_sample, shift_sample, pool_sample = trunk(
        x_sample, PAST_LEN, state_shift, state_wkv, state_pool, p)
    return (y_prompt, y_sample, wkv_prompt, shift_prompt, pool_prompt, wkv_sample, shift_sample, pool_sample)


_drawn_inputs = setup_inputs


def setup_inputs(seed=0):
    import zlib

    import numpy as np

    out = dict(_drawn_inputs(seed))
    spreads = {}
    factors = {'rwkv_gn_b': 5.686}
    for name, (base, spread) in spreads.items():
        noise = np.random.default_rng([zlib.crc32(name.encode()), seed]).standard_normal(out[name].shape)
        drawn = base * np.exp(spread * noise) if base else spread * noise
        out[name] = __import__('jax').numpy.asarray(drawn.astype(out[name].dtype))
    for name, factor in factors.items():
        out[name] = (out[name] * factor).astype(out[name].dtype)
    return out
```

```python
from contextlib import ExitStack

import numpy as np
import concourse.bass as bass
from concourse import mybir

F32 = mybir.dt.float32
F32R = mybir.dt.float32r
ALU = mybir.AluOpType
ACT = mybir.ActivationFunctionType
MUL, ADD, SUB, MAX, BYP = ALU.mult, ALU.add, ALU.subtract, ALU.max, ALU.bypass

P = 128
D = 1024
KT = D // P
SEQ, NB, DS = 512, 8, 4
NS = NB * DS
T = SEQ + NS
TH = T // 2
HD, NH = 64, 16
DFF = 4 * D
UW = 256
POOLS = (2, 4, 8, 16)
PBUF = 15
LW, LA, LG = 64, 64, 160
DECAY = float(np.exp(-0.5))
NORM_EPS, GN_EPS = 1e-6, 64e-5

NMIX, NFFN, NFIN, MIX = 0, 16, 32, 40
KK_, KA_, RK_, GNW, GNB = 88, 96, 104, 112, 120
PSC, SHF = 0, 8
XS_ORDER = (3, 4, 5, 0, 1, 2)

U_W1, U_A1, U_G1, U_RKV, U_WO = 0, 1, 2, 3, 15
U_F0 = 19
U_POOL = U_F0 + 32
U_F1 = U_POOL + 1
FFN_U, FFN_J = 8, 16
CHUNKS = DFF // D

J_X, J_PRM, J_N0 = 0, 5, 6
J_W1, J_A1, J_G1, J_R, J_K, J_V = 7, 8, 9, 11, 19, 27
J_SHO = 35
J_WKV = 36
WKV_JOBS = ("wpre", "apre", "norm2", "MT", "M", "N", "P2", "P2T", "RB", "XT2", "P4", "RK", "XT3",
            "trA", "FT", "F", "trB", "X", "F2", "F2T", "trK", "Z2", "F4", "trV", "bonus", "Z3", "TT", "W1T", "TNT",
            "U0", "YS0", "SS0", "U1", "YS1", "SS1", "YU")
JP = len(WKV_JOBS)
assert JP % 4 == 0
TILES = SEQ // P
J_STO = J_WKV + JP * TILES
SMP_JOBS = ("wpre", "apre", "norm2", "MT", "M", "N", "P2", "RB", "XT2", "RK", "trA", "trB", "trK", "trV", "bonus",
            "W1T", "TNT", "s0t0", "s0t1", "s0t2", "s0t3", "UY", "trU", "YU", "SO0", "SO1", "SO2", "SO3")
J_SMP = J_STO + 1
J_GN = J_SMP + len(SMP_JOBS)
J_WO = J_GN + 3 * KT
J_N1 = J_WO + KT
J_F0 = J_N1 + 1
J_N2 = J_F0 + FFN_J * CHUNKS
J_PST = J_N2 + 1
J_PO = J_PST + 1
J_PW = J_PO + 2
J_N3 = J_PW + KT
J_F1 = J_N3 + 1
J_N4 = J_F1 + FFN_J * CHUNKS
J_Y = J_N4 + 1

DVE_FEATURES = ("KQ", "KSQ", "SG", "CS", "CX", "RI", "KK", "AT", "AG", "BB", "BH", "T1", "T2", "KP", "KH", "RT", "BD",
                "KD", "Z", "ZR")
DVE_SUMS = ("XT1a", "XT1b", "Z1a", "Z1b", "STD0", "STD1")
ACT_FEATURES = ("VC", "NR", "EL", "EN", "EX")
SMP_ACT = ACT_FEATURES[1:]
SMP_DVE = DVE_FEATURES + ("XT1", "DC", "DIAG", "MASKB0", "MASKK0", "MASKB1", "MASKK1", "MASKB2", "MASKK2", "MASKB3",
                               "MASKK3")


def constants():
    s = np.arange(P)[:, None]
    c = np.arange(HD)[None, :]
    r = s % HD
    same8 = (r // 8) == (c // 8)
    e = np.arange(P)[None, :]
    parts = {
        "ident": (s == e), "ones": np.ones((P, P)), "bones": (s // HD == e // HD),
        "bmean": (s // HD == e // HD) / HD,
        "U8": (c > r) & same8, "L8": (c < r) & same8, "LO": (c < r) & ~same8, "LS": c < r, "UI": c >= r,
        "I64": c == r,
    }
    q = np.arange(NS)[None, :]
    sameb = (s % NS) // DS == q // DS
    parts |= {"SU": (q > s % NS) & sameb, "SL": (q < s % NS) & sameb, "SUI": (q >= s % NS) & sameb,
              "SI": q == s % NS, "SB": (s % NS) // DS == np.arange(NB)[None, :]}
    t = np.arange(16)[None, :]
    for w in POOLS:
        parts[f"corr{w}"] = np.broadcast_to(w / np.minimum(t + 1, w), (P, 16))
    parts["eps"] = np.broadcast_to(np.array([[NORM_EPS, GN_EPS]]), (P, 2))
    at, n = {}, 0
    for k, v in parts.items():
        at[k] = (n, v.shape[1])
        n += v.shape[1]
    table = np.concatenate([np.asarray(v, np.float32) for v in parts.values()], axis=1).astype(np.float32)
    resets = np.ones((1, KT * P + KT * NS), np.float32)
    resets[0, 0:KT * P:HD] = 0
    resets[0, KT * P::DS] = 0
    return table, at, resets


def build(nc, a, o):
    table, CAT, _ = constants()
    ctx = ExitStack()
    with ctx:
        cursor = [(nc.sbuf_base + 31) // 32 * 32]

        def region(nbytes):
            off = cursor[0]
            cursor[0] += (nbytes + 31) // 32 * 32
            assert cursor[0] <= nc.sbuf_usable_end, (cursor[0], nc.sbuf_usable_end)
            return off

        def at(name, shape, off, dt=F32):
            return nc.alloc_sbuf_tensor_at(name, shape, dt, offset=off)

        def sem(name):
            return ctx.enter_context(nc.semaphore(name))

        FB = 4 * KT * T
        X = at("x_res", [P, KT, T], region(FB))
        CT = at("const_sb", [P, table.shape[1]], region(4 * table.shape[1]))
        PRM = at("params", [P, P], region(4 * P))
        PRM2 = at("params2", [P, 72], region(4 * 72))
        OMM = at("one_minus_mix", [P, 48], region(4 * 48))
        o_rst = region(4 * (KT * P + KT * NS))
        XF = at("xs_full", [P, 2, T], o_rst)
        RST = at("resets_sb", [P, KT * P + KT * NS], o_rst)
        o_raw, o_w = region(2 * 8192), region(4 * 8192)
        RAW = [at(f"w_raw{b}", [P, KT, UW], o_raw + 8192 * b) for b in range(2)]
        WHI = [at(f"w_hi{b}", [P, KT, UW], o_w + 8192 * b, F32R) for b in range(2)]
        WLO = [at(f"w_lo{b}", [P, KT, UW], o_w + 8192 * (2 + b), F32R) for b in range(2)]
        o_a, o_b, o_h, o_l = region(4 * FB), region(2 * FB), region(4 * KT * 553), region(4 * 4 * T)
        o_s = region(4096)
        XSH = [at(f"xs_hi{b}", [P, KT, T], o_a + 2 * FB * b, F32R) for b in range(2)]
        XSL = [at(f"xs_lo{b}", [P, KT, T], o_a + 2 * FB * b + FB, F32R) for b in range(2)]
        R = at("r_all", [P, KT, T], o_b)
        K = at("k_all", [P, KT, T], o_b + FB)
        H = at("h_shift", [P, KT, 553], o_h)
        V = at("v_all", [P, KT, T], o_h)
        WH = at("w_hidden", [P, T], o_l)
        AH = at("a_hidden", [P, T], o_l + 4 * T)
        GH = at("g_hidden", [P, 2, T], o_l + 8 * T)
        ST = at("state", [P, KT, HD], o_s)
        STD = at("state_decayed", [P, KT, HD], o_s + 2048)
        SHT = at("shift_cols", [P, KT, 9], o_s + 2048)
        XIN = at("x_rows", [P, 5, D], o_a)
        PR = at("param_rows", [P, P], o_w)
        PR2 = at("param_rows2", [72, P], o_w + 512)
        SQ = at("squares", [P, KT, T], o_b)
        HN = at("normed", [P, KT, T], o_b + FB)
        RS0, RS1 = at("rstd0", [P, T], o_l), at("rstd1", [P, T], o_h)
        slots = [o_a + 4096 * n for n in range(17)] + [o_w + 4096 * n for n in range(8)]
        W2A, A2A = (at(n, [P, D], slots.pop()) for n in ("w2_aug", "a2_aug"))
        feat, TMs, MS = slots[0:9], slots[9:13], slots[13:]
        assert len(MS) == 10
        WT = {}
        for name, n in (("TW", 0), ("SG", 0), ("CX", 0), ("AG", 0), ("BB", 0), ("BH", 0), ("CS", 1), ("RT", 1),
                        ("EL", 2), ("EN", 3), ("BD", 3), ("EX", 4), ("AT", 4), ("TA", 5), ("T1", 5), ("KP", 5),
                        ("KQ", 6), ("KK", 6), ("Z", 6), ("KSQ", 7), ("NR", 7), ("KH", 7), ("KD", 8)):
            WT[name] = at("wkv_" + name, [P, KT, P], feat[n])
        for n, name in enumerate(("A_TM", "B_TM", "K_TM", "V_TM")):
            WT[name] = at("wkv_" + name, [P, D], TMs[n])
        for name, n in (("P1T", 0), ("P4", 0), ("Z1", 0), ("P1", 1), ("FT", 1), ("F4", 1), ("MO", 2), ("F2T", 2),
                        ("NM", 3), ("RBT", 4), ("RKT", 5), ("XT", 6), ("TT", 6), ("P2", 7), ("F", 7), ("TNT", 7),
                        ("P2T", 8), ("X", 8), ("F2", 9)):
            WT[name] = at("wkv_" + name, [P, 2, KT, HD], MS[n])
        WT["W1T"] = at("wkv_W1T", [P, 2, KT, HD], MS[9])
        WT["U"] = at("wkv_U", [P, 2, KT, HD], feat[4])
        WT["VC"] = at("wkv_VC", [P, KT, P], TMs[3])
        SHO = at("shift_rows", [9, D], TMs[3])
        STO = at("state_rows", [HD, D], MS[8])
        SM = {}
        for name, n in (("TW", 0), ("SG", 0), ("CX", 0), ("AG", 0), ("BB", 0), ("BH", 0), ("CS", 1), ("RT", 1),
                        ("EL", 2), ("EN", 3), ("BD", 3), ("EX", 4), ("AT", 4), ("TA", 5), ("T1", 5), ("KP", 5),
                        ("KQ", 6), ("KK", 6), ("Z", 6), ("KSQ", 7), ("NR", 7), ("KH", 7), ("KD", 8), ("W1T", 9),
                        ("UT", 10)):
            SM[name] = at("smp_" + name, [P, KT, NS], feat[n // 4] + 1024 * (n % 4))
        for n, name in enumerate(("A_TM", "B_TM", "K_TM", "V_TM")):
            SM[name] = at("smp_" + name, [NS, D], TMs[n])
        for n, name in enumerate(("P1T", "P1", "NM", "RBT", "RKT", "XT", "P2", "TNT")):
            SM[name] = at("smp_" + name, [NS, 2, KT, NS], feat[3 + n // 2] + 2048 * (n % 2))
        SM["U_TM"] = at("smp_U_TM", [NS, D], feat[7])
        SM["DC"] = at("smp_DC", [P, KT, NB], feat[8])
        S0L = at("smp_state_rows", [HD, NB, NH, HD], o_raw)
        S0T = at("smp_state", [P, NB, KT, HD], o_b + FB)
        DG = at("smp_decay_diag", [P, KT, NB, HD], o_a + 4096 * 13)
        MB = at("smp_masked_b", [NS, 4, NB, HD], o_w)
        MK = at("smp_masked_k", [NS, 4, NB, HD], o_w + 8192)
        SO = at("smp_state_out", [P, KT, NB, HD], o_raw)
        G2A, G2B = at("g2_a", [P, D], o_a), at("g2_b", [LG - P, D], o_a + 4096)
        GQ = at("gn_squares", [P, 2, T], o_a + 8192)
        GR = at("gn_rstd", [P, 2, T], o_a + 8192 + 8 * T)
        EXT = at("pool_ext", [P, KT, PBUF + SEQ + NB * (PBUF + DS)], o_b)
        WS = [at(f"pool_sum{b}", [P, 2, PBUF + SEQ + NB * (PBUF + DS)], o_a + 2 * FB + 5440 * b) for b in range(2)]
        DF = at("pool_diff", [P, KT, T], o_a + 2 * FB + 11264)
        PSI = at("pool_state_rows", [P, D], o_l)
        PCO = at("pool_out_cols", [P, KT, NB, PBUF], o_l + 4096)
        PRO = [at(f"pool_out_rows{n}", [P, D], o_w + 4096 * (4 + n)) for n in range(2)]
        HH, HL = XSH[1], XSL[1]
        RL = at("relu_tmp", [P, 2, T], o_l)
        QL = at("square_tmp", [P, 2, T], o_l + 8 * T)
        YO = [at(f"y_rows{n}", [P, D], o_a + 4096 * n) for n in range(5)]

        CC = {k: CT[:, n:n + w] for k, (n, w) in CAT.items()}
        ident, ones, bones, bmean = (CC[k] for k in ("ident", "ones", "bones", "bmean"))

        PS = ctx.enter_context(nc.psum_tensor("ps", [P, 8, 512], F32))

        def bank(j, half):
            return PS[:, 2 * (j % 4) + half, :]

        def both(j, n=512):
            return PS[:, 2 * (j % 4):2 * (j % 4) + 2, 0:n]

        def halves(ap):
            return ap.rearrange("p (a t) -> p a t", a=2)

        def col(n):
            return PRM[:, n:n + 1]

        def spread(ap, n):
            return ap.unsqueeze(2).to_broadcast([ap.shape[0], ap.shape[1], n])

        def over(ap, n):
            return ap.unsqueeze(1).to_broadcast([ap.shape[0], n, ap.shape[1]])

        filled = sem("psum_filled")
        emptied = [sem(f"psum_emptied{n}") for n in range(4)]
        raw_loaded = [sem(f"raw_loaded{b}") for b in range(2)]
        whi_made, wlo_made = sem("whi_made"), sem("wlo_made")
        const_loaded, x_loaded, prm_loaded = sem("const_loaded"), sem("x_loaded"), sem("prm_loaded")
        omm_made, pads_made = sem("omm_made"), sem("pads_made")
        sq_made, rstd_made, hn_made = sem("sq_made"), sem("rstd_made"), sem("hn_made")
        xt_made, xf_made, xhi_made, xlo_made = sem("xt_made"), sem("xf_made"), sem("xhi_made"), sem("xlo_made")
        gsig_made = sem("gsig_made")
        aug_loaded, resets_loaded, s0_loaded, g2_loaded, pst_loaded = (sem(n) for n in (
            "aug_loaded", "resets_loaded", "s0_loaded", "g2_loaded", "pst_loaded"))
        out_stored, sht_made = sem("out_stored"), sem("sht_made")
        own_part, smp_part = sem("own_part_filled"), sem("sample_part_filled")
        settled = sem("settled")
        square_made, hhi_made, hlo_made = sem("square_made"), sem("hhi_made"), sem("hlo_made")
        dve_feature, act_feature, dve_sum = sem("dve_feature"), sem("act_feature"), sem("dve_sum")
        smp_dve, smp_act = sem("smp_dve_feature"), sem("smp_act_feature")
        gn_squared, gn_step, gn_hi, gn_lo = sem("gn_squared"), sem("gn_step"), sem("gn_hi"), sem("gn_lo")
        pool_win, pool_diff, pool_hi, pool_lo = (sem(n) for n in ("pool_window", "pool_diff", "pool_hi", "pool_lo"))
        pool_cols = sem("pool_cols")

        def wait_filled(eng, j, half=1):
            eng.wait_ge(filled, 2 * j + half + 1)

        def wait_emptied(eng, j, half=1):
            eng.wait_ge(emptied[j % 4], 2 * (j // 4) + half + 1)

        def wait_free(pe, j, half=1):
            if j >= 4:
                wait_emptied(pe, j - 4, half)

        def jw(name):
            return J_WKV + WKV_JOBS.index(name)

        def js(name):
            return J_SMP + SMP_JOBS.index(name)

        def w_filled(eng, i, name, half=1):
            eng.wait_ge(filled, i * (2 * JP) + (2 * jw(name) + half + 1))

        def w_kept(eng, i, name, half=1):
            j = jw(name)
            eng.wait_ge(emptied[j % 4], i * (JP // 2) + (2 * (j // 4) + half + 1))

        def w_free(pe, i, name):
            j = jw(name) - 4
            pe.wait_ge(emptied[j % 4], i * (JP // 2) + (2 * (j // 4) + 2))

        def w_dve(eng, i, name):
            eng.wait_ge(dve_feature, i * len(DVE_FEATURES) + DVE_FEATURES.index(name) + 1)

        def w_sum(eng, i, name):
            eng.wait_ge(dve_sum, i * len(DVE_SUMS) + DVE_SUMS.index(name) + 1)

        def w_state(eng, i, c):
            j = jw(f"SS{1 - c}") - (JP if c == 0 else 0)
            eng.wait_ge(emptied[j % 4], i * (JP // 2) + 2 * (j // 4) + 2)

        def w_act(eng, i, name):
            eng.wait_ge(act_feature, i * len(ACT_FEATURES) + ACT_FEATURES.index(name) + 1)

        def s_dve(eng, name):
            eng.wait_ge(smp_dve, SMP_DVE.index(name) + 1)

        def s_act(eng, name):
            eng.wait_ge(smp_act, SMP_ACT.index(name) + 1)

        def last_job(u):
            if u < U_RKV:
                return (J_W1, J_A1, J_G1 + 1)[u]
            if u < U_WO:
                return J_R + 2 * (u - U_RKV) + 1
            if u < U_F0:
                return J_WO + 2 * (u - U_WO) + 1
            if u < U_POOL:
                return J_F0 + 2 * (u - U_F0) + 1
            return J_PW + 7 if u == U_POOL else J_F1 + 2 * (u - U_F1) + 1

        w1_v = a["rwkv_w1"][0].rearrange("(k p) n -> p k n", p=P)
        a1_v = a["rwkv_a1"][0].rearrange("(k p) n -> p k n", p=P)
        g1_v = a["rwkv_g1"][0].rearrange("(k p) n -> p k n", p=P)
        rkv_v = a["rwkv_w_rkv"][0].rearrange("j (k p) n -> j p k n", p=P)
        wo_v = a["rwkv_w_o"][0].rearrange("(k p) n -> p k n", p=P)
        up_v = [a["ffn_w1"][l].rearrange("(k p) (c n) -> p k c n", p=P, n=D) for l in range(2)]
        dn_v = [a["ffn_w2"][l].rearrange("(c k p) n -> c p k n", p=P, k=KT) for l in range(2)]
        pool_v = a["pool_w"][0].rearrange("g (k p) n -> p (g k) n", p=P)

        def unit_width(u):
            return {U_W1: LW, U_A1: LA, U_G1: LG}.get(u, UW)

        def sp_unit(sp, u, src, i=0):
            if u >= 2:
                sp.wait_ge(whi_made, i * FFN_U + u - 1)
                sp.wait_ge(wlo_made, i * FFN_U + u - 1)
            sp.dma_start(RAW[u % 2][:, :, 0:unit_width(u)], src).then_inc(raw_loaded[u % 2], 16)

        def store(sp, dst, src):
            sp.dma_start(dst, src).then_inc(out_stored, 16)
            stores[0] += 1

        stores = [0]

        def sp_ffn(sp, l, i):
            u0 = (U_F0, U_F1)[l]
            for q in range(4):
                sp_unit(sp, u0 + q, up_v[l][:, :, i, q * UW:(q + 1) * UW], i)
            for q in range(4):
                sp_unit(sp, u0 + 4 + q, dn_v[l][i, :, :, q * UW:(q + 1) * UW], i)

        def run_sp(sp):
            sp.dma_start(CT[:], a["const_table"]).then_inc(const_loaded, 16)
            xp = a["x_prompt"][0].rearrange("(a p) d -> a p d", p=P)
            for n in range(4):
                sp.dma_start(XIN[:, n, :], xp[n]).then_inc(x_loaded, 16)
            sp.dma_start(XIN[0:NS, 4, :], a["x_sample"].rearrange("b t d -> (b t) d")).then_inc(x_loaded, 16)
            rows = lambda ap: ap.rearrange("a (k p) -> (a k) p", p=P)
            for name, r0, n in (("norm_mix", NMIX, 2), ("norm_ffn", NFFN, 2), ("rwkv_k_k", KK_, 1), ("rwkv_k_a", KA_, 1),
                                ("rwkv_gn_w", GNW, 1), ("rwkv_gn_b", GNB, 1)):
                sp.dma_start(PR[r0:r0 + 8 * n, :], rows(a[name])).then_inc(prm_loaded, 16)
            sp.dma_start(PR[NFIN:NFIN + 8, :], a["norm_final"].rearrange("(k p) -> k p", p=P)).then_inc(prm_loaded, 16)
            sp.dma_start(PR[MIX:MIX + 48, :], rows(a["rwkv_mix"][0])).then_inc(prm_loaded, 16)
            sp.dma_start(PR[RK_:RK_ + 8, :], a["rwkv_r_k"][0].rearrange("(k e) d -> k (e d)", e=2)).then_inc(prm_loaded, 16)
            sp.dma_start(PR2[PSC:PSC + 8, :], rows(a["pool_scale"])).then_inc(prm_loaded, 16)
            sp.dma_start(PR2[SHF:SHF + 64, :], a["state_shift"][0].rearrange("b (k p) -> (b k) p", p=P)).then_inc(prm_loaded, 16)
            sp_unit(sp, U_W1, w1_v)
            sp_unit(sp, U_A1, a1_v)
            sp_unit(sp, U_G1, g1_v)
            for n in range(12):
                j, q = n // 4, n % 4
                sp_unit(sp, U_RKV + n, rkv_v[j, :, :, q * UW:(q + 1) * UW])
            sp.wait_ge(xlo_made, 48)
            sp.dma_start(RST[:], a["resets"].to_broadcast([P, KT * P + KT * NS])).then_inc(resets_loaded, 16)
            wait_filled(sp, J_V + 7)
            sp.dma_start(W2A[0:LW, :], a["rwkv_w2"][0]).then_inc(aug_loaded, 16)
            sp.dma_start(W2A[LW:LW + 1, :], a["rwkv_w0"]).then_inc(aug_loaded, 16)
            sp.dma_start(A2A[0:LA, :], a["rwkv_a2"][0]).then_inc(aug_loaded, 16)
            sp.dma_start(A2A[LA:LA + 1, :], a["rwkv_a0"]).then_inc(aug_loaded, 16)
            wait_emptied(sp, J_SHO)
            store(sp, o["shift_prompt"][0], SHO[0:1, :])
            store(sp, o["shift_sample"][0], SHO[1:9, :])
            wait_filled(sp, J_STO - 1)
            for b in range(NB):
                sp.dma_start(S0L[:, b], a["state_wkv"][0, b].rearrange("h v k -> v h k")).then_inc(s0_loaded, 16)
            wait_emptied(sp, J_STO)
            store(sp, o["wkv_prompt"][0, 0].rearrange("h v k -> v h k"), STO[:].rearrange("v (h k) -> v h k", k=HD))
            for q in range(4):
                wait_emptied(sp, js(f"SO{q}"))
                for g in (2 * q, 2 * q + 1):
                    store(sp, o["wkv_sample"][0].rearrange("b h v k -> (h v) b k")[g * P:(g + 1) * P], SO[:, g])
            sp.dma_start(G2A[:], a["rwkv_g2"][0, 0:P]).then_inc(g2_loaded, 16)
            sp.dma_start(G2B[:], a["rwkv_g2"][0, P:LG]).then_inc(g2_loaded, 16)
            sp.wait_ge(out_stored, 16 * stores[0])
            for n in range(4):
                sp_unit(sp, U_WO + n, wo_v[:, :, n * UW:(n + 1) * UW])
            with sp.Fori(0, CHUNKS) as i:
                sp_ffn(sp, 0, i)
            sp_unit(sp, U_POOL, pool_v)
            wait_filled(sp, J_N2)
            sp.dma_start(PSI[0:NB * PBUF, :], a["state_pool"][0].rearrange("b t d -> (b t) d")).then_inc(pst_loaded, 16)
            for n in range(2):
                sp_unit(sp, U_F1 + n, up_v[1][:, :, 0, n * UW:(n + 1) * UW])
            wait_emptied(sp, J_PO)
            store(sp, o["pool_prompt"][0, 0], PRO[0][0:PBUF, :])
            wait_emptied(sp, J_PO + 1)
            store(sp, o["pool_sample"][0].rearrange("b t d -> (b t) d"), PRO[1][0:NB * PBUF, :])
            for q in range(2, 4):
                sp_unit(sp, U_F1 + q, up_v[1][:, :, 0, q * UW:(q + 1) * UW])
            for q in range(4):
                sp_unit(sp, U_F1 + 4 + q, dn_v[1][0, :, :, q * UW:(q + 1) * UW])
            with sp.Fori(1, CHUNKS) as i:
                sp_ffn(sp, 1, i)
            for n in range(5):
                wait_emptied(sp, J_Y + n)
                if n < 4:
                    store(sp, o["y_prompt"][0, n * P:(n + 1) * P, :], YO[n][:])
                else:
                    store(sp, o["y_sample"].rearrange("b t d -> (b t) d"), YO[n][0:NS, :])
            sp.wait_ge(out_stored, 16 * stores[0])

        def pe_unit(pe, u, j0, xh, xl, mtiles, ready=None, i=0, ktiles=None):
            pe.wait_ge(whi_made, i * FFN_U + u + 1)
            pe.wait_ge(wlo_made, i * FFN_U + u + 1)
            wh, wl = WHI[u % 2], WLO[u % 2]
            for m, (c0, w) in enumerate(mtiles):
                j = j0 + m
                pe.wait_ge(emptied[(j - 4) % 4], i * (FFN_J // 2) + 2 * ((j - 4) // 4) + 2)
                ks = ktiles[m] if ktiles else [(k, k) for k in range(KT)]
                for n, (kw, kx) in enumerate(ks):
                    if ready is not None:
                        ready(pe, m, kx)
                    for wt, xt in ((wh, xh), (wh, xl), (wl, xh)):
                        for h in range(2):
                            mm = nc.tensor.matmul(bank(j, h)[0:w, 0:TH], wt[:, kw, c0:c0 + w],
                                                  xt[:, kx, h * TH:(h + 1) * TH],
                                                  start=(n == 0 and wt is wh and xt is xh),
                                                  stop=(n == len(ks) - 1 and wt is wl))
                mm.then_inc(filled, 2)

        def pe_transposes(pe, j, items, n=P):
            wait_free(pe, j)
            for out, in_ in items:
                k = in_.shape[0]
                mm = nc.tensor.transpose(out, in_, ident[0:k, 0:k])
            mm.then_inc(filled, 2)

        def pe_norm(pe, n, j):
            wait_free(pe, j)
            for k in range(KT):
                pe.wait_ge(sq_made, KT * n + k + 1)
                for h in range(2):
                    mm = nc.tensor.matmul(bank(j, h)[:, 0:TH], ones, SQ[:, k, h * TH:(h + 1) * TH],
                                          start=(k == 0), stop=(k == KT - 1))
            mm.then_inc(filled, 2)

        def pe_small(pe, j, h, groups, i):
            for out, lhsT, rhs, start, stop in groups:
                mm = nc.tensor.matmul(out, lhsT, rhs, start=start, stop=stop, skip_group_check=not (start and stop))
            mm.then_inc(filled, 1)

        def chans(T3, p, g, c):
            return T3[p * HD:(p + 1) * HD, g, c * HD:(c + 1) * HD]

        DIAGONAL = ((0, 0), (1, 1), (1, 0), (0, 1))

        def settle(pe):
            pe.sem_inc(settled, 1)


        def w_products(pe, i, name, L, Rt):
            j = jw(name)
            w_free(pe, i, name)
            settle(pe)
            for g in range(KT):
                for p, c in DIAGONAL:
                    mm = nc.tensor.matmul(bank(j, p)[c * HD:(c + 1) * HD, g * HD:(g + 1) * HD],
                                          chans(L, p, g, c), chans(Rt, p, g, c), start=True, stop=True)
            mm.then_inc(filled, 2)

        def w_square(pe, i, name, L, Rt, needs):
            j = jw(name)
            for h in range(2):
                w_free(pe, i, name)
                for need in needs:
                    need(h)
                settle(pe)
                for g in range(KT):
                    for c in range(2):
                        rows = slice(c * HD, (c + 1) * HD)
                        rhs = Rt[rows, :] if Rt is CC["I64"] else Rt[rows, h, g, :]
                        mm = nc.tensor.matmul(bank(j, h)[rows, g * HD:(g + 1) * HD], L[rows, h, g, :], rhs,
                                              start=True, stop=True)
                mm.then_inc(filled, 1)

        def w_turn(pe, i, name, src):
            j = jw(name)
            for h in range(2):
                w_free(pe, i, name)
                for g in range(4):
                    mm = nc.tensor.transpose(bank(j, h)[:, g * P:(g + 1) * P], src(4 * h + g), ident)
                mm.then_inc(filled, 1)

        def pe_tile(pe, i):
            t0 = i * P
            tok = bass.ds(t0, P)
            for name, wa, hid in (("wpre", W2A, WH), ("apre", A2A, AH)):
                for h in range(2):
                    w_free(pe, i, name)
                    for g in range(4):
                        mm = nc.tensor.matmul(bank(jw(name), h)[:, g * P:(g + 1) * P],
                                              wa[0:LW + 1, (4 * h + g) * P:(4 * h + g + 1) * P], hid[0:LW + 1, tok],
                                              start=True, stop=True)
                    mm.then_inc(filled, 1)
            w_dve(pe, i, "KSQ")
            w_pairsum(pe, i, "norm2", WT["KSQ"])
            w_dve(pe, i, "BH")
            w_products(pe, i, "MT", WT["BH"], WT["AT"])
            w_products(pe, i, "M", WT["AT"], WT["BH"])
            w_dve(pe, i, "KH")
            w_products(pe, i, "N", WT["AT"], WT["KH"])
            kept = lambda name: (lambda h: w_kept(pe, i, name, h))
            made = lambda name: (lambda h: w_sum(pe, i, name + "ab"[h]))
            w_square(pe, i, "P2", WT["P1T"], WT["P1"], [kept("MT"), kept("M")])
            w_square(pe, i, "P2T", WT["P1"], WT["P1T"], [])
            w_dve(pe, i, "RT")
            w_products(pe, i, "RB", WT["BH"], WT["RT"])
            w_square(pe, i, "XT2", WT["P2"], WT["XT"], [kept("P2"), made("XT1")])
            w_square(pe, i, "P4", WT["P2T"], WT["P2"], [kept("P2T")])
            w_products(pe, i, "RK", WT["KH"], WT["RT"])
            w_square(pe, i, "XT3", WT["P4"], WT["XT"], [kept("P4"), kept("XT2")])
            w_turn(pe, i, "trA", lambda g: WT["AT"][:, g, :])
            w_square(pe, i, "FT", WT["MO"], WT["XT"], [kept("XT3")])
            w_square(pe, i, "F", WT["XT"], WT["MO"], [])
            w_dve(pe, i, "KD")
            w_turn(pe, i, "trB", lambda g: WT["BD"][:, g, :])
            w_square(pe, i, "X", WT["XT"], CC["I64"], [])
            w_square(pe, i, "F2", WT["FT"], WT["F"], [kept("F")])
            w_square(pe, i, "F2T", WT["F"], WT["FT"], [])
            w_turn(pe, i, "trK", lambda g: WT["KD"][:, g, :])
            w_square(pe, i, "Z2", WT["F2"], WT["Z1"], [kept("F2"), made("Z1")])
            w_square(pe, i, "F4", WT["F2T"], WT["F2"], [kept("F2T")])
            w_act(pe, i, "VC")
            w_turn(pe, i, "trV", lambda g: WT["VC"][:, g, :])
            w_dve(pe, i, "ZR")
            w_pairsum(pe, i, "bonus", WT["Z"])
            w_square(pe, i, "Z3", WT["F4"], WT["Z1"], [kept("F4")])
            w_square(pe, i, "TT", WT["X"], WT["Z1"], [kept("Z3")])
            j = jw("W1T")
            w_free(pe, i, "W1T")
            w_kept(pe, i, "trA")
            w_kept(pe, i, "TT")
            settle(pe)
            for g in range(KT):
                for c, p in DIAGONAL:
                    rows, n = slice(c * HD, (c + 1) * HD), 2 * g + p
                    mm = nc.tensor.matmul(bank(j, c)[p * HD:(p + 1) * HD, g * HD:(g + 1) * HD],
                                          WT["A_TM"][rows, n * HD:(n + 1) * HD], WT["TT"][rows, p, g, :],
                                          start=True, stop=True)
            mm.then_inc(filled, 2)
            w_square(pe, i, "TNT", WT["NM"], WT["TT"], [kept("N")])
            U, VT, BT, KTM = WT["U"], WT["V_TM"], WT["B_TM"], WT["K_TM"]
            w_kept(pe, i, "trV")
            for c in range(2):
                rows = slice(c * HD, (c + 1) * HD)
                w_free(pe, i, f"U{c}")
                if c == 0:
                    w_kept(pe, i, "TNT")
                settle(pe)
                j = jw(f"U{c}")
                for n in range(NH):
                    g, p = n // 2, n % 2
                    mm = nc.tensor.matmul(bank(j, p)[rows, g * HD:(g + 1) * HD], WT["TNT"][rows, p, g, :],
                                          VT[rows, n * HD:(n + 1) * HD], start=(g == 0), stop=False,
                                          skip_group_check=True)
                mm.then_inc(own_part, 1)
                if c == 0:
                    w_kept(pe, i, "W1T")
                w_state(pe, i, c)
                pe.wait_ge(own_part, 2 * i + (c + 1))
                settle(pe)
                for n in range(NH):
                    g, p = n // 2, n % 2
                    mm = nc.tensor.matmul(bank(j, p)[rows, g * HD:(g + 1) * HD], WT["W1T"][p * HD:(p + 1) * HD, c, g, :],
                                          ST[p * HD:(p + 1) * HD, g, :], start=False, stop=True, skip_group_check=True)
                mm.then_inc(filled, 2)
                w_free(pe, i, f"YS{c}")
                settle(pe)
                j = jw(f"YS{c}")
                for n in range(NH):
                    g, p = n // 2, n % 2
                    mm = nc.tensor.matmul(bank(j, 0)[p * HD:(p + 1) * HD, g * HD:(g + 1) * HD],
                                          ST[p * HD:(p + 1) * HD, g, :], chans(WT["RT"], p, g, c), start=True, stop=True)
                mm.then_inc(filled, 2)
                w_free(pe, i, f"SS{c}")
                w_kept(pe, i, f"U{c}")
                if c == 0:
                    w_kept(pe, i, "trK")
                settle(pe)
                j = jw(f"SS{c}")
                for n in range(NH):
                    g, p = n // 2, n % 2
                    out = bank(j, 0)[p * HD:(p + 1) * HD, g * HD:(g + 1) * HD]
                    nc.tensor.matmul(out, BT[rows, n * HD:(n + 1) * HD], U[rows, p, g, :], start=True, stop=False)
                    mm = nc.tensor.matmul(out, KTM[rows, n * HD:(n + 1) * HD], VT[rows, n * HD:(n + 1) * HD],
                                          start=False, stop=True)
                mm.then_inc(filled, 2)
            j = jw("YU")
            w_kept(pe, i, "RB")
            w_free(pe, i, "YU")
            settle(pe)
            for g in range(KT):
                for c, p in DIAGONAL:
                    rows, n = slice(c * HD, (c + 1) * HD), 2 * g + p
                    out = bank(j, c)[p * HD:(p + 1) * HD, g * HD:(g + 1) * HD]
                    nc.tensor.matmul(out, U[rows, p, g, :], WT["RBT"][rows, p, g, :], start=True, stop=False)
                    mm = nc.tensor.matmul(out, VT[rows, n * HD:(n + 1) * HD], WT["RKT"][rows, p, g, :],
                                          start=False, stop=True)
            mm.then_inc(filled, 2)

        def w_pairsum(pe, i, name, src):
            for h in range(2):
                w_free(pe, i, name)
                mm = nc.tensor.matmul(bank(jw(name), h), bones, src[:, 4 * h:4 * h + 4, :].rearrange("p a b -> p (a b)"),
                                      start=True, stop=True)
                mm.then_inc(filled, 1)

        def pe_samples(pe):
            t0 = SEQ
            for name, wa, hid in (("wpre", W2A, WH), ("apre", A2A, AH)):
                wait_free(pe, js(name))
                for g in range(KT):
                    mm = nc.tensor.matmul(bank(js(name), 0)[:, g * NS:(g + 1) * NS], wa[0:LW + 1, g * P:(g + 1) * P],
                                          hid[0:LW + 1, t0:t0 + NS], start=True, stop=True)
                mm.then_inc(filled, 2)

            def pairsum(name, src):
                wait_free(pe, js(name))
                nc.tensor.matmul(bank(js(name), 0)[:, 0:KT * NS], bones, src[:].rearrange("p a b -> p (a b)"),
                                 start=True, stop=True).then_inc(filled, 2)

            def products(name, L, Rt):
                wait_free(pe, js(name))
                for n in range(NH):
                    g, p = n // 2, n % 2
                    mm = nc.tensor.matmul(bank(js(name), p)[0:NS, g * NS:(g + 1) * NS], L[p * HD:(p + 1) * HD, g, :],
                                          Rt[p * HD:(p + 1) * HD, g, :], start=True, stop=True)
                mm.then_inc(filled, 2)

            def square(name, L, Rt):
                wait_free(pe, js(name))
                for n in range(NH):
                    g, p = n // 2, n % 2
                    mm = nc.tensor.matmul(bank(js(name), p)[0:NS, g * NS:(g + 1) * NS], L[:, p, g, :], Rt[:, p, g, :],
                                          start=True, stop=True)
                mm.then_inc(filled, 2)

            def turn(name, src):
                j = js(name)
                pe_transposes(pe, j, [(bank(j, g // 4)[0:NS, (g % 4) * P:(g % 4 + 1) * P], src(g)) for g in range(KT)])

            s_dve(pe, "KSQ")
            pairsum("norm2", SM["KSQ"])
            s_dve(pe, "BH")
            products("MT", SM["BH"], SM["AT"])
            products("M", SM["AT"], SM["BH"])
            s_dve(pe, "KH")
            products("N", SM["AT"], SM["KH"])
            wait_emptied(pe, js("M"))
            wait_emptied(pe, js("MT"))
            square("P2", SM["P1T"], SM["P1"])
            s_dve(pe, "RT")
            products("RB", SM["BH"], SM["RT"])
            wait_emptied(pe, js("P2"))
            s_dve(pe, "XT1")
            square("XT2", SM["P2"], SM["XT"])
            products("RK", SM["KH"], SM["RT"])
            turn("trA", lambda g: SM["AT"][:, g, :])
            s_dve(pe, "KD")
            turn("trB", lambda g: SM["BD"][:, g, :])
            turn("trK", lambda g: SM["KD"][:, g, :])
            turn("trV", lambda g: V[:, g, SEQ:T])
            s_dve(pe, "ZR")
            pairsum("bonus", SM["Z"])
            wait_emptied(pe, js("XT2"))
            wait_emptied(pe, js("trA"))
            wait_free(pe, js("W1T"))
            for n in range(NH):
                g, p = n // 2, n % 2
                mm = nc.tensor.matmul(bank(js("W1T"), 0)[p * HD:(p + 1) * HD, g * NS:(g + 1) * NS],
                                      SM["A_TM"][:, n * HD:(n + 1) * HD], SM["XT"][:, p, g, :], start=True, stop=True)
            mm.then_inc(filled, 2)
            square("TNT", SM["NM"], SM["XT"])
            for q in range(4):
                j = js(f"s0t{q}")
                if q == 0:
                    pe.wait_ge(s0_loaded, 16 * NB)
                pe_transposes(pe, j, [(bank(j, bb)[:, g * HD:(g + 1) * HD],
                                       S0L[:, 2 * q + bb, 2 * g:2 * g + 2, :].rearrange("v h k -> v (h k)"))
                                      for bb in range(2) for g in range(KT)])
            j = js("UY")
            wait_free(pe, j)
            wait_emptied(pe, js("TNT"))
            wait_emptied(pe, js("W1T"))
            wait_emptied(pe, js("trV"))
            wait_emptied(pe, js("RK"))
            wait_emptied(pe, js("s0t3"))
            for b_, m_ in ((0, "TNT"), (1, "RKT")):
                for n in range(NH):
                    g, p = n // 2, n % 2
                    mm = nc.tensor.matmul(bank(j, b_)[p * HD:(p + 1) * HD, g * NS:(g + 1) * NS],
                                          SM["V_TM"][:, n * HD:(n + 1) * HD], SM[m_][:, p, g, :],
                                          start=(g == 0), stop=False, skip_group_check=True)
            mm.then_inc(smp_part, 1)
            pe.wait_ge(smp_part, 1)
            for b_, m_ in ((0, "W1T"), (1, "RT")):
                for n in range(NH):
                    g, p = n // 2, n % 2
                    for b in range(NB):
                        cols = slice(g * NS + b * DS, g * NS + (b + 1) * DS)
                        mm = nc.tensor.matmul(bank(j, b_)[p * HD:(p + 1) * HD, cols], S0T[p * HD:(p + 1) * HD, b, g, :],
                                              SM[m_][p * HD:(p + 1) * HD, g, b * DS:(b + 1) * DS],
                                              start=False, stop=True, skip_group_check=True)
            mm.then_inc(filled, 2)
            wait_emptied(pe, j)
            turn("trU", lambda g: SM["UT"][:, g, :])
            j = js("YU")
            wait_free(pe, j)
            wait_emptied(pe, js("trU"))
            wait_emptied(pe, js("RB"))
            for n in range(NH):
                g, p = n // 2, n % 2
                mm = nc.tensor.matmul(bank(j, 0)[p * HD:(p + 1) * HD, g * NS:(g + 1) * NS],
                                      SM["U_TM"][:, n * HD:(n + 1) * HD], SM["RBT"][:, p, g, :], start=True, stop=True)
            mm.then_inc(filled, 2)
            s_dve(pe, "DIAG")
            for q in range(4):
                j = js(f"SO{q}")
                wait_free(pe, j)
                s_dve(pe, f"MASKK{q}")
                for gg in range(2):
                    for p in range(2):
                        n = 2 * (2 * q + gg) + p
                        out = bank(j, gg)[p * HD:(p + 1) * HD, :]
                        for tm, mk, first in ((SM["U_TM"], MB, True), (SM["V_TM"], MK, False)):
                            mm = nc.tensor.matmul(out, tm[:, n * HD:(n + 1) * HD],
                                                  mk[:, 2 * gg + p].rearrange("t b k -> t (b k)"),
                                                  start=first, stop=False, skip_group_check=True)
                mm.then_inc(smp_part, 1)
                pe.wait_ge(smp_part, q + 2)
                for gg in range(2):
                    g = 2 * q + gg
                    for b in range(NB):
                        for p in range(2):
                            mm = nc.tensor.matmul(bank(j, gg)[p * HD:(p + 1) * HD, b * HD:(b + 1) * HD],
                                                  S0T[p * HD:(p + 1) * HD, b, g, :], DG[p * HD:(p + 1) * HD, g, b, :],
                                                  start=False, stop=True, skip_group_check=True)
                mm.then_inc(filled, 2)

        def pe_ffn(pe, l, i):
            u0, j0 = ((U_F0, J_F0), (U_F1, J_F1))[l]
            nn = (1, 3)[l]
            first = lambda pe, m, k: pe.wait_ge(xlo_made, xlo_at(nn, k))
            for q in range(4):
                pe_unit(pe, u0 + q, j0 + 2 * q, XSH[0], XSL[0], ((0, P), (P, P)), first if q == 0 else None, i)
            hid = lambda pe, m, k: pe.wait_ge(hlo_made, i * KT + (KT * CHUNKS * l + k + 1))
            for q in range(4):
                pe_unit(pe, u0 + 4 + q, j0 + 8 + 2 * q, HH, HL, ((0, P), (P, P)), hid if q == 0 else None, i)

        def xlo_at(n, k):
            return 48 + KT * {1: 0, 3: 1}[n] + k + 1

        def run_pe(pe):
            pe.wait_ge(const_loaded, 16)
            for n in range(5):
                pe.wait_ge(x_loaded, 80)
                j, w = J_X + n, P if n < 4 else NS
                pe_transposes(pe, j, [(bank(j, k // 4)[:, (k % 4) * w:(k % 4 + 1) * w], XIN[0:w, n, k * P:(k + 1) * P])
                                      for k in range(KT)])
            pe.wait_ge(prm_loaded, 16 * 11)
            pe_transposes(pe, J_PRM, [(bank(J_PRM, 0)[:, 0:P], PR[:]), (bank(J_PRM, 1)[:, 0:72], PR2[:])])
            pe_norm(pe, 0, J_N0)
            for jx, (u, j, mt) in enumerate(((U_W1, J_W1, ((0, LW),)), (U_A1, J_A1, ((0, LA),)),
                                             (U_G1, J_G1, ((0, P), (P, LG - P))))):
                ready = lambda pe, m, k, jx=jx: pe.wait_ge(xlo_made, KT * jx + k + 1)
                pe_unit(pe, u, j, XSH[jx % 2], XSL[jx % 2], mt, ready)
            for n in range(12):
                jx = 3 + n // 4
                ready = lambda pe, m, k, jx=jx: pe.wait_ge(xlo_made, KT * jx + k + 1)
                pe_unit(pe, U_RKV + n, J_R + 2 * n, XSH[jx % 2], XSL[jx % 2], ((0, P), (P, P)),
                        ready if n % 4 == 0 else None)
            pe.wait_ge(sht_made, 1)
            pe_transposes(pe, J_SHO, [(bank(J_SHO, k // 4)[0:9, (k % 4) * P:(k % 4 + 1) * P], SHT[:, k, :])
                                      for k in range(KT)])
            pe.wait_ge(aug_loaded, 64)
            pe.wait_ge(gsig_made, 2)
            pe.wait_ge(pads_made, 5)
            with pe.Fori(0, TILES) as i:
                pe_tile(pe, i)
            wait_emptied(pe, J_STO - 2)
            pe_transposes(pe, J_STO, [(bank(J_STO, g // 4)[0:HD, (g % 4) * P:(g % 4 + 1) * P], ST[:, g, :])
                                      for g in range(KT)])
            pe_samples(pe)
            pe.wait_ge(g2_loaded, 32)
            for k in range(KT):
                for n in range(3):
                    j = J_GN + 3 * k + n
                    wait_free(pe, j)
                    if n == 1:
                        pe.wait_ge(gn_squared, k + 1)
                    for h in range(2):
                        cols = slice(h * TH, (h + 1) * TH)
                        out = bank(j, h)[:, 0:TH]
                        if n == 0:
                            mm = nc.tensor.matmul(out, bmean, R[:, k, cols], start=True, stop=True)
                        elif n == 1:
                            mm = nc.tensor.matmul(out, bmean, GQ[:, k % 2, cols], start=True, stop=True)
                        else:
                            nc.tensor.matmul(out, G2A[:, k * P:(k + 1) * P], GH[:, 0, cols], start=True, stop=False)
                            mm = nc.tensor.matmul(out, G2B[:, k * P:(k + 1) * P], GH[0:LG - P, 1, cols],
                                                  start=False, stop=True)
                    mm.then_inc(filled, 2)
            ready = lambda pe, m, k: pe.wait_ge(gn_lo, k + 1)
            for n in range(4):
                pe_unit(pe, U_WO + n, J_WO + 2 * n, XSH[1], XSL[1], ((0, P), (P, P)), ready if n == 0 else None)
            pe_norm(pe, 1, J_N1)
            with pe.Fori(0, CHUNKS) as i:
                pe_ffn(pe, 0, i)
            pe_norm(pe, 2, J_N2)
            pe.wait_ge(pst_loaded, 16)
            pe_transposes(pe, J_PST, [(bank(J_PST, k // 4)[:, (k % 4) * 120:(k % 4 + 1) * 120],
                                       PSI[0:120, k * P:(k + 1) * P]) for k in range(KT)])
            pe.wait_ge(hn_made, 3 * KT)
            pe_transposes(pe, J_PO, [(bank(J_PO, k // 4)[0:PBUF, (k % 4) * P:(k % 4 + 1) * P],
                                      EXT[:, k, SEQ:SEQ + PBUF]) for k in range(KT)])
            pe.wait_ge(pool_cols, 1)
            pe_transposes(pe, J_PO + 1, [(bank(J_PO + 1, k // 4)[0:120, (k % 4) * P:(k % 4 + 1) * P],
                                          PCO[:, k].rearrange("p b t -> p (b t)")) for k in range(KT)])
            pool_k = [[(2 * g + 0, 2 * g + 0), (2 * g + 1, 2 * g + 1)] for g in range(4) for _ in range(2)]
            ready = lambda pe, m, k: pe.wait_ge(pool_lo, k + 1)
            pe_unit(pe, U_POOL, J_PW, XSH[0], XSL[0], [(P * (m % 2), P) for m in range(KT)], ready, ktiles=pool_k)
            pe_norm(pe, 3, J_N3)
            with pe.Fori(0, CHUNKS) as i:
                pe_ffn(pe, 1, i)
            pe_norm(pe, 4, J_N4)
            pe.wait_ge(hn_made, 5 * KT)
            for n in range(5):
                j, w = J_Y + n, P if n < 4 else NS
                pe_transposes(pe, j, [(bank(j, k // 4)[0:w, (k % 4) * P:(k % 4 + 1) * P], HN[:, k, n * P:n * P + w])
                                      for k in range(KT)])

        def timeline():
            steps = [("split", 0)] + [("xs", n) for n in range(8)]
            for u, js_ in ((0, (J_W1,)), (1, (J_A1,)), (2, (J_G1, J_G1 + 1))):
                steps += [("split", u + 1)] + [("xs", 8 * (u + 1) + n) for n in range(8)] + [("out", j) for j in js_]
            for n in range(12):
                if n < 11:
                    steps += [("split", U_RKV + n + 1)]
                if n < 8:
                    steps += [("xs", 32 + 2 * n), ("xs", 33 + 2 * n)]
                steps += [("out", J_R + 2 * n), ("out", J_R + 2 * n + 1)]
            return steps

        def wait_split(eng, u, i=0):
            eng.wait_ge(raw_loaded[u % 2], i * (16 * FFN_U // 2) + 16 * (u // 2 + 1))
            if u >= 2:
                j = {U_F0 + 1: J_F0 - 1, U_F1 + 1: J_F1 - 1}.get(u, last_job(u - 2))
                eng.wait_ge(filled, i * (2 * FFN_J) + 2 * j + 2)

        act = nc.scalar.activation

        def act_split(eng, u, i=0):
            wait_split(eng, u, i)
            w = unit_width(u)
            act(WHI[u % 2][:, :, 0:w], RAW[u % 2][:, :, 0:w], ACT.Copy).then_inc(whi_made, 1)

        def act_norm(eng, n, j, ready):
            for k in range(KT):
                ready(k)
                act(SQ[:, k, :], X[:, k, :], ACT.Square).then_inc(sq_made, 1)
            wait_filled(eng, j)
            rs = RS1 if n else RS0
            act(halves(rs[:]), both(j, TH), ACT.Sqrt, bias=CC["eps"][:, 0:1], scale=1.0 / D).then_inc(emptied[j % 4], 2)

        def act_copy_out(eng, j, dst, src, func=ACT.Copy, scale=1.0):
            wait_filled(eng, j)
            act(dst, src, func, scale=scale).then_inc(emptied[j % 4], 2)

        def act_tile(eng, i):
            tok0 = i * P
            eng.wait_ge(filled, i * (2 * JP) + 2 * J_WKV)
            def copy_half(name, dst, func=ACT.Copy, scale=1.0, q=0):
                j = jw(name)
                for h in range(2):
                    w_filled(eng, i, name, h)
                    act(dst(h), bank(j, h), func, scale=scale).then_inc(emptied[j % 4], 1)
            feats = lambda T3: (lambda h: T3[:, 4 * h:4 * h + 4, :].rearrange("p a b -> p (a b)"))
            mats = lambda T4: (lambda h: T4[:, h].rearrange("p a b -> p (a b)"))
            toks = lambda T2: (lambda h: T2[:, 512 * h:512 * h + 512])
            act(WT["VC"][:], V[:, :, bass.ds(tok0, P)], ACT.Copy).then_inc(act_feature, 1)
            copy_half("wpre", feats(WT["TW"]), ACT.Tanh, 0.5)
            copy_half("apre", feats(WT["TA"]), ACT.Tanh, 0.5)
            w_kept(eng, i, "norm2")
            act(WT["NR"][:], WT["NR"][:], ACT.Sqrt).then_inc(act_feature, 1)
            w_dve(eng, i, "CS")
            act(WT["EL"][:], WT["CS"][:], ACT.Exp, scale=-DECAY).then_inc(act_feature, 1)
            act(WT["EN"][:], WT["CS"][:], ACT.Exp, scale=DECAY).then_inc(act_feature, 1)
            w_dve(eng, i, "CX")
            act(WT["EX"][:], WT["CX"][:], ACT.Exp, scale=-DECAY).then_inc(act_feature, 1)
            for name, dst in (("P2", mats(WT["P2"])), ("P2T", mats(WT["P2T"])), ("P4", mats(WT["P4"])),
                              ("trA", toks(WT["A_TM"])), ("FT", mats(WT["FT"])), ("F", mats(WT["F"])),
                              ("trB", toks(WT["B_TM"])), ("X", mats(WT["X"])), ("F2", mats(WT["F2"])),
                              ("F2T", mats(WT["F2T"])), ("trK", toks(WT["K_TM"])), ("F4", mats(WT["F4"])),
                              ("trV", toks(WT["V_TM"])), ("TT", mats(WT["TT"])), ("W1T", mats(WT["W1T"])),
                              ("TNT", mats(WT["TNT"]))):
                copy_half(name, dst)
            for c in range(2):
                rows = slice(c * HD, (c + 1) * HD)
                j = jw(f"U{c}")
                w_filled(eng, i, f"U{c}")
                for p in range(2):
                    act(WT["U"][rows, p].rearrange("p a b -> p (a b)"), bank(j, p)[rows, :], ACT.Copy).then_inc(emptied[j % 4], 1)
                j = jw(f"YS{c}")
                w_filled(eng, i, f"YS{c}")
                act(R[:, :, bass.ds(tok0 + c * HD, HD)], bank(j, 0).rearrange("p (a b) -> p a b", a=KT), ACT.Copy)\
                    .then_inc(emptied[j % 4], 2)

        def act_samples(eng):
            s8 = lambda j: bank(j, 0)[:, 0:KT * NS].rearrange("p (a b) -> p a b", a=KT)
            act_copy_out(eng, js("wpre"), SM["TW"][:], s8(js("wpre")), ACT.Tanh, 0.5)
            act_copy_out(eng, js("apre"), SM["TA"][:], s8(js("apre")), ACT.Tanh, 0.5)
            wait_emptied(eng, js("norm2"))
            act(SM["NR"][:], SM["NR"][:], ACT.Sqrt).then_inc(smp_act, 1)
            s_dve(eng, "CS")
            act(SM["EL"][:], SM["CS"][:], ACT.Exp, scale=-DECAY).then_inc(smp_act, 1)
            act(SM["EN"][:], SM["CS"][:], ACT.Exp, scale=DECAY).then_inc(smp_act, 1)
            s_dve(eng, "CX")
            act(SM["EX"][:], SM["CX"][:], ACT.Exp, scale=-DECAY).then_inc(smp_act, 1)
            small = lambda j: both(j, KT * NS)[0:NS]
            flat = lambda T4: T4[:].rearrange("p e a b -> p e (a b)")
            rows2 = lambda T2: T2[:].rearrange("p (e n) -> p e n", e=2)
            act_copy_out(eng, js("P2"), flat(SM["P2"]), small(js("P2")))
            for name, dst in (("trA", "A_TM"), ("trB", "B_TM"), ("trK", "K_TM"), ("trV", "V_TM")):
                act_copy_out(eng, js(name), rows2(SM[dst]), both(js(name))[0:NS])
            act_copy_out(eng, js("W1T"), SM["W1T"][:], s8(js("W1T")))
            act_copy_out(eng, js("TNT"), flat(SM["TNT"]), small(js("TNT")))
            for q in range(4):
                act_copy_out(eng, js(f"s0t{q}"), S0T[:, 2 * q:2 * q + 2].rearrange("p b g v -> p b (g v)"), both(js(f"s0t{q}")))
            j = js("UY")
            wait_filled(eng, j)
            act(SM["UT"][:], s8(j), ACT.Copy).then_inc(emptied[j % 4], 1)
            act(R[:, :, SEQ:T], bank(j, 1)[:, 0:KT * NS].rearrange("p (a b) -> p a b", a=KT), ACT.Copy).then_inc(emptied[j % 4], 1)
            act_copy_out(eng, js("trU"), rows2(SM["U_TM"]), both(js("trU"))[0:NS])
            for q in range(4):
                act_copy_out(eng, js(f"SO{q}"), SO[:, 2 * q:2 * q + 2].rearrange("p g b k -> p g (b k)"), both(js(f"SO{q}")))

        def act_ffn(eng, l, i, last):
            u0, j0 = ((U_F0, J_F0), (U_F1, J_F1))[l]
            h0 = KT * CHUNKS * l
            for q in range(8):
                if not (last and q == 7):
                    act_split(eng, u0 + q + 1, i)
                for m in (2 * q, 2 * q + 1):
                    if q < 4:
                        j = j0 + m
                        eng.wait_ge(filled, i * (2 * FFN_J) + 2 * j + 2)
                        if m >= 2:
                            eng.wait_ge(square_made, i * KT + (h0 + m - 1))
                        act(halves(RL[:, m % 2, :]), both(j, TH), ACT.Relu).then_inc(emptied[j % 4], 2)
                        if m >= 1:
                            act_hidden_hi(eng, i, h0, m - 1)
                if q == 3:
                    act_hidden_hi(eng, i, h0, 7)

        def act_hidden_hi(eng, i, h0, m):
            eng.wait_ge(square_made, i * KT + (h0 + m + 1))
            act(HH[:, m, :], QL[:, m % 2, :], ACT.Copy).then_inc(hhi_made, 1)

        def run_act(eng):
            eng.wait_ge(const_loaded, 16)
            for n in range(5):
                j = J_X + n
                w = P if n < 4 else NS
                wait_filled(eng, j)
                for h in range(2):
                    act(X[:, 4 * h:4 * h + 4, n * P:n * P + w], bank(j, h)[:, 0:4 * w].rearrange("p (a b) -> p a b", a=4),
                        ACT.Copy).then_inc(emptied[j % 4], 1)
            wait_filled(eng, J_PRM)
            act(PRM[:], bank(J_PRM, 0)[:, 0:P], ACT.Copy).then_inc(emptied[J_PRM % 4], 1)
            act(PRM2[:], bank(J_PRM, 1)[:, 0:72], ACT.Copy).then_inc(emptied[J_PRM % 4], 1)
            act_norm(eng, 0, J_N0, lambda k: wait_emptied(eng, J_X + 3) if k else wait_emptied(eng, J_X + 4))
            eng.wait_ge(hn_made, KT)
            eng.wait_ge(pads_made, 3)

            def shifted(n):
                jx, k = n // 8, n % 8
                if n >= 2:
                    eng.wait_ge(xlo_made, n - 1)
                m = col(MIX + 8 * XS_ORDER[jx] + k)
                act(XF[:, n % 2, 0:SEQ], H[:, k, 0:SEQ], ACT.Copy, scale=m)
                act(XF[:, n % 2, SEQ:T].rearrange("p (b t) -> p b t", b=NB),
                    H[:, k, 513:553].rearrange("p (b t) -> p b t", b=NB)[:, :, 0:DS], ACT.Copy, scale=m).then_inc(xt_made, 1)

            def shifted_hi(n):
                jx, k = n // 8, n % 8
                if k == 0 and jx >= 2:
                    wait_filled(eng, (J_W1, J_A1, J_G1 + 1, J_R + 7)[jx - 2])
                eng.wait_ge(xf_made, n + 1)
                act(XSH[jx % 2][:, k, :], XF[:, n % 2, :], ACT.Copy).then_inc(xhi_made, 1)

            for what, n in timeline():
                if what == "split":
                    act_split(eng, n)
                elif what == "xs":
                    if n == 0:
                        shifted(0)
                    if n + 1 < 48:
                        shifted(n + 1)
                    shifted_hi(n)
                elif n == J_W1:
                    act_copy_out(eng, n, halves(WH[0:LW, :]), both(n, TH)[0:LW], ACT.Tanh)
                elif n == J_A1:
                    act_copy_out(eng, n, halves(AH[0:LA, :]), both(n, TH)[0:LA])
                elif n == J_G1:
                    act_copy_out(eng, n, halves(GH[:, 0, :]), both(n, TH), ACT.Tanh, 0.5)
                elif n == J_G1 + 1:
                    act_copy_out(eng, n, halves(GH[0:LG - P, 1, :]), both(n, TH)[0:LG - P], ACT.Tanh, 0.5)
                else:
                    m = n - J_R
                    if m == 16:
                        eng.wait_ge(xf_made, 48)
                        eng.wait_ge(sht_made, 1)
                    act_copy_out(eng, n, halves((R, K, V)[m // 8][:, m % 8, :]), both(n, TH))
            act_copy_out(eng, J_SHO, SHO[:].rearrange("p (e n) -> p e n", e=2), both(J_SHO)[0:9])
            eng.wait_ge(out_stored, 32)
            with eng.Fori(0, TILES) as i:
                act_tile(eng, i)
            act_copy_out(eng, J_STO, STO[:].rearrange("p (e n) -> p e n", e=2), both(J_STO)[0:HD])
            act_samples(eng)
            for k in range(KT):
                wait_emptied(eng, J_GN + 3 * k)
                act(GQ[:, k % 2, :], R[:, k, :], ACT.Square).then_inc(gn_squared, 1)
                j = J_GN + 3 * k + 1
                wait_filled(eng, j)
                if k >= 2:
                    eng.wait_ge(gn_step, 4 * (k - 2) + 2)
                act(halves(GR[:, k % 2, :]), both(j, TH), ACT.Sqrt, bias=CC["eps"][:, 1:2]).then_inc(emptied[j % 4], 2)
                wait_emptied(eng, J_GN + 3 * k + 2)
                act(XSH[1][:, k, :], R[:, k, :], ACT.Copy).then_inc(gn_hi, 1)
            act_split(eng, U_WO)
            for n in range(4):
                if n < 3:
                    act_split(eng, U_WO + n + 1)
            act_norm(eng, 1, J_N1, lambda k: wait_emptied(eng, J_WO + k))
            act_split(eng, U_F0)
            act_hi_norm(eng, 1)
            with eng.Fori(0, CHUNKS - 1) as i:
                act_ffn(eng, 0, i, False)
            act_ffn(eng, 0, CHUNKS - 1, False)
            act_norm(eng, 2, J_N2, lambda k: wait_emptied(eng, J_N2 - KT + k))
            act_copy_out(eng, J_PO, PRO[0][0:PBUF, :].rearrange("p (e n) -> p e n", e=2), both(J_PO)[0:PBUF])
            act_copy_out(eng, J_PO + 1, PRO[1][0:120, :].rearrange("p (e n) -> p e n", e=2), both(J_PO + 1)[0:120])
            for k in range(KT):
                eng.wait_ge(pool_diff, k + 1)
                act(XSH[0][:, k, :], DF[:, k, :], ACT.Copy).then_inc(pool_hi, 1)
            act_norm(eng, 3, J_N3, lambda k: wait_emptied(eng, J_PW + KT - 1 if k == 0 else J_PW + KT - 2))
            eng.wait_ge(out_stored, 16 * OUT_BEFORE_F1)
            act_split(eng, U_F1)
            act_hi_norm(eng, 3)
            with eng.Fori(0, CHUNKS - 1) as i:
                act_ffn(eng, 1, i, False)
            act_ffn(eng, 1, CHUNKS - 1, True)
            act_norm(eng, 4, J_N4, lambda k: wait_emptied(eng, J_N4 - KT + k))
            for n in range(5):
                w = P if n < 4 else NS
                act_copy_out(eng, J_Y + n, YO[n][0:w, :].rearrange("p (e n) -> p e n", e=2), both(J_Y + n)[0:w])

        OUT_BEFORE_F1 = 2 + 1 + 8 + 2

        def act_hi_norm(eng, n):
            for k in range(KT):
                eng.wait_ge(hn_made, KT * n + k + 1)
                act(XSH[0][:, k, :], HN[:, k, :], ACT.Copy).then_inc(xhi_made, 1)

        tt, ts, stt = nc.vector.tensor_tensor, nc.vector.tensor_scalar, nc.vector.scalar_tensor_tensor

        def dve_split(eng, u, i=0):
            eng.wait_ge(raw_loaded[u % 2], i * (16 * FFN_U // 2) + 16 * (u // 2 + 1))
            eng.wait_ge(whi_made, i * FFN_U + u + 1)
            w = unit_width(u)
            b = u % 2
            tt(WLO[b][:, :, 0:w], RAW[b][:, :, 0:w], WHI[b][:, :, 0:w].bitcast(F32), SUB).then_inc(wlo_made, 1)

        def dve_norm(eng, n, j, gcol, dst):
            wait_emptied(eng, j)
            RS = RS1 if n else RS0
            nc.vector.reciprocal(RS[:], RS[:]).then_inc(rstd_made, 1)
            eng.wait_ge(rstd_made, n + 1)
            for k in range(KT):
                for d, cols in dst(k):
                    x_, r_ = X[:, k, cols], RS[:, cols]
                    if len(d.shape) == 3:
                        x_ = x_.rearrange("p (b t) -> p b t", b=NB)
                        r_ = r_.rearrange("p (b t) -> p b t", b=NB)
                    ins = stt(d, x_, col(gcol + k), r_, MUL, MUL)
                ins.then_inc(hn_made, 1)

        def dve_lo_norm(eng, n):
            for k in range(KT):
                eng.wait_ge(xhi_made, 48 + KT * {1: 0, 3: 1}[n] + k + 1)
                tt(XSL[0][:, k, :], HN[:, k, :], XSH[0][:, k, :].bitcast(F32), SUB).then_inc(xlo_made, 1)

        def dve_features(eng, A, n_tok, tok, rst, need, act_need, feature, wait_w, wait_a, norm2):
            bc = lambda c0: spread(PRM[:, c0:c0 + KT], n_tok)
            f = lambda ins: ins.then_inc(feature, 1)
            r_, k_ = R[:, :, tok], K[:, :, tok]
            f(tt(A["KQ"][:], k_, bc(KK_), MUL))
            need("KQ")
            f(tt(A["KSQ"][:], A["KQ"][:], A["KQ"][:], MUL))
            wait_w()
            f(ts(A["SG"][:], A["TW"][:], 0.5, 0.5, MUL, ADD))
            need("SG")
            f(nc.vector.tensor_tensor_scan(flat2(A["CS"]), rst, flat2(A["SG"]), 0.0, MUL, ADD))
            need("CS")
            f(tt(A["CX"][:], A["CS"][:], A["SG"][:], SUB))
            norm2()
            act_need("NR")
            f(nc.vector.reciprocal(A["NR"][:], A["NR"][:]))
            need("RI")
            f(tt(A["KK"][:], A["KQ"][:], A["NR"][:], MUL))
            need("KK")
            act_need("EX")
            f(stt(A["AT"][:], A["KK"][:], -1.0, A["EX"][:], MUL, MUL))
            wait_a()
            f(ts(A["AG"][:], A["TA"][:], 0.5, 0.5, MUL, ADD))
            need("AG")
            f(tt(A["BB"][:], A["KK"][:], A["AG"][:], MUL))
            need("BB")
            f(tt(A["BH"][:], A["BB"][:], A["EN"][:], MUL))
            f(ts(A["T1"][:], A["TA"][:], 0.5, 0.5, MUL, SUB))
            need("T1")
            f(tt(A["T1"][:], A["T1"][:], bc(KA_), MUL))
            need("T2")
            f(stt(A["KP"][:], A["T1"][:], 1.0, k_, ADD, MUL))
            need("KP")
            f(tt(A["KH"][:], A["KP"][:], A["EN"][:], MUL))
            f(tt(A["RT"][:], r_, A["EL"][:], MUL))

        def flat2(T3):
            return T3[:].rearrange("p a b -> p (a b)")

        def dve_features2(eng, A, n_tok, tok, chunk, need, feature):
            f = lambda ins: ins.then_inc(feature, 1)
            n = n_tok // chunk
            end = A["EL"][:].rearrange("p g (c t) -> p g c t", t=chunk)[:, :, :, chunk - 1:chunk]\
                .to_broadcast([P, KT, n, chunk])
            v4 = lambda T3: T3[:].rearrange("p g (c t) -> p g c t", t=chunk)
            f(tt(v4(A["BD"]), v4(A["BH"]), end, MUL))
            f(tt(v4(A["KD"]), v4(A["KH"]), end, MUL))
            f(tt(A["Z"][:], R[:, :, tok], A["KP"][:], MUL))
            need("Z")
            f(tt(A["Z"][:], A["Z"][:], spread(PRM[:, RK_:RK_ + KT], n_tok), MUL))

        def dve_tile(eng, i):
            tok = bass.ds(i * P, P)
            eng.wait_ge(filled, i * (2 * JP) + 2 * J_WKV)
            A = WT
            need = lambda name: w_dve(eng, i, name)

            def norm2():
                j = jw("norm2")
                for h in range(2):
                    w_filled(eng, i, "norm2", h)
                    ts(A["NR"][:, 4 * h:4 * h + 4, :].rearrange("p a b -> p (a b)"), bank(j, h), 1e-24, None, MAX)\
                        .then_inc(emptied[j % 4], 1)

            dve_features(eng, A, P, tok, RST[:, 0:KT * P], need, lambda n: w_act(eng, i, n), dve_feature,
                         lambda: w_kept(eng, i, "wpre"), lambda: w_kept(eng, i, "apre"), norm2)
            m3 = lambda T4, h: T4[:, h]
            b3 = lambda name, h: bank(jw(name), h).rearrange("p (a b) -> p a b", a=8)

            def masked(name, dsts):
                for h in range(2):
                    w_filled(eng, i, name, h)
                    for dst, mask in dsts:
                        ins = tt(m3(dst, h), b3(name, h), over(CC[mask], 8), MUL)
                    ins.then_inc(emptied[jw(name) % 4], 1)

            def added(name, dst):
                for h in range(2):
                    w_filled(eng, i, name, h)
                    tt(m3(dst, h), m3(dst, h), b3(name, h), ADD).then_inc(emptied[jw(name) % 4], 1)

            masked("MT", [(A["P1T"], "U8")])
            for h in range(2):
                w_kept(eng, i, "MT", h)
                tt(m3(A["XT"], h), m3(A["P1T"], h), over(CC["I64"], 8), ADD).then_inc(dve_sum, 1)
            masked("M", [(A["P1"], "L8"), (A["MO"], "LO")])
            masked("N", [(A["NM"], "LS")])
            dve_features2(eng, A, P, tok, HD, need, dve_feature)
            masked("RB", [(A["RBT"], "UI")])
            added("XT2", A["XT"])
            masked("RK", [(A["RKT"], "UI")])
            added("XT3", A["XT"])
            for h in range(2):
                w_kept(eng, i, "FT", h)
                tt(m3(A["Z1"], h), m3(A["FT"], h), over(CC["I64"], 8), ADD).then_inc(dve_sum, 1)
            added("Z2", A["Z1"])
            for h in range(2):
                w_filled(eng, i, "bonus", h)
                vv = V[:, 4 * h:4 * h + 4, tok]
                tt(vv, vv, bank(jw("bonus"), h).rearrange("p (a b) -> p a b", a=4), MUL).then_inc(emptied[jw("bonus") % 4], 1)
            added("Z3", A["Z1"])
            for c in range(2):
                end = A["EL"][:, :, (c + 1) * HD - 1:(c + 1) * HD].to_broadcast([P, KT, HD])
                w_state(eng, i, c)
                tt(STD[:], ST[:], end, MUL).then_inc(dve_sum, 1)
                w_sum(eng, i, f"STD{c}")
                w_filled(eng, i, f"SS{c}")
                tt(ST[:], STD[:], bank(jw(f"SS{c}"), 0).rearrange("p (a b) -> p a b", a=KT), ADD)\
                    .then_inc(emptied[jw(f"SS{c}") % 4], 2)
            w_kept(eng, i, "YS1")
            for h in range(2):
                w_filled(eng, i, "YU", h)
                rr = R[:, :, bass.ds(i * P + h * HD, HD)]
                tt(rr, rr, bank(jw("YU"), h).rearrange("p (a b) -> p a b", a=KT), ADD).then_inc(emptied[jw("YU") % 4], 1)

        def dve_samples(eng):
            A = SM
            need = lambda name: s_dve(eng, name)
            f = lambda ins: ins.then_inc(smp_dve, 1)
            tok = slice(SEQ, T)
            s8 = lambda j: bank(j, 0)[:, 0:KT * NS].rearrange("p (a b) -> p a b", a=KT)
            eng.wait_ge(emptied[J_STO % 4], 2 * (J_STO // 4) + 2)

            def norm2():
                j = js("norm2")
                wait_filled(eng, j)
                ts(A["NR"][:], s8(j), 1e-24, None, MAX).then_inc(emptied[j % 4], 2)

            dve_features(eng, A, NS, tok, RST[:, KT * P:], need, lambda n: s_act(eng, n), smp_dve,
                         lambda: wait_emptied(eng, js("wpre")), lambda: wait_emptied(eng, js("apre")), norm2)
            small = lambda j: both(j, KT * NS)[0:NS].rearrange("p e (a b) -> p e a b", a=KT)
            c4 = lambda name: CC[name][0:NS].unsqueeze(1).to_broadcast([NS, KT, NS])

            def masked(name, dst, mask):
                wait_filled(eng, js(name))
                for e in range(2):
                    ins = tt(dst[:, e], small(js(name))[:, e], c4(mask), MUL)
                    ins.then_inc(emptied[js(name) % 4], 1)

            masked("MT", A["P1T"], "SU")
            masked("M", A["P1"], "SL")
            masked("N", A["NM"], "SL")
            dve_features2(eng, A, NS, tok, DS, need, smp_dve)
            for e in range(2):
                ins = tt(A["XT"][:, e], A["P1T"][:, e], c4("SI"), ADD)
            f(ins)
            masked("RB", A["RBT"], "SUI")
            need("XT1")
            wait_filled(eng, js("XT2"))
            for e in range(2):
                tt(A["XT"][:, e], A["XT"][:, e], small(js("XT2"))[:, e], ADD).then_inc(emptied[js("XT2") % 4], 1)
            masked("RK", A["RKT"], "SUI")
            j = js("bonus")
            wait_filled(eng, j)
            tt(V[:, :, tok], V[:, :, tok], s8(j), MUL).then_inc(emptied[j % 4], 2)
            f(nc.vector.tensor_copy(A["DC"][:], A["EL"][:].rearrange("p g (b t) -> p g b t", t=DS)[:, :, :, DS - 1]))
            need("DC")
            wait_filled(eng, js("s0t3"))
            f(tt(DG[:].rearrange("p g b k -> p (g b) k"), over(CC["I64"], KT * NB),
                 spread(A["DC"][:].rearrange("p g b -> p (g b)"), HD), MUL))
            wait_filled(eng, js("YU"))
            wait_emptied(eng, js("UY"))
            tt(R[:, :, tok], R[:, :, tok], s8(js("YU")), ADD).then_inc(emptied[js("YU") % 4], 2)
            wait_emptied(eng, js("trK"))
            sel = CC["SB"][0:NS].unsqueeze(1).unsqueeze(3).to_broadcast([NS, 4, NB, HD])
            for q in range(4):
                if q:
                    wait_filled(eng, js(f"SO{q - 1}"))
                for tm, mk in ((A["B_TM"], MB), (A["K_TM"], MK)):
                    src = tm[:, 4 * q * HD:4 * (q + 1) * HD].rearrange("t (h k) -> t h k", h=4).unsqueeze(2)\
                        .to_broadcast([NS, 4, NB, HD])
                    f(tt(mk[:], src, sel, MUL))

        def dve_ffn(eng, l, i, last):
            u0, j0 = ((U_F0, J_F0), (U_F1, J_F1))[l]
            h0 = KT * CHUNKS * l
            for q in range(8):
                if not (last and q == 7):
                    dve_split(eng, u0 + q + 1, i)
                for m in (2 * q, 2 * q + 1):
                    j = j0 + m
                    if q < 4:
                        eng.wait_ge(emptied[j % 4], i * (FFN_J // 2) + 2 * (j // 4) + 2)
                        if m >= 2:
                            eng.wait_ge(hlo_made, i * KT + (h0 + m - 1))
                        tt(QL[:, m % 2, :], RL[:, m % 2, :], RL[:, m % 2, :], MUL).then_inc(square_made, 1)
                        if m >= 1:
                            dve_hidden_lo(eng, i, h0, m - 1)
                    else:
                        eng.wait_ge(filled, i * (2 * FFN_J) + 2 * j + 2)
                        tt(halves(X[:, m - 8, :]), halves(X[:, m - 8, :]), both(j, TH), ADD).then_inc(emptied[j % 4], 2)
                if q == 3:
                    dve_hidden_lo(eng, i, h0, 7)

        def dve_hidden_lo(eng, i, h0, m):
            eng.wait_ge(hhi_made, i * KT + (h0 + m + 1))
            tt(HL[:, m, :], QL[:, m % 2, :], HH[:, m, :].bitcast(F32), SUB).then_inc(hlo_made, 1)

        def run_dve(eng):
            nc.vector.memset(ST[:], 0.0).then_inc(pads_made, 1)
            nc.vector.memset(H[:, :, 0:1], 0.0).then_inc(pads_made, 1)
            wait_emptied(eng, J_PRM)
            nc.vector.tensor_copy(H[:, :, 513:553].rearrange("p k (b t) -> p k b t", b=NB)[:, :, :, 0],
                                  PRM2[:, SHF:SHF + 64].rearrange("p (b k) -> p k b", b=NB)).then_inc(pads_made, 1)
            ts(OMM[:], PRM[:, MIX:MIX + 48], -1.0, 1.0, MUL, ADD).then_inc(omm_made, 1)
            samples = lambda ap, lo, n: ap.rearrange("p (b t) -> p b t", b=NB)[:, :, lo:lo + n]
            dve_norm(eng, 0, J_N0, NMIX, lambda k: [(H[:, k, 1:513], slice(0, SEQ)),
                                                     (samples(H[:, k, 513:553], 1, DS), slice(SEQ, T))])
            eng.wait_ge(hn_made, KT)
            nc.vector.memset(WH[LW:LW + 1, :], 1.0).then_inc(pads_made, 1)
            nc.vector.memset(AH[LA:LA + 1, :], 1.0).then_inc(pads_made, 1)
            nc.vector.tensor_copy(SHT[:, :, 0:1], H[:, :, 512:513])
            nc.vector.tensor_copy(SHT[:, :, 1:9], H[:, :, 513:553].rearrange("p k (b t) -> p k b t", b=NB)[:, :, :, DS])\
                .then_inc(sht_made, 1)
            eng.wait_ge(omm_made, 1)

            def mixed(n):
                jx, k = n // 8, n % 8
                eng.wait_ge(xt_made, n + 1)
                c = 8 * XS_ORDER[jx] + k
                stt(XF[:, n % 2, 0:SEQ], H[:, k, 1:513], OMM[:, c:c + 1], XF[:, n % 2, 0:SEQ], MUL, ADD)
                d = XF[:, n % 2, SEQ:T].rearrange("p (b t) -> p b t", b=NB)
                stt(d, samples(H[:, k, 513:553], 1, DS), OMM[:, c:c + 1], d, MUL, ADD).then_inc(xf_made, 1)

            def mixed_lo(n):
                jx, k = n // 8, n % 8
                eng.wait_ge(xhi_made, n + 1)
                tt(XSL[jx % 2][:, k, :], XF[:, n % 2, :], XSH[jx % 2][:, k, :].bitcast(F32), SUB).then_inc(xlo_made, 1)

            for what, n in timeline():
                if what == "split":
                    dve_split(eng, n)
                elif what == "xs":
                    if n == 0:
                        mixed(0)
                    if n + 1 < 48:
                        mixed(n + 1)
                    mixed_lo(n)
                elif n in (J_G1, J_G1 + 1):
                    wait_emptied(eng, n)
                    g = GH[:, 0, :] if n == J_G1 else GH[0:LG - P, 1, :]
                    ts(g, g, 0.5, 0.5, MUL, ADD).then_inc(gsig_made, 1)
            eng.wait_ge(resets_loaded, 16)
            with eng.Fori(0, TILES) as i:
                dve_tile(eng, i)
            dve_samples(eng)
            for k in range(KT):
                j = J_GN + 3 * k
                wait_filled(eng, j)
                tt(halves(R[:, k, :]), halves(R[:, k, :]), both(j, TH), SUB).then_inc(emptied[j % 4], 2)
                wait_emptied(eng, j + 1)
                nc.vector.reciprocal(GR[:, k % 2, :], GR[:, k % 2, :]).then_inc(gn_step, 1)
                eng.wait_ge(gn_step, 4 * k + 1)
                tt(R[:, k, :], R[:, k, :], GR[:, k % 2, :], MUL).then_inc(gn_step, 1)
                eng.wait_ge(gn_step, 4 * k + 2)
                ts(R[:, k, :], R[:, k, :], col(GNW + k), col(GNB + k), MUL, ADD).then_inc(gn_step, 1)
                eng.wait_ge(gn_step, 4 * k + 3)
                tt(R[:, k, :], R[:, k, :], V[:, k, :], ADD).then_inc(gn_step, 1)
                eng.wait_ge(gn_step, 4 * k + 4)
                wait_filled(eng, j + 2)
                tt(halves(R[:, k, :]), halves(R[:, k, :]), both(j + 2, TH), MUL).then_inc(emptied[(j + 2) % 4], 2)
                eng.wait_ge(gn_hi, k + 1)
                tt(XSL[1][:, k, :], R[:, k, :], XSH[1][:, k, :].bitcast(F32), SUB).then_inc(gn_lo, 1)
            dve_split(eng, U_WO)
            for n in range(4):
                if n < 3:
                    dve_split(eng, U_WO + n + 1)
                for m in (2 * n, 2 * n + 1):
                    j = J_WO + m
                    wait_filled(eng, j)
                    tt(halves(X[:, m, :]), halves(X[:, m, :]), both(j, TH), ADD).then_inc(emptied[j % 4], 2)
            dve_split(eng, U_F0)
            whole = lambda k: [(HN[:, k, :], slice(0, T))]
            dve_norm(eng, 1, J_N1, NFFN, whole)
            dve_lo_norm(eng, 1)
            with eng.Fori(0, CHUNKS - 1) as i:
                dve_ffn(eng, 0, i, False)
            dve_ffn(eng, 0, CHUNKS - 1, False)
            SEG = PBUF + DS
            S0_ = PBUF + SEQ
            wait_filled(eng, J_N2)
            nc.vector.memset(EXT[:, :, 0:PBUF], 0.0)
            dve_norm(eng, 2, J_N2, NMIX + 8, lambda k: [(EXT[:, k, PBUF:S0_], slice(0, SEQ)),
                                                         (samples(EXT[:, k, S0_:], PBUF, DS), slice(SEQ, T))])
            wait_filled(eng, J_PST)
            for k in range(KT):
                ins = nc.vector.tensor_copy(samples(EXT[:, k, S0_:], 0, PBUF),
                                            bank(J_PST, k // 4)[:, (k % 4) * 120:(k % 4 + 1) * 120]
                                            .rearrange("p (b t) -> p b t", b=NB))
                if k % 4 == 3:
                    ins.then_inc(emptied[J_PST % 4], 1)
            wait_emptied(eng, J_PST)
            eng.wait_ge(hn_made, 3 * KT)
            for k in range(KT):
                ins = nc.vector.tensor_copy(PCO[:, k], samples(EXT[:, k, S0_:], DS, PBUF))
            ins.then_inc(pool_cols, 1)
            wins = 0
            for g, w in enumerate(POOLS):
                src = EXT[:, 2 * g:2 * g + 2, :]
                if g:
                    eng.wait_ge(pool_diff, 2 * g)
                step, b = 1, 0
                while step < w:
                    dst = WS[b][:]
                    tt(dst[:, :, 2 * step - 1:], src[:, :, 2 * step - 1:], src[:, :, step - 1:-step], ADD).then_inc(pool_win, 1)
                    wins += 1
                    eng.wait_ge(pool_win, wins)
                    src, step, b = dst, 2 * step, 1 - b
                for kk in range(2):
                    k = 2 * g + kk
                    head = src[:, kk, PBUF:PBUF + 16]
                    tt(head, head, CC[f"corr{w}"], MUL).then_inc(pool_win, 1)
                    wins += 1
                    eng.wait_ge(pool_win, wins)
                    stt(DF[:, k, 0:SEQ], src[:, kk, PBUF:S0_], 1.0 / w, EXT[:, k, PBUF:S0_], MUL, SUB)
                    stt(samples(DF[:, k, SEQ:T], 0, DS), samples(src[:, kk, S0_:], PBUF, DS), 1.0 / w,
                        samples(EXT[:, k, S0_:], PBUF, DS), MUL, SUB).then_inc(pool_diff, 1)
            for k in range(KT):
                eng.wait_ge(pool_hi, k + 1)
                tt(XSL[0][:, k, :], DF[:, k, :], XSH[0][:, k, :].bitcast(F32), SUB).then_inc(pool_lo, 1)
            for m in range(KT):
                j = J_PW + m
                wait_filled(eng, j)
                stt(halves(X[:, m, :]), both(j, TH), PRM2[:, PSC + m:PSC + m + 1], halves(X[:, m, :]), MUL, ADD)\
                    .then_inc(emptied[j % 4], 2)
            dve_split(eng, U_F1)
            dve_norm(eng, 3, J_N3, NFFN + 8, whole)
            dve_lo_norm(eng, 3)
            with eng.Fori(0, CHUNKS - 1) as i:
                dve_ffn(eng, 1, i, False)
            dve_ffn(eng, 1, CHUNKS - 1, True)
            dve_norm(eng, 4, J_N4, NFIN, whole)

        block = ctx.enter_context(nc.Block())

        @block.sync
        def _(sp):
            run_sp(sp)

        @block.tensor
        def _(pe):
            run_pe(pe)

        @block.scalar
        def _(eng):
            run_act(eng)

        @block.vector
        def _(eng):
            run_dve(eng)


OUTS = (("y_prompt", (1, SEQ, D)), ("y_sample", (NB, DS, D)), ("wkv_prompt", (1, 1, NH, HD, HD)),
        ("shift_prompt", (1, 1, D)), ("pool_prompt", (1, 1, PBUF, D)), ("wkv_sample", (1, NB, NH, HD, HD)),
        ("shift_sample", (1, NB, D)), ("pool_sample", (1, NB, PBUF, D)))
UNUSED = ("rwkv_v0", "rwkv_v1", "rwkv_v2")


def kernel(**inputs):
    import numpy as np
    import concourse.bacc as bacc
    from concourse import mybir
    from concourse.bass_utils import run_bass_kernel_spmd

    nc = bacc.Bacc("TRN2", target_bir_lowering=False, num_devices=1)
    table, _, resets = constants()
    arrays = {n: np.ascontiguousarray(v) for n, v in inputs.items() if n not in UNUSED}
    arrays |= {"const_table": table, "resets": resets}
    a = {n: nc.dram_tensor(f"in_{n}", v.shape, mybir.dt.from_np(v.dtype), kind="ExternalInput").ap()
         for n, v in arrays.items()}
    o = {n: nc.dram_tensor(f"out_{n}", s, mybir.dt.float32, kind="ExternalOutput").ap() for n, s in OUTS}
    build(nc, a, o)
    r = run_bass_kernel_spmd(nc, [{f"in_{n}": v for n, v in arrays.items()}], core_ids=[0])
    return tuple(r.results[0][f"out_{n}"] for n, _ in OUTS)
```

```python
from contextlib import ExitStack

import numpy as np
import concourse.bass as bass
from concourse import mybir

F32 = mybir.dt.float32
F32R = mybir.dt.float32r
ALU = mybir.AluOpType
ACT = mybir.ActivationFunctionType
MUL, ADD, SUB, MAX, BYP = ALU.mult, ALU.add, ALU.subtract, ALU.max, ALU.bypass

P = 128
D = 1024
KT = D // P
SEQ, NB, DS = 512, 8, 4
NS = NB * DS
T = SEQ + NS
TH = T // 2
HD, NH = 64, 16
DFF = 4 * D
UW = 256
POOLS = (2, 4, 8, 16)
PBUF = 15
GROUP_ORDER = (3, 2, 1, 0)
POOL_ORDER = [2 * g + e for g in GROUP_ORDER for e in range(2)]
LW, LA, LG = 64, 64, 160
DECAY = float(np.exp(-0.5))
NORM_EPS, GN_EPS = 1e-6, 64e-5

NMIX, NFFN, NFIN, MIX = 0, 16, 32, 40
KK_, KA_, RK_, GNW, GNB = 88, 96, 104, 112, 120
PSC, SHF = 0, 8
XS_ORDER = (3, 4, 5, 0, 1, 2)

U_W1, U_A1, U_G1, U_RKV, U_WO = 0, 1, 2, 3, 15
U_F0 = 19
U_POOL = U_F0 + 32
U_F1 = U_POOL + 1
FFN_U, FFN_J = 8, 16
CHUNKS = DFF // D

J_X, J_PRM, J_N0 = 0, 5, 6
J_W1, J_A1, J_G1, J_R, J_K, J_V = 7, 8, 9, 11, 19, 27
V_SEQ = ("V0", "V1", "V2", "V3", "wpre", "apre", "norm2", "V4", "V5", "norm3", "V6", "V7")
J_SHO = J_V + len(V_SEQ)
PREP_JOBS = ("wpre", "apre", "norm2", "norm3")
J_WKV = J_SHO + 1
WKV_JOBS = ("Q0", "Q1", "Q2", "Q3", "M", "P2", "P2T", "bonus", "XT2", "P4", "tb0", "XT3", "tb1", "X", "wpre", "F",
            "apre", "FT", "tv0", "F2", "tv1", "T1a", "T1b", "norm2", "T2", "F4", "NV", "T3", "AS0", "norm3", "U0",
            "SY0", "AS1", "U1", "SY1", "YU")
LAST_JOBS = [n for n in WKV_JOBS if n not in PREP_JOBS]
JP = len(WKV_JOBS)
assert JP % 4 == 0 and len(PREP_JOBS) == 4
TILES = SEQ // P
J_LAST = J_WKV + JP * (TILES - 1)
J_STO = J_LAST + len(LAST_JOBS)
SMP_JOBS = ("wpre", "apre", "norm2", "s0t0", "s0t1", "s0t2", "s0t3", "Q", "M", "P2", "tBK", "XT2", "tV", "bonus", "GY",
            "tG", "U", "YU", "SS0", "SS1", "TO0", "TO1", "SS2", "TO2", "TO3", "SS3", "TO4", "TO5", "TO6", "TO7")
J_SMP = J_STO + 1
J_GN = J_SMP + len(SMP_JOBS)
GN_JOBS = ([("mean", k) for k in range(KT)] + [("gate", k) for k in range(4)] + [("var", 0)]
           + [("gate", k) for k in range(4, KT)] + [("spread", k) for k in range(KT)])
J_WO = J_GN + len(GN_JOBS)
J_N1 = J_WO + KT
J_F0 = J_N1 + 1
J_N2 = J_F0 + FFN_J * CHUNKS
J_PST = J_N2 + 1
J_PW = J_PST + 1
J_PO = J_PW + 6
J_N3 = J_PW + KT + 2
J_F1 = J_N3 + 1
J_N4 = J_F1 + FFN_J * CHUNKS
J_Y = J_N4 + 1
J_YT = J_Y + 1

DVE_PREP = ("KQ", "KSQ", "SG", "CS", "CX", "T1", "KP", "RI", "BB", "BH", "KH", "BD", "KD", "Z", "ZR", "AT", "ELE", "RT")
ACT_PREP = ("EL", "EN", "EX", "NR")
FIRST = {DVE_PREP: ("KQ", "KSQ", "SG", "CS", "CX", "RI", "T1", "KP", "BB", "BH", "KH", "AT", "ELE", "RT", "BD", "KD", "Z",
                    "ZR"), ACT_PREP: ("EL", "EN", "NR", "EX")}
DVE_SUMS = ("XT1a", "XT1b", "STD0", "STD1")
DVE_FEATURES = ("KQ", "KSQ", "SG", "CS", "CX", "RI", "KK", "AT", "AG", "BB", "BH", "T1", "T2", "KP", "KH", "RT", "BD",
                "KD", "Z", "ZR")
ACT_FEATURES = ("NR", "EL", "EN", "EX")
SMP_ACT = ACT_FEATURES + ("UM0", "UM1", "UM2", "UM3")
SMP_DVE = DVE_FEATURES + ("XT1", "DC", "SW0", "SW1", "SW2", "SW3")


def constants():
    s = np.arange(P)[:, None]
    c = np.arange(HD)[None, :]
    r = s % HD
    same8 = (r // 8) == (c // 8)
    e = np.arange(P)[None, :]
    parts = {
        "ident": (s == e), "ones": np.ones((P, P)), "bones": (s // HD == e // HD),
        "bmean": (s // HD == e // HD) / HD,
        "U8": (c > r) & same8, "L8": (c < r) & same8, "UO": (c > r) & ~same8, "US": c > r, "UI": c >= r,
        "I64": c == r,
    }
    q = np.arange(NS)[None, :]
    sameb = (s % NS) // DS == q // DS
    parts |= {"SU": (q > s % NS) & sameb, "SL": (q < s % NS) & sameb, "SUI": (q >= s % NS) & sameb,
              "SI": q == s % NS, "SB": (s % NS) // DS == np.arange(NB)[None, :]}
    t = np.arange(16)[None, :]
    for w in POOLS:
        parts[f"corr{w}"] = np.broadcast_to(w / np.minimum(t + 1, w), (P, 16))
    parts["headsum"] = (np.arange(30)[None, :] - 14) == s // HD
    parts["eps"] = np.broadcast_to(np.array([[NORM_EPS, GN_EPS]]), (P, 2))
    at, n = {}, 0
    for k, v in parts.items():
        at[k] = (n, v.shape[1])
        n += v.shape[1]
    table = np.concatenate([np.asarray(v, np.float32) for v in parts.values()], axis=1).astype(np.float32)
    resets = np.ones((1, KT * P + KT * NS), np.float32)
    resets[0, 0:KT * P:HD] = 0
    resets[0, KT * P::DS] = 0
    n = np.arange(NH)[:, None, None]
    headrow = (n // 2 == np.arange(KT)[None, :, None]) & (n % 2 == np.arange(P)[None, None, :] // HD)
    return table, at, resets, headrow.reshape(NH, KT * P).astype(np.float32)


def build(nc, a, o):
    table, CAT, _, _ = constants()
    ctx = ExitStack()
    with ctx:
        cursor = [(nc.sbuf_base + 31) // 32 * 32]

        def region(nbytes):
            off = cursor[0]
            cursor[0] += (nbytes + 31) // 32 * 32
            assert cursor[0] <= nc.sbuf_usable_end, (cursor[0], nc.sbuf_usable_end)
            return off

        def at(name, shape, off, dt=F32):
            return nc.alloc_sbuf_tensor_at(name, shape, dt, offset=off)

        def sem(name):
            return ctx.enter_context(nc.semaphore(name))

        FB = 4 * KT * T
        X = at("x_res", [P, KT, T], region(FB))
        CT = at("const_sb", [P, table.shape[1]], region(4 * table.shape[1]))
        PRM = at("params", [P, P], region(4 * P))
        PRM2 = at("params2", [P, 72], region(4 * 72))
        o_rst = region(4 * (KT * P + KT * NS))
        XF = at("xs_full", [P, 2, T], o_rst)
        RST = at("resets_sb", [P, KT * P + KT * NS], o_rst)
        o_raw, o_w = region(2 * 8192), region(4 * 8192)
        RAW = [at(f"w_raw{b}", [P, KT, UW], o_raw + 8192 * b) for b in range(2)]
        WHI = [at(f"w_hi{b}", [P, KT, UW], o_w + 8192 * b, F32R) for b in range(2)]
        WLO = [at(f"w_lo{b}", [P, KT, UW], o_w + 8192 * (2 + b), F32R) for b in range(2)]
        o_a, o_b, o_h, o_l = region(4 * FB), region(2 * FB), region(4 * KT * 553), region(4 * 4 * T)
        o_s = region(4096)
        XSH = [at(f"xs_hi{b}", [P, KT, T], o_a + 2 * FB * b, F32R) for b in range(2)]
        XSL = [at(f"xs_lo{b}", [P, KT, T], o_a + 2 * FB * b + FB, F32R) for b in range(2)]
        R = at("r_all", [P, KT, T], o_b)
        K = at("k_all", [P, KT, T], o_b + FB)
        H = at("h_shift", [P, KT, 553], o_h)
        V = at("v_all", [P, KT, T], o_h)
        WH = at("w_hidden", [P, T], o_l)
        AH = at("a_hidden", [P, T], o_l + 4 * T)
        GH = at("g_hidden", [P, 2, T], o_l + 8 * T)
        ST = at("state", [P, KT, HD], o_s)
        STD = at("state_decayed", [P, KT, HD], o_s + 2048)
        SHT = at("shift_cols", [P, KT, 9], o_s + 2048)
        XIN = at("x_rows", [P, 5, D], o_a)
        PR = at("param_rows", [P, P], o_w)
        PR2 = at("param_rows2", [72, P], o_w + 512)
        SQ = at("squares", [P, KT, T], o_b)
        HN = at("normed", [P, KT, T], o_b + FB)
        DX = at("shift_diff", [P, KT, T], o_b + FB)
        RS0, RS1 = at("rstd0", [P, T], o_l), at("rstd1", [P, T], o_h)
        slots = [o_a + 4096 * n for n in range(17)]
        feat, TMs = slots[0:9], slots[9:13]
        rw = lambda n: o_raw + 4096 * n
        ww = lambda n: o_w + 4096 * n
        W2A, A2A = at("w2_aug", [P, D], slots[6]), at("a2_aug", [P, D], slots[7])
        AR = at("rates_recept", [P, 2 * KT, 2, HD], slots[8])
        BKH = at("b_k_hat", [P, 2 * KT, 2, HD], slots[0])
        BKD = at("b_k_decayed", [P, 2 * KT, 2, HD], slots[2])
        WT = {}
        slots += [ww(6), ww(7)]
        for name, n in (("TA", 0), ("KSQ", 1), ("TW", 2), ("SG", 2), ("CX", 2), ("BB", 2), ("CS", 3), ("EN", 3),
                        ("EL", 4), ("KQ", 5), ("KK", 5), ("VC", 12), ("T1", 17), ("KP", 17), ("Z", 17), ("EX", 18)):
            WT[name] = at("wkv_" + name, [P, KT, P], slots[n])
        for name, off in (("P1T", slots[10]), ("F", slots[10]), ("P1", slots[11]), ("F2T", slots[11]),
                          ("P2", slots[13]), ("F2", slots[13]), ("P2T", slots[14]), ("F4", slots[14]),
                          ("P4", ww(4)), ("X", ww(4)), ("OT", ww(5)), ("NV", slots[12])):
            WT[name] = at("wkv_" + name, [P, 2, KT, HD], off)
        FX = at("wkv_FT_XT", [P, 2, KT, 2, HD], slots[15])
        NT = at("wkv_NT", [P, 2, 2 * KT, HD], rw(0))
        HROWS = slice(96, 96 + NH)
        HR = at("head_rows", [P, KT, P], o_l)[HROWS]
        RBK = at("wkv_RBK", [P, 2, 2 * KT, HD], rw(2))
        UV = at("wkv_UV", [P, 2, D], ww(0))
        BKT = at("wkv_BKT", [P, 2, D], ww(2))
        o_x = region(64 + 512 + 32)
        HKA = at("half_k_a", [P, KT], o_x + 576)
        ELE = at("chunk_decay", [P, KT, 2], o_x)
        NRM = at("head_norms", [P, P], o_x + 64)[HROWS]
        SHO = at("shift_rows", [9, D], TMs[3])
        STO = at("state_rows", [HD, D], ww(4))
        SM = {}
        unit = lambda n: feat[n // 4] + 1024 * (n % 4)
        for name, n in (("TW", 0), ("SG", 0), ("CX", 0), ("AG", 0), ("BB", 0), ("CS", 1), ("EL", 2), ("EN", 3), ("EX", 4),
                        ("TA", 5), ("T1", 5), ("KP", 5), ("KQ", 6), ("KK", 6), ("Z", 6), ("KSQ", 7), ("NR", 7),
                        ("GT", 14)):
            SM[name] = at("smp_" + name, [P, KT, NS], unit(n))
        for name, first, second, n in (("AR", "AT", "RT", 8), ("BKH", "BH", "KH", 10), ("BKD", "BD", "KD", 12)):
            SM[name] = at("smp_" + name, [P, KT, 2, NS], unit(n))
            SM[first], SM[second] = SM[name][:, :, 0, :], SM[name][:, :, 1, :]
        SM["DC"] = at("smp_DC", [P, KT, NB], unit(15))
        for n, name in enumerate(("P1T", "P1", "NT", "RBK", "XT", "P2")):
            SM[name] = at("smp_" + name, [2 * NS, 2, KT, NS], feat[4] + 2048 * n)
        SM["BKT"] = at("smp_BKT", [2 * NS, D], feat[7])
        SM["UV"] = at("smp_UV", [2 * NS, D], feat[8])
        SM["G"] = at("smp_G", [NS, D], TMs[0])
        UVM = [at(f"smp_uv_masked{n}", [2 * NS, 2, D], slots[10] + 8192 * n) for n in range(2)]
        S0L = at("smp_state_rows", [HD, NB, NH, HD], o_raw)
        S0T = at("smp_state", [P, NB, KT, HD], o_b + FB)
        SO = at("smp_state_out", [HD, NB, D], o_raw)
        G2A, G2B = at("g2_a", [P, D], o_a), at("g2_b", [LG - P, D], o_a + 4096)
        GG = at("gn_gate", [P, KT, T], o_a + 8192)
        GR = at("gn_rstd", [P, T], o_a + 8192 + FB)[HROWS]
        GQ = at("gn_squares", [P, KT, T], o_b + FB)
        EXT = at("pool_ext", [P, KT, PBUF + SEQ + NB * (PBUF + DS)], o_b)
        WS = [at(f"pool_sum{b}", [P, 2, PBUF + SEQ + NB * (PBUF + DS)], o_a + 2 * FB + 5440 * b) for b in range(2)]
        DF = at("pool_diff", [P, KT, T], o_a + 2 * FB + 11264)
        PSI = at("pool_state_rows", [P, D], o_l)
        PCO = at("pool_out_cols", [P, KT, NB, PBUF], o_l + 4096)
        PRO = [at(f"pool_out_rows{n}", [P, D], o_h + 4096 * (1 + n)) for n in range(2)]
        S0_ = PBUF + SEQ
        HH, HL = XSH[1], XSL[1]
        RL = at("relu_tmp", [P, 2, T], o_l)
        QL = at("square_tmp", [P, 2, T], o_l + 8 * T)
        YR = at("y_rstd", [P, 5], o_h + 4 * T)
        YO = [at(f"y_rows{n}", [P, D], o_a + 4096 * n) for n in range(5)]

        CC = {k: CT[:, n:n + w] for k, (n, w) in CAT.items()}
        ident, ones, bones, bmean = (CC[k] for k in ("ident", "ones", "bones", "bmean"))

        PS = ctx.enter_context(nc.psum_tensor("ps", [P, 8, 512], F32))

        def bank(j, half):
            return PS[:, 2 * (j % 4) + half, :]

        def both(j, n=512):
            return PS[:, 2 * (j % 4):2 * (j % 4) + 2, 0:n]

        def halves(ap):
            return ap.rearrange("p (a t) -> p a t", a=2)

        def col(n):
            return PRM[:, n:n + 1]

        def spread(ap, n):
            return ap.unsqueeze(2).to_broadcast([ap.shape[0], ap.shape[1], n])

        def over(ap, n):
            return ap.unsqueeze(1).to_broadcast([ap.shape[0], n, ap.shape[1]])

        filled = sem("psum_filled")
        emptied = [sem(f"psum_emptied{n}") for n in range(4)]
        raw_loaded = [sem(f"raw_loaded{b}") for b in range(2)]
        whi_made, wlo_made = sem("whi_made"), sem("wlo_made")
        const_loaded, x_loaded, prm_loaded = sem("const_loaded"), sem("x_loaded"), sem("prm_loaded")
        pads_made = sem("pads_made")
        sq_made, rstd_made, hn_made = sem("sq_made"), sem("rstd_made"), sem("hn_made")
        dx_made, xf_made, xhi_made, xlo_made = sem("dx_made"), sem("xf_made"), sem("xhi_made"), sem("xlo_made")
        gsig_made = sem("gsig_made")
        aug_loaded, resets_loaded, s0_loaded, g2_loaded, pst_loaded = (sem(n) for n in (
            "aug_loaded", "resets_loaded", "s0_loaded", "g2_loaded", "pst_loaded"))
        out_stored, sht_made = sem("out_stored"), sem("sht_made")
        headrow_loaded, vc_made = sem("headrow_loaded"), sem("vc_made")
        settled, ys_filled = sem("settled"), sem("ys_filled")
        square_made, hhi_made, hlo_made = sem("square_made"), sem("hhi_made"), sem("hlo_made")
        dve_prep, act_prep, dve_sum = sem("dve_prep"), sem("act_prep"), sem("dve_sum")
        smp_dve, smp_act = sem("smp_dve_feature"), sem("smp_act_feature")
        gn_squared, gn_rstd, gn_step, gn_gated, gn_hi, gn_lo = (sem(n) for n in (
            "gn_squared", "gn_rstd", "gn_step", "gn_gated", "gn_hi", "gn_lo"))
        pool_win, pool_diff, pool_hi, pool_lo = (sem(n) for n in ("pool_window", "pool_diff", "pool_hi", "pool_lo"))
        pool_cols = sem("pool_cols")

        def wait_filled(eng, j, half=1):
            eng.wait_ge(filled, 2 * j + half + 1)

        def wait_emptied(eng, j, half=1):
            eng.wait_ge(emptied[j % 4], 2 * (j // 4) + half + 1)

        def wait_free(pe, j, half=1):
            if j >= 4:
                wait_emptied(pe, j - 4, half)

        def jv(name):
            return J_V + V_SEQ.index(name)

        def spot(i, name):
            if i is None:
                return jv(name), 0
            if isinstance(i, int):
                return J_LAST + LAST_JOBS.index(name), 0
            return J_WKV + WKV_JOBS.index(name), i

        def jw(i, name):
            return spot(i, name)[0]

        def jg(what, k):
            return J_GN + GN_JOBS.index((what, k))

        def js(name):
            return J_SMP + SMP_JOBS.index(name)

        def w_filled(eng, i, name, half=1):
            j, n = spot(i, name)
            eng.wait_ge(filled, n * (2 * JP) + (2 * j + half + 1))

        def w_kept(eng, i, name, half=1):
            j, n = spot(i, name)
            eng.wait_ge(emptied[j % 4], n * (JP // 2) + (2 * (j // 4) + half + 1))

        def w_free(pe, i, name):
            j, n = spot(i, name)
            pe.wait_ge(emptied[j % 4], n * (JP // 2) + 2 * ((j - 4) // 4) + 2)

        def prep_count(i, names, name):
            return FIRST[names].index(name) + 1 if i is None else (i + 1) * len(names) + names.index(name) + 1

        def w_prep(eng, i, name):
            eng.wait_ge(dve_prep, i * len(DVE_PREP) + DVE_PREP.index(name) + 1)

        def w_sum(eng, i, name):
            eng.wait_ge(dve_sum, i * len(DVE_SUMS) + DVE_SUMS.index(name) + 1)

        def s_dve(eng, name):
            eng.wait_ge(smp_dve, SMP_DVE.index(name) + 1)

        def s_act(eng, name):
            eng.wait_ge(smp_act, SMP_ACT.index(name) + 1)

        ORDER = {n: list(range(KT)) for n in (0, 1, 2, 4)} | {3: POOL_ORDER}

        def jy(n):
            return J_Y if n == 0 else J_YT + n

        def jpw(m):
            return J_PW + POOL_ORDER.index(m) + (2 if m in POOL_ORDER[6:] else 0)

        def last_job(u):
            if u < U_RKV:
                return (J_W1, J_A1, J_G1 + 1)[u]
            if u < U_WO:
                return J_R + 2 * (u - U_RKV) + 1 if u < U_RKV + 8 else jv(f"V{2 * (u - U_RKV) - 15}")
            if u < U_F0:
                return J_WO + 2 * (u - U_WO) + 1
            if u < U_POOL:
                return J_F0 + 2 * (u - U_F0) + 1
            return J_PW + KT + 1 if u == U_POOL else J_F1 + 2 * (u - U_F1) + 1

        w1_v = a["rwkv_w1"][0].rearrange("(k p) n -> p k n", p=P)
        a1_v = a["rwkv_a1"][0].rearrange("(k p) n -> p k n", p=P)
        g1_v = a["rwkv_g1"][0].rearrange("(k p) n -> p k n", p=P)
        rkv_v = a["rwkv_w_rkv"][0].rearrange("j (k p) n -> j p k n", p=P)
        wo_v = a["rwkv_w_o"][0].rearrange("(k p) n -> p k n", p=P)
        up_v = [a["ffn_w1"][l].rearrange("(k p) (c n) -> p k c n", p=P, n=D) for l in range(2)]
        dn_v = [a["ffn_w2"][l].rearrange("(c k p) n -> c p k n", p=P, k=KT) for l in range(2)]
        pool_v = a["pool_w"][0].rearrange("g (k p) n -> p (g k) n", p=P)

        def unit_width(u):
            return {U_W1: LW, U_A1: LA, U_G1: LG}.get(u, UW)

        def sp_unit(sp, u, src, i=0):
            if u >= 2:
                sp.wait_ge(whi_made, i * FFN_U + u - 1)
                sp.wait_ge(wlo_made, i * FFN_U + u - 1)
            sp.dma_start(RAW[u % 2][:, :, 0:unit_width(u)], src).then_inc(raw_loaded[u % 2], 16)

        def store(sp, dst, src):
            sp.dma_start(dst, src).then_inc(out_stored, 16)
            stores[0] += 1

        stores = [0]

        def sp_ffn(sp, l, i):
            u0 = (U_F0, U_F1)[l]
            for q in range(4):
                sp_unit(sp, u0 + q, up_v[l][:, :, i, q * UW:(q + 1) * UW], i)
            for q in range(4):
                sp_unit(sp, u0 + 4 + q, dn_v[l][i, :, :, q * UW:(q + 1) * UW], i)

        def run_sp(sp):
            sp.dma_start(CT[:], a["const_table"]).then_inc(const_loaded, 16)
            xp = a["x_prompt"][0].rearrange("(a p) d -> a p d", p=P)
            for n in range(4):
                sp.dma_start(XIN[:, n, :], xp[n]).then_inc(x_loaded, 16)
            sp.dma_start(XIN[0:NS, 4, :], a["x_sample"].rearrange("b t d -> (b t) d")).then_inc(x_loaded, 16)
            rows = lambda ap: ap.rearrange("a (k p) -> (a k) p", p=P)
            for name, r0, n in (("norm_mix", NMIX, 2), ("norm_ffn", NFFN, 2), ("rwkv_k_k", KK_, 1), ("rwkv_k_a", KA_, 1),
                                ("rwkv_gn_w", GNW, 1), ("rwkv_gn_b", GNB, 1)):
                sp.dma_start(PR[r0:r0 + 8 * n, :], rows(a[name])).then_inc(prm_loaded, 16)
            sp.dma_start(PR[NFIN:NFIN + 8, :], a["norm_final"].rearrange("(k p) -> k p", p=P)).then_inc(prm_loaded, 16)
            sp.dma_start(PR[MIX:MIX + 48, :], rows(a["rwkv_mix"][0])).then_inc(prm_loaded, 16)
            sp.dma_start(PR[RK_:RK_ + 8, :], a["rwkv_r_k"][0].rearrange("(k e) d -> k (e d)", e=2)).then_inc(prm_loaded, 16)
            sp.dma_start(PR2[PSC:PSC + 8, :], rows(a["pool_scale"])).then_inc(prm_loaded, 16)
            sp.dma_start(PR2[SHF:SHF + 64, :], a["state_shift"][0].rearrange("b (k p) -> (b k) p", p=P)).then_inc(prm_loaded, 16)
            sp_unit(sp, U_W1, w1_v)
            sp_unit(sp, U_A1, a1_v)
            sp_unit(sp, U_G1, g1_v)
            def sp_rkv(n):
                sp_unit(sp, U_RKV + n, rkv_v[n // 4, :, :, (n % 4) * UW:(n % 4 + 1) * UW])

            for n in range(8):
                sp_rkv(n)
            sp.wait_ge(hn_made, KT)
            sp.dma_start(HR[:], a["head_rows"].rearrange("n (k p) -> n k p", k=KT)).then_inc(headrow_loaded, 16)
            sp.wait_ge(xlo_made, 48)
            sp.dma_start(RST[:], a["resets"].to_broadcast([P, KT * P + KT * NS])).then_inc(resets_loaded, 16)
            for n in (8, 9):
                sp_rkv(n)
            wait_filled(sp, J_K + 7)
            sp.dma_start(W2A[0:LW, :], a["rwkv_w2"][0]).then_inc(aug_loaded, 16)
            sp.dma_start(W2A[LW:LW + 1, :], a["rwkv_w0"]).then_inc(aug_loaded, 16)
            sp.dma_start(A2A[0:LA, :], a["rwkv_a2"][0]).then_inc(aug_loaded, 16)
            sp.dma_start(A2A[LA:LA + 1, :], a["rwkv_a0"]).then_inc(aug_loaded, 16)
            for n in (10, 11):
                sp_rkv(n)
            wait_emptied(sp, J_SHO)
            store(sp, o["shift_prompt"][0], SHO[0:1, :])
            store(sp, o["shift_sample"][0], SHO[1:9, :])
            wait_filled(sp, J_STO - 1)
            for b in range(NB):
                sp.dma_start(S0L[:, b], a["state_wkv"][0, b].rearrange("h v k -> v h k")).then_inc(s0_loaded, 16)
            wait_emptied(sp, J_STO)
            store(sp, o["wkv_prompt"][0, 0].rearrange("h v k -> v h k"), STO[:].rearrange("v (h k) -> v h k", k=HD))
            wait_emptied(sp, js("GY"))
            sp.dma_start(G2A[:], a["rwkv_g2"][0, 0:P]).then_inc(g2_loaded, 16)
            sp.dma_start(G2B[:], a["rwkv_g2"][0, P:LG]).then_inc(g2_loaded, 16)
            for b in range(NB):
                wait_emptied(sp, js(f"TO{b}"))
                store(sp, o["wkv_sample"][0, b].rearrange("h v k -> v h k"), SO[:, b].rearrange("v (h k) -> v h k", k=HD))
            sp.wait_ge(out_stored, 16 * stores[0])
            for n in range(4):
                sp_unit(sp, U_WO + n, wo_v[:, :, n * UW:(n + 1) * UW])
            with sp.Fori(0, CHUNKS) as i:
                sp_ffn(sp, 0, i)
            sp_unit(sp, U_POOL, pool_v)
            wait_filled(sp, J_N2)
            sp.dma_start(PSI[0:NB * PBUF, :], a["state_pool"][0].rearrange("b t d -> (b t) d")).then_inc(pst_loaded, 16)
            for n in range(2):
                sp_unit(sp, U_F1 + n, up_v[1][:, :, 0, n * UW:(n + 1) * UW])
            wait_emptied(sp, J_PO)
            store(sp, o["pool_prompt"][0, 0], PRO[0][0:PBUF, :])
            wait_emptied(sp, J_PO + 1)
            store(sp, o["pool_sample"][0].rearrange("b t d -> (b t) d"), PRO[1][0:NB * PBUF, :])
            for q in range(2, 4):
                sp_unit(sp, U_F1 + q, up_v[1][:, :, 0, q * UW:(q + 1) * UW])
            for q in range(4):
                sp_unit(sp, U_F1 + 4 + q, dn_v[1][0, :, :, q * UW:(q + 1) * UW])
            with sp.Fori(1, CHUNKS) as i:
                sp_ffn(sp, 1, i)
            for n in range(5):
                wait_emptied(sp, jy(n))
                if n < 4:
                    store(sp, o["y_prompt"][0, n * P:(n + 1) * P, :], YO[n][:])
                else:
                    store(sp, o["y_sample"].rearrange("b t d -> (b t) d"), YO[n][0:NS, :])
            sp.wait_ge(out_stored, 16 * stores[0])

        def pe_unit(pe, u, j0, xh, xl, mtiles, ready=None, i=0, ktiles=None):
            pe.wait_ge(whi_made, i * FFN_U + u + 1)
            pe.wait_ge(wlo_made, i * FFN_U + u + 1)
            wh, wl = WHI[u % 2], WLO[u % 2]
            for m, (c0, w) in enumerate(mtiles):
                j = j0 + m
                pe.wait_ge(emptied[(j - 4) % 4], i * (FFN_J // 2) + 2 * ((j - 4) // 4) + 2)
                ks = ktiles[m] if ktiles else [(k, k) for k in range(KT)]
                for n, (kw, kx) in enumerate(ks):
                    if ready is not None:
                        ready(pe, m, kx)
                    for wt, xt in ((wh, xh), (wh, xl), (wl, xh)):
                        for h in range(2):
                            mm = nc.tensor.matmul(bank(j, h)[0:w, 0:TH], wt[:, kw, c0:c0 + w],
                                                  xt[:, kx, h * TH:(h + 1) * TH],
                                                  start=(n == 0 and wt is wh and xt is xh),
                                                  stop=(n == len(ks) - 1 and wt is wl))
                mm.then_inc(filled, 2)

        def pe_transposes(pe, j, items, n=P):
            wait_free(pe, j)
            for out, in_ in items:
                k = in_.shape[0]
                mm = nc.tensor.transpose(out, in_, ident[0:k, 0:k])
            mm.then_inc(filled, 2)

        def pe_norm(pe, n, j):
            wait_free(pe, j)
            sq = DF if n == 3 else SQ
            for i, k in enumerate(ORDER[n]):
                pe.wait_ge(sq_made, KT * n + i + 1)
                for h in range(2):
                    mm = nc.tensor.matmul(bank(j, h)[:, 0:TH], ones, sq[:, k, h * TH:(h + 1) * TH],
                                          start=(i == 0), stop=(i == KT - 1))
            mm.then_inc(filled, 2)

        DIAGONAL = ((0, 0), (1, 1), (1, 0), (0, 1))

        def settle(pe):
            pe.sem_inc(settled, 1)


        def w_square(pe, i, name, L, Rt, needs=()):
            j = jw(i, name)
            for h in range(2):
                w_free(pe, i, name)
                for need in needs:
                    need(h)
                settle(pe)
                for g in range(KT):
                    for c in range(2):
                        rows = slice(c * HD, (c + 1) * HD)
                        rhs = Rt[rows, :] if Rt is CC["I64"] else Rt[rows, h, g, :]
                        mm = nc.tensor.matmul(bank(j, h)[rows, g * HD:(g + 1) * HD], L[rows, h, g, :], rhs,
                                              start=True, stop=True)
                mm.then_inc(filled, 1)

        XT_ = FX[:, :, :, 1, :]
        FT_ = FX[:, :, :, 0, :]

        def pe_lora(pe, i, name, tok):
            wa, hid = {"wpre": (W2A, WH), "apre": (A2A, AH)}[name]
            for h in range(2):
                w_free(pe, i, name)
                for g in range(4):
                    mm = nc.tensor.matmul(bank(jw(i, name), h)[:, g * P:(g + 1) * P],
                                          wa[0:LW + 1, (4 * h + g) * P:(4 * h + g + 1) * P], hid[0:LW + 1, tok],
                                          start=True, stop=True)
                mm.then_inc(filled, 1)

        def pe_headsums(pe, i):
            j = jw(i, "norm2")
            w_free(pe, i, "norm2")
            pe.wait_ge(dve_prep, prep_count(i, DVE_PREP, "KSQ"))
            c0 = CAT["headsum"][0] + 14
            for g in range(KT):
                mm = nc.tensor.matmul(bank(j, 0)[0:NH, 0:P], CT[:, c0 - 2 * g:c0 - 2 * g + NH], WT["KSQ"][:, g, :],
                                      start=(g == 0), stop=(g == KT - 1))
            mm.then_inc(filled, 2)

        def pe_headspread(pe, i):
            j = jw(i, "norm3")
            w_free(pe, i, "norm3")
            pe.wait_ge(dve_prep, prep_count(i, DVE_PREP, "RI"))
            for g in range(KT):
                mm = nc.tensor.matmul(bank(j, g // 4)[:, (g % 4) * P:(g % 4 + 1) * P], HR[:, g, :], NRM[:],
                                      start=True, stop=True)
                if g % 4 == 3:
                    mm.then_inc(filled, 1)

        def pe_tile(pe, i, last=False):
            if not last:
                nxt = bass.ds(i * P + P, P)
            kept = lambda name: (lambda h: w_kept(pe, i, name, h))
            w_prep(pe, i, "RT")
            for q in range(4):
                j = jw(i, f"Q{q}")
                w_free(pe, i, f"Q{q}")
                settle(pe)
                for gg in range(2):
                    for c in range(2):
                        for p in range(2):
                            gc, rows = 2 * (2 * q + gg) + c, slice(p * HD, (p + 1) * HD)
                            cols = slice((2 * gg + c) * P, (2 * gg + c + 1) * P)
                            mm = nc.tensor.matmul(bank(j, p)[:, cols], BKH[rows, gc].rearrange("p x n -> p (x n)"),
                                                  AR[rows, gc].rearrange("p x n -> p (x n)"), start=True, stop=True)
                mm.then_inc(filled, 2)
            j = jw(i, "M")
            w_free(pe, i, "M")
            settle(pe)
            for g in range(KT):
                for p, c in DIAGONAL:
                    rows = slice(p * HD, (p + 1) * HD)
                    mm = nc.tensor.matmul(bank(j, p)[c * HD:(c + 1) * HD, g * HD:(g + 1) * HD],
                                          AR[rows, 2 * g + c, 0, :], BKH[rows, 2 * g + c, 0, :], start=True, stop=True)
            mm.then_inc(filled, 2)
            w_square(pe, i, "P2", WT["P1T"], WT["P1"], [kept("Q3"), kept("M")])
            w_square(pe, i, "P2T", WT["P1"], WT["P1T"])
            for h in range(2):
                w_free(pe, i, "bonus")
                mm = nc.tensor.matmul(bank(jw(i, "bonus"), h), bones,
                                      WT["Z"][:, 4 * h:4 * h + 4, :].rearrange("p a b -> p (a b)"), start=True, stop=True)
                mm.then_inc(filled, 1)
            w_square(pe, i, "XT2", WT["P2"], XT_, [kept("P2"), lambda h: w_sum(pe, i, "XT1" + "ab"[h])])
            w_square(pe, i, "P4", WT["P2T"], WT["P2"], [kept("P2T")])

            def turn_bk(q):
                j = jw(i, f"tb{q}")
                w_free(pe, i, f"tb{q}")
                for c in range(2):
                    for g in range(4):
                        mm = nc.tensor.transpose(bank(j, c)[:, g * P:(g + 1) * P],
                                                 BKD[:, 2 * (4 * q + g) + c].rearrange("p x n -> p (x n)"), ident)
                mm.then_inc(filled, 2)

            def turn_v(q):
                j = jw(i, f"tv{q}")
                w_free(pe, i, f"tv{q}")
                settle(pe)
                for c in range(2):
                    for g in range(4):
                        mm = nc.tensor.matmul(bank(j, c)[HD:P, g * P:(g + 1) * P],
                                              WT["VC"][:, 4 * q + g, c * HD:(c + 1) * HD], ident, start=True, stop=True)
                mm.then_inc(filled, 2)

            turn_bk(0)
            w_square(pe, i, "XT3", WT["P4"], XT_, [kept("P4"), kept("XT2")])
            turn_bk(1)
            w_square(pe, i, "X", XT_, CC["I64"], [kept("XT3")])
            if not last:
                pe_lora(pe, i, "wpre", nxt)
            w_square(pe, i, "F", WT["OT"], WT["X"], [kept("X")])
            if not last:
                pe_lora(pe, i, "apre", nxt)
            w_square(pe, i, "FT", WT["X"], WT["OT"])
            pe.wait_ge(vc_made, i + 1)
            turn_v(0)
            w_square(pe, i, "F2", FT_, WT["F"], [kept("F"), kept("FT")])
            turn_v(1)
            for h in range(2):
                name = "T1" + "ab"[h]
                j = jw(i, name)
                w_free(pe, i, name)
                settle(pe)
                for g in range(KT):
                    for c in range(2):
                        rows = slice(c * HD, (c + 1) * HD)
                        mm = nc.tensor.matmul(bank(j, g // 4)[rows, (g % 4) * P:(g % 4 + 1) * P], WT["F"][rows, h, g, :],
                                              FX[rows, h, g].rearrange("p x n -> p (x n)"), start=True, stop=True)
                    if g % 4 == 3:
                        mm.then_inc(filled, 1)
            if not last:
                pe_headsums(pe, i)
            w_square(pe, i, "T2", WT["F2"], XT_, [kept("F2"), lambda h: w_kept(pe, i, "T1" + "ab"[h], 0)])
            w_square(pe, i, "F4", WT["F2T"], WT["F2"], [lambda h: w_kept(pe, i, "T1" + "ab"[h])])
            j = jw(i, "NV")
            w_free(pe, i, "NV")
            w_kept(pe, i, "tv1")
            settle(pe)
            for g in range(KT):
                for c in range(2):
                    for p in range(2):
                        mm = nc.tensor.matmul(bank(j, p)[c * HD:(c + 1) * HD, g * HD:(g + 1) * HD],
                                              NT[HD:P, p, 2 * g + c, :],
                                              UV[HD:P, c, (2 * g + p) * HD:(2 * g + p + 1) * HD], start=True, stop=True)
            mm.then_inc(filled, 2)
            w_square(pe, i, "T3", WT["F4"], XT_, [kept("F4"), kept("T2")])
            for c in range(2):
                rows = slice(c * HD, (c + 1) * HD)
                j = jw(i, f"AS{c}")
                w_free(pe, i, f"AS{c}")
                if c == 1:
                    w_kept(pe, i, "SY0")
                settle(pe)
                for g in range(KT):
                    for p in range(2):
                        ch = slice(p * HD, (p + 1) * HD)
                        mm = nc.tensor.matmul(bank(j, p)[rows, g * HD:(g + 1) * HD], AR[ch, 2 * g + c, 0, :],
                                              ST[ch, g, :], start=True, stop=True)
                mm.then_inc(filled, 2)
                if c == 0 and not last:
                    pe_headspread(pe, i)
                j = jw(i, f"SY{c}")
                w_free(pe, i, f"SY{c}")
                settle(pe)
                for n in range(NH):
                    g, p = n // 2, n % 2
                    ch = slice(p * HD, (p + 1) * HD)
                    mm = nc.tensor.matmul(bank(j, 0)[ch, g * HD:(g + 1) * HD], ST[ch, g, :], AR[ch, 2 * g + c, 1, :],
                                          start=True, stop=True)
                mm.then_inc(ys_filled, 1)
                j = jw(i, f"U{c}")
                w_free(pe, i, f"U{c}")
                w_kept(pe, i, f"AS{c}")
                w_kept(pe, i, "T3")
                settle(pe)
                for g in range(KT):
                    for p in range(2):
                        mm = nc.tensor.matmul(bank(j, p)[0:HD, g * HD:(g + 1) * HD], FX[rows, p, g, 1, :],
                                              WT["NV"][rows, p, g, :], start=True, stop=True)
                mm.then_inc(filled, 2)
                j = jw(i, f"SY{c}")
                w_kept(pe, i, f"U{c}")
                settle(pe)
                for n in range(NH):
                    g, p = n // 2, n % 2
                    vals = slice(n * HD, (n + 1) * HD)
                    mm = nc.tensor.matmul(bank(j, 1)[p * HD:(p + 1) * HD, g * HD:(g + 1) * HD],
                                          BKT[:, c, vals], UV[:, c, vals], start=True, stop=True)
                mm.then_inc(filled, 2)
            j = jw(i, "YU")
            w_free(pe, i, "YU")
            settle(pe)
            for g in range(KT):
                for c in range(2):
                    for p in range(2):
                        n = 2 * g + p
                        mm = nc.tensor.matmul(bank(j, c)[p * HD:(p + 1) * HD, g * HD:(g + 1) * HD],
                                              UV[:, c, n * HD:(n + 1) * HD], RBK[:, p, 2 * g + c, :], start=True, stop=True)
            mm.then_inc(filled, 2)

        def pe_samples(pe):
            t0 = SEQ
            for name, wa, hid in (("wpre", W2A, WH), ("apre", A2A, AH)):
                wait_free(pe, js(name))
                for g in range(KT):
                    mm = nc.tensor.matmul(bank(js(name), 0)[:, g * NS:(g + 1) * NS], wa[0:LW + 1, g * P:(g + 1) * P],
                                          hid[0:LW + 1, t0:t0 + NS], start=True, stop=True)
                mm.then_inc(filled, 2)

            def pairsum(name, src):
                wait_free(pe, js(name))
                nc.tensor.matmul(bank(js(name), 0)[:, 0:KT * NS], bones, src[:].rearrange("p a b -> p (a b)"),
                                 start=True, stop=True).then_inc(filled, 2)

            def square(name, L, Rt):
                wait_free(pe, js(name))
                for n in range(NH):
                    g, p = n // 2, n % 2
                    mm = nc.tensor.matmul(bank(js(name), p)[0:NS, g * NS:(g + 1) * NS], L[0:NS, p, g, :],
                                          Rt[0:NS, p, g, :], start=True, stop=True)
                mm.then_inc(filled, 2)

            s_dve(pe, "KSQ")
            pairsum("norm2", SM["KSQ"])
            for q in range(4):
                j = js(f"s0t{q}")
                if q == 0:
                    pe.wait_ge(s0_loaded, 16 * NB)
                pe_transposes(pe, j, [(bank(j, bb)[:, g * HD:(g + 1) * HD],
                                       S0L[:, 2 * q + bb, 2 * g:2 * g + 2, :].rearrange("v h k -> v (h k)"))
                                      for bb in range(2) for g in range(KT)])
            s_dve(pe, "RT")
            j = js("Q")
            wait_free(pe, j)
            for n in range(NH):
                g, p = n // 2, n % 2
                ch = slice(p * HD, (p + 1) * HD)
                mm = nc.tensor.matmul(bank(j, p)[0:2 * NS, g * 2 * NS:(g + 1) * 2 * NS],
                                      SM["BKH"][ch, g].rearrange("p x n -> p (x n)"),
                                      SM["AR"][ch, g].rearrange("p x n -> p (x n)"), start=True, stop=True)
            mm.then_inc(filled, 2)
            j = js("M")
            wait_free(pe, j)
            for n in range(NH):
                g, p = n // 2, n % 2
                ch = slice(p * HD, (p + 1) * HD)
                mm = nc.tensor.matmul(bank(j, p)[0:NS, g * NS:(g + 1) * NS], SM["AT"][ch, g, :], SM["BH"][ch, g, :],
                                      start=True, stop=True)
            mm.then_inc(filled, 2)
            wait_emptied(pe, js("Q"))
            wait_emptied(pe, js("M"))
            square("P2", SM["P1T"], SM["P1"])
            s_dve(pe, "KD")
            j = js("tBK")
            pe_transposes(pe, j, [(bank(j, g // 4)[0:2 * NS, (g % 4) * P:(g % 4 + 1) * P],
                                   SM["BKD"][:, g].rearrange("p x n -> p (x n)")) for g in range(KT)])
            wait_emptied(pe, js("P2"))
            s_dve(pe, "XT1")
            square("XT2", SM["P2"], SM["XT"])
            j = js("tV")
            wait_free(pe, j)
            for g in range(KT):
                mm = nc.tensor.matmul(bank(j, g // 4)[NS:2 * NS, (g % 4) * P:(g % 4 + 1) * P], V[:, g, SEQ:T], ident,
                                      start=True, stop=True)
            mm.then_inc(filled, 2)
            s_dve(pe, "ZR")
            pairsum("bonus", SM["Z"])
            j = js("GY")
            wait_free(pe, j)
            wait_emptied(pe, js("tV"))
            wait_emptied(pe, js("s0t3"))
            for n in range(NH):
                g, p = n // 2, n % 2
                mm = nc.tensor.matmul(bank(j, 1)[p * HD:(p + 1) * HD, g * NS:(g + 1) * NS],
                                      SM["UV"][NS:2 * NS, n * HD:(n + 1) * HD], SM["NT"][NS:2 * NS, p, g, :],
                                      start=True, stop=True)
            for g in range(KT):
                for b in range(NB):
                    for p in range(2):
                        ch = slice(p * HD, (p + 1) * HD)
                        out = bank(j, 0)[ch].rearrange("p (x a n) -> p x a n", x=2, a=KT)
                        mm = nc.tensor.matmul(out[:, :, g, b * DS:(b + 1) * DS], S0T[ch, b, g, :],
                                              SM["AR"][ch, g, :, b * DS:(b + 1) * DS], start=True, stop=True)
            mm.then_inc(filled, 2)
            wait_emptied(pe, j)
            j = js("tG")
            pe_transposes(pe, j, [(bank(j, g // 4)[0:NS, (g % 4) * P:(g % 4 + 1) * P], SM["GT"][:, g, :])
                                  for g in range(KT)])
            j = js("U")
            wait_free(pe, j)
            wait_emptied(pe, js("tG"))
            wait_emptied(pe, js("XT2"))
            for n in range(NH):
                g, p = n // 2, n % 2
                mm = nc.tensor.matmul(bank(j, p)[0:NS, g * HD:(g + 1) * HD], SM["XT"][0:NS, p, g, :],
                                      SM["G"][:, n * HD:(n + 1) * HD], start=True, stop=True)
            mm.then_inc(filled, 2)
            j = js("YU")
            wait_free(pe, j)
            wait_emptied(pe, js("U"))
            for n in range(NH):
                g, p = n // 2, n % 2
                mm = nc.tensor.matmul(bank(j, 0)[p * HD:(p + 1) * HD, g * NS:(g + 1) * NS],
                                      SM["UV"][:, n * HD:(n + 1) * HD], SM["RBK"][:, p, g, :], start=True, stop=True)
            mm.then_inc(filled, 2)

            def sums(q):
                j = js(f"SS{q}")
                wait_free(pe, j)
                s_act(pe, f"UM{q}")
                for n in range(NH):
                    g, p = n // 2, n % 2
                    vals = slice(n * HD, (n + 1) * HD)
                    mm = nc.tensor.matmul(bank(j, g // 4)[p * HD:(p + 1) * HD, (g % 4) * P:(g % 4 + 1) * P],
                                          SM["BKT"][:, vals], UVM[q % 2][:, :, vals], start=True, stop=True)
                mm.then_inc(filled, 2)

            def out_rows(b):
                j = js(f"TO{b}")
                wait_emptied(pe, js(f"SS{b // 2}"))
                pe_transposes(pe, j, [(bank(j, g // 4)[0:HD, (g % 4) * P:(g % 4 + 1) * P], S0T[:, b, g, :])
                                      for g in range(KT)])

            for q in range(4):
                sums(q)
                if q:
                    out_rows(2 * q - 2)
                    out_rows(2 * q - 1)
            out_rows(NB - 2)
            out_rows(NB - 1)

        def pe_ffn(pe, l, i):
            u0, j0 = ((U_F0, J_F0), (U_F1, J_F1))[l]
            nn = (1, 3)[l]
            first = lambda pe, m, k: pe.wait_ge(xlo_made, xlo_at(nn, k))
            for q in range(4):
                pe_unit(pe, u0 + q, j0 + 2 * q, XSH[0], XSL[0], ((0, P), (P, P)), first if q == 0 else None, i,
                        [[(k, k) for k in ORDER[nn]]] * 2)
            hid = lambda pe, m, k: pe.wait_ge(hlo_made, i * KT + (KT * CHUNKS * l + k + 1))
            for q in range(4):
                pe_unit(pe, u0 + 4 + q, j0 + 8 + 2 * q, HH, HL, ((0, P), (P, P)), hid if q == 0 else None, i)

        def xlo_at(n, k):
            return 48 + KT * {1: 0, 3: 1}[n] + ORDER[n].index(k) + 1

        def run_pe(pe):
            pe.wait_ge(const_loaded, 16)
            for n in range(5):
                pe.wait_ge(x_loaded, 80)
                j, w = J_X + n, P if n < 4 else NS
                pe_transposes(pe, j, [(bank(j, k // 4)[:, (k % 4) * w:(k % 4 + 1) * w], XIN[0:w, n, k * P:(k + 1) * P])
                                      for k in range(KT)])
            pe.wait_ge(prm_loaded, 16 * 11)
            pe_transposes(pe, J_PRM, [(bank(J_PRM, 0)[:, 0:P], PR[:]), (bank(J_PRM, 1)[:, 0:72], PR2[:])])
            pe_norm(pe, 0, J_N0)
            for jx, (u, j, mt) in enumerate(((U_W1, J_W1, ((0, LW),)), (U_A1, J_A1, ((0, LA),)),
                                             (U_G1, J_G1, ((0, P), (P, LG - P))))):
                ready = lambda pe, m, k, jx=jx: pe.wait_ge(xlo_made, KT * jx + k + 1)
                pe_unit(pe, u, j, XSH[jx % 2], XSL[jx % 2], mt, ready)
            for n in range(12):
                jx = 3 + n // 4
                ready = lambda pe, m, k, jx=jx: pe.wait_ge(xlo_made, KT * jx + k + 1)
                pe_unit(pe, U_RKV + n, J_R + 2 * n if n < 8 else jv(f"V{2 * n - 16}"), XSH[jx % 2], XSL[jx % 2],
                        ((0, P), (P, P)), ready if n % 4 == 0 else None)
                if n == 9:
                    pe.wait_ge(aug_loaded, 64)
                    pe.wait_ge(pads_made, 6)
                    for name in ("wpre", "apre"):
                        pe_lora(pe, None, name, slice(0, P))
                    pe_headsums(pe, None)
                if n == 10:
                    pe.wait_ge(headrow_loaded, 16)
                    pe_headspread(pe, None)
            pe.wait_ge(sht_made, 1)
            pe_transposes(pe, J_SHO, [(bank(J_SHO, k // 4)[0:9, (k % 4) * P:(k % 4 + 1) * P], SHT[:, k, :])
                                      for k in range(KT)])
            pe.wait_ge(gsig_made, 2)
            with pe.Fori(0, TILES - 1) as i:
                pe_tile(pe, i)
            pe_tile(pe, TILES - 1, last=True)
            wait_emptied(pe, J_STO - 2)
            pe_transposes(pe, J_STO, [(bank(J_STO, g // 4)[0:HD, (g % 4) * P:(g % 4 + 1) * P], ST[:, g, :])
                                      for g in range(KT)])
            pe_samples(pe)
            c0 = CAT["headsum"][0] + 14
            for what, k in GN_JOBS:
                j = jg(what, k)
                wait_free(pe, j)
                if what == "var":
                    for kk in range(KT):
                        pe.wait_ge(gn_squared, kk + 1)
                        for h in range(2):
                            mm = nc.tensor.matmul(bank(j, h)[0:NH, 0:TH], CT[:, c0 - 2 * kk:c0 - 2 * kk + NH],
                                                  GQ[:, kk, h * TH:(h + 1) * TH], start=(kk == 0), stop=(kk == KT - 1))
                    mm.then_inc(filled, 2)
                    continue
                if (what, k) == ("gate", 0):
                    pe.wait_ge(g2_loaded, 32)
                if what == "spread":
                    pe.wait_ge(gn_rstd, 1)
                for h in range(2):
                    cols = slice(h * TH, (h + 1) * TH)
                    out = bank(j, h)[:, 0:TH]
                    if what == "mean":
                        mm = nc.tensor.matmul(out, bmean, R[:, k, cols], start=True, stop=True)
                    elif what == "spread":
                        mm = nc.tensor.matmul(out, HR[:, k, :], GR[:, cols], start=True, stop=True)
                    else:
                        nc.tensor.matmul(out, G2A[:, k * P:(k + 1) * P], GH[:, 0, cols], start=True, stop=False)
                        mm = nc.tensor.matmul(out, G2B[:, k * P:(k + 1) * P], GH[0:LG - P, 1, cols],
                                              start=False, stop=True)
                mm.then_inc(filled, 2)
            ready = lambda pe, m, k: pe.wait_ge(gn_lo, k + 1)
            for n in range(4):
                pe_unit(pe, U_WO + n, J_WO + 2 * n, XSH[1], XSL[1], ((0, P), (P, P)), ready if n == 0 else None)
            pe_norm(pe, 1, J_N1)
            with pe.Fori(0, CHUNKS) as i:
                pe_ffn(pe, 0, i)
            pe_norm(pe, 2, J_N2)
            pe.wait_ge(pst_loaded, 16)
            pe_transposes(pe, J_PST, [(bank(J_PST, k // 4)[:, (k % 4) * 120:(k % 4 + 1) * 120],
                                       PSI[0:120, k * P:(k + 1) * P]) for k in range(KT)])
            ready = lambda pe, m, k: pe.wait_ge(pool_lo, POOL_ORDER.index(k) + 1)

            def pool_products(first, n):
                pe_unit(pe, U_POOL, jpw(POOL_ORDER[first]), XSH[0], XSL[0], [(P * (m % 2), P) for m in range(n)], ready,
                        ktiles=[[(2 * g, 2 * g), (2 * g + 1, 2 * g + 1)] for g in GROUP_ORDER for _ in range(2)][first:])

            pool_products(0, 6)
            pe.wait_ge(hn_made, 2 * KT)
            pe_transposes(pe, J_PO, [(bank(J_PO, k // 4)[0:PBUF, (k % 4) * P:(k % 4 + 1) * P],
                                      EXT[:, k, SEQ:SEQ + PBUF]) for k in range(KT)])
            pe.wait_ge(pool_cols, KT)
            pe_transposes(pe, J_PO + 1, [(bank(J_PO + 1, k // 4)[0:120, (k % 4) * P:(k % 4 + 1) * P],
                                          PCO[:, k].rearrange("p b t -> p (b t)")) for k in range(KT)])
            pool_products(6, 2)
            pe_norm(pe, 3, J_N3)
            with pe.Fori(0, CHUNKS) as i:
                pe_ffn(pe, 1, i)
            pe_norm(pe, 4, J_N4)
            pe.wait_ge(xhi_made, 48 + 3 * KT)
            for n in range(5):
                j, w = jy(n), P if n < 4 else NS
                pe_transposes(pe, j, [(bank(j, k // 4)[0:w, (k % 4) * P:(k % 4 + 1) * P], HN[:, k, n * P:n * P + w])
                                      for k in range(KT)])
                if n == 0:
                    wait_emptied(pe, J_N4)
                    wait_free(pe, J_YT)
                    for i in range(5):
                        w = P if i < 4 else NS
                        mm = nc.tensor.matmul(bank(J_YT, 0)[0:w, i:i + 1], RS1[0:1, i * P:i * P + w], ones[0:1, 0:1],
                                              start=True, stop=True)
                    mm.then_inc(filled, 2)

        def timeline():
            steps = [("split", 0)] + [("xs", n) for n in range(8)]
            for u, js_ in ((0, (J_W1,)), (1, (J_A1,)), (2, (J_G1, J_G1 + 1))):
                steps += [("split", u + 1)] + [("xs", 8 * (u + 1) + n) for n in range(8)] + [("out", j) for j in js_]
            for n in range(12):
                if n < 11:
                    steps += [("split", U_RKV + n + 1)]
                if n < 4:
                    steps += [("xs", 32 + 2 * n), ("xs", 33 + 2 * n)]
                elif n < 6:
                    steps += [("xs", 24 + 4 * n + m) for m in range(4)]
                if n == 5:
                    steps += [("out", J_K), ("out", J_K + 1)]
                if n == 10:
                    steps += [("first", "exps"), ("first", "root")]
                if n >= 8:
                    steps += [("out", jv(f"V{2 * n - 16}")), ("out", jv(f"V{2 * n - 15}"))]
                elif n != 4:
                    steps += [("out", J_R + 2 * n), ("out", J_R + 2 * n + 1)]
                if n in (8, 9):
                    steps += [("first", ("squares", "lora")[n - 8])]
            return steps

        def wait_split(eng, u, i=0):
            eng.wait_ge(raw_loaded[u % 2], i * (16 * FFN_U // 2) + 16 * (u // 2 + 1))
            if u >= 2:
                j = {U_F0 + 1: J_F0 - 1, U_F1 + 1: J_F1 - 1}.get(u, last_job(u - 2))
                eng.wait_ge(filled, i * (2 * FFN_J) + 2 * j + 2)

        act = nc.scalar.activation

        def act_split(eng, u, i=0):
            wait_split(eng, u, i)
            w = unit_width(u)
            act(WHI[u % 2][:, :, 0:w], RAW[u % 2][:, :, 0:w], ACT.Copy).then_inc(whi_made, 1)

        def act_norm(eng, n, j, ready):
            for k in range(KT):
                ready(k)
                act(SQ[:, k, :], X[:, k, :], ACT.Square).then_inc(sq_made, 1)
            wait_filled(eng, j)
            rs = RS1 if n else RS0
            act(halves(rs[:]), both(j, TH), ACT.Sqrt, bias=CC["eps"][:, 0:1], scale=1.0 / D).then_inc(emptied[j % 4], 2)

        def act_copy_out(eng, j, dst, src, func=ACT.Copy, scale=1.0):
            wait_filled(eng, j)
            act(dst, src, func, scale=scale).then_inc(emptied[j % 4], 2)

        def act_lora(eng, i, name):
            j = jw(i, name)
            dst = WT[{"wpre": "TW", "apre": "TA"}[name]]
            for h in range(2):
                w_filled(eng, i, name, h)
                act(dst[:, 4 * h:4 * h + 4, :].rearrange("p a b -> p (a b)"), bank(j, h), ACT.Tanh, scale=0.5)\
                    .then_inc(emptied[j % 4], 1)

        def act_exps(eng, i):
            eng.wait_ge(dve_prep, prep_count(i, DVE_PREP, "CS"))
            act(WT["EL"][:], WT["CS"][:], ACT.Exp, scale=-DECAY).then_inc(act_prep, 1)
            eng.wait_ge(dve_prep, prep_count(i, DVE_PREP, "CX"))
            act(WT["EN"][:], WT["CS"][:], ACT.Exp, scale=DECAY).then_inc(act_prep, 1)

        def act_exp_before(eng):
            act(WT["EX"][:], WT["CX"][:], ACT.Exp, scale=-DECAY).then_inc(act_prep, 1)

        def act_root_heads(eng, i):
            w_kept(eng, i, "norm2")
            act(NRM[:], NRM[:], ACT.Sqrt).then_inc(act_prep, 1)

        def act_tile(eng, i, last=False):
            tok0 = i * P
            act(WT["VC"][:], V[:, :, bass.ds(tok0, P)], ACT.Copy).then_inc(vc_made, 1)

            def mats(name, T4=None):
                T4 = WT[name][:] if T4 is None else T4
                j = jw(i, name)
                for h in range(2):
                    w_filled(eng, i, name, h)
                    act(T4[:, h], bank(j, h).rearrange("p (a b) -> p a b", a=KT), ACT.Copy).then_inc(emptied[j % 4], 1)

            def turned(name, dst, rows=slice(0, P)):
                j = jw(i, name)
                w_filled(eng, i, name)
                act(dst, both(j)[rows], ACT.Copy).then_inc(emptied[j % 4], 2)

            mats("P2")
            mats("P2T")
            mats("P4")
            turned("tb0", BKT[:, :, 0:512])
            turned("tb1", BKT[:, :, 512:1024])
            mats("X")
            if not last:
                act_lora(eng, i, "wpre")
            mats("F")
            if not last:
                act_lora(eng, i, "apre")
            mats("FT", FT_)
            if not last:
                act_exps(eng, i)
                act_exp_before(eng)
            turned("tv0", UV[HD:P, :, 0:512], slice(HD, P))
            mats("F2")
            turned("tv1", UV[HD:P, :, 512:1024], slice(HD, P))
            for h in range(2):
                j = jw(i, "T1" + "ab"[h])
                w_kept(eng, i, "T1" + "ab"[h], 0)
                act(WT["F2T"][:, h].rearrange("p (b a) n -> p b a n", b=2),
                    both(j).rearrange("p b (a x) -> p b a x", a=4)[:, :, :, 0:HD], ACT.Copy).then_inc(emptied[j % 4], 1)
            mats("F4")
            mats("NV")
            if not last:
                act_root_heads(eng, i)
            for c in range(2):
                eng.wait_ge(ys_filled, 2 * i + c + 1)
                act(R[:, :, bass.ds(tok0 + c * HD, HD)],
                    bank(jw(i, f"SY{c}"), 0).rearrange("p (a b) -> p a b", a=KT), ACT.Copy)\
                    .then_inc(emptied[jw(i, f"SY{c}") % 4], 1)
                j = jw(i, f"U{c}")
                w_filled(eng, i, f"U{c}")
                act(UV[0:HD, c].rearrange("s (g p v) -> s p g v", g=KT, p=2),
                    both(j)[0:HD].rearrange("s p (g v) -> s p g v", g=KT), ACT.Copy).then_inc(emptied[j % 4], 2)

        def act_samples(eng):
            s8 = lambda j: bank(j, 0)[:, 0:KT * NS].rearrange("p (a b) -> p a b", a=KT)
            act_copy_out(eng, js("wpre"), SM["TW"][:], s8(js("wpre")), ACT.Tanh, 0.5)
            act_copy_out(eng, js("apre"), SM["TA"][:], s8(js("apre")), ACT.Tanh, 0.5)
            wait_emptied(eng, js("norm2"))
            act(SM["NR"][:], SM["NR"][:], ACT.Sqrt).then_inc(smp_act, 1)
            s_dve(eng, "CS")
            act(SM["EL"][:], SM["CS"][:], ACT.Exp, scale=-DECAY).then_inc(smp_act, 1)
            act(SM["EN"][:], SM["CS"][:], ACT.Exp, scale=DECAY).then_inc(smp_act, 1)
            s_dve(eng, "CX")
            act(SM["EX"][:], SM["CX"][:], ACT.Exp, scale=-DECAY).then_inc(smp_act, 1)
            for q in range(4):
                if q == 0:
                    s_dve(eng, "KP")
                act_copy_out(eng, js(f"s0t{q}"), S0T[:, 2 * q:2 * q + 2].rearrange("p b g v -> p b (g v)"), both(js(f"s0t{q}")))
            rows2 = lambda T2: T2.rearrange("p (e n) -> p e n", e=2)
            j = js("P2")
            act_copy_out(eng, j, SM["P2"][0:NS].rearrange("p e a b -> p e (a b)"), both(j, KT * NS)[0:NS])
            act_copy_out(eng, js("tBK"), rows2(SM["BKT"][:]), both(js("tBK"))[0:2 * NS])
            act_copy_out(eng, js("tV"), rows2(SM["UV"][NS:2 * NS]), both(js("tV"))[NS:2 * NS])
            j = js("GY")
            wait_filled(eng, j)
            act(SM["GT"][:], bank(j, 1)[:, 0:KT * NS].rearrange("p (a b) -> p a b", a=KT), ACT.Copy).then_inc(emptied[j % 4], 1)
            act_copy_out(eng, js("tG"), rows2(SM["G"][:]), both(js("tG"))[0:NS])
            j = js("U")
            act_copy_out(eng, j, SM["UV"][0:NS].rearrange("s (g p v) -> s p g v", g=KT, p=2),
                         both(j)[0:NS].rearrange("s p (g v) -> s p g v", g=KT))

            def masked_uv(q):
                if q == 0:
                    wait_emptied(eng, js("U"))
                if q >= 2:
                    wait_filled(eng, js(f"SS{q - 2}"))
                for bb in range(2):
                    ins = act(UVM[q % 2][:, bb, :], SM["UV"][:], ACT.Copy, scale=CC["SB"][0:2 * NS, 2 * q + bb:2 * q + bb + 1])
                ins.then_inc(smp_act, 1)

            masked_uv(0)
            masked_uv(1)
            for q in range(4):
                for b in (2 * q, 2 * q + 1):
                    act_copy_out(eng, js(f"TO{b}"), rows2(SO[:, b]), both(js(f"TO{b}"))[0:HD])
                if q < 2:
                    masked_uv(q + 2)

        def act_ffn(eng, l, i, last):
            u0, j0 = ((U_F0, J_F0), (U_F1, J_F1))[l]
            h0 = KT * CHUNKS * l
            for q in range(8):
                if not (last and q == 7):
                    act_split(eng, u0 + q + 1, i)
                for m in (2 * q, 2 * q + 1):
                    if q < 4:
                        j = j0 + m
                        eng.wait_ge(emptied[j % 4], i * (FFN_J // 2) + 2 * (j // 4) + 2)
                        if m >= 2:
                            eng.wait_ge(hlo_made, i * KT + (h0 + m - 1))
                        act(QL[:, m % 2, :], RL[:, m % 2, :], ACT.Square).then_inc(square_made, 1)
                        if m >= 1:
                            act_hidden_hi(eng, i, h0, m - 1)
                if q == 3:
                    act_hidden_hi(eng, i, h0, 7)

        def act_hidden_hi(eng, i, h0, m):
            eng.wait_ge(square_made, i * KT + (h0 + m + 1))
            act(HH[:, m, :], QL[:, m % 2, :], ACT.Copy).then_inc(hhi_made, 1)

        def run_act(eng):
            eng.wait_ge(const_loaded, 16)
            for n in range(5):
                j = J_X + n
                w = P if n < 4 else NS
                wait_filled(eng, j)
                for h in range(2):
                    act(X[:, 4 * h:4 * h + 4, n * P:n * P + w], bank(j, h)[:, 0:4 * w].rearrange("p (a b) -> p a b", a=4),
                        ACT.Copy).then_inc(emptied[j % 4], 1)
            wait_filled(eng, J_PRM)
            act(PRM[:], bank(J_PRM, 0)[:, 0:P], ACT.Copy).then_inc(emptied[J_PRM % 4], 1)
            act(PRM2[:], bank(J_PRM, 1)[:, 0:72], ACT.Copy).then_inc(emptied[J_PRM % 4], 1)
            act_norm(eng, 0, J_N0, lambda k: wait_emptied(eng, J_X + 3) if k else wait_emptied(eng, J_X + 4))
            def shifted_hi(n):
                jx, k = n // 8, n % 8
                if k == 0 and jx >= 2:
                    wait_filled(eng, (J_W1, J_A1, J_G1 + 1, J_R + 7)[jx - 2])
                eng.wait_ge(xf_made, n + 1)
                act(XSH[jx % 2][:, k, :], XF[:, n % 2, :], ACT.Copy).then_inc(xhi_made, 1)

            for what, n in timeline():
                if what == "split":
                    act_split(eng, n)
                elif what == "xs":
                    shifted_hi(n)
                elif what == "first":
                    if n == "lora":
                        act_lora(eng, None, "wpre")
                        act_lora(eng, None, "apre")
                    elif n == "exps":
                        act_exps(eng, None)
                    elif n == "root":
                        act_root_heads(eng, None)
                elif n == J_W1:
                    act_copy_out(eng, n, halves(WH[0:LW, :]), both(n, TH)[0:LW], ACT.Tanh)
                elif n == J_A1:
                    act_copy_out(eng, n, halves(AH[0:LA, :]), both(n, TH)[0:LA])
                elif n == J_G1:
                    act_copy_out(eng, n, halves(GH[:, 0, :]), both(n, TH), ACT.Tanh, 0.5)
                elif n == J_G1 + 1:
                    act_copy_out(eng, n, halves(GH[0:LG - P, 1, :]), both(n, TH)[0:LG - P], ACT.Tanh, 0.5)
                else:
                    m = n - J_R if n < J_V else 16 + int(V_SEQ[n - J_V][1])
                    if m == 8:
                        eng.wait_ge(xf_made, 48)
                    if m == 16:
                        eng.wait_ge(sht_made, 1)
                    act_copy_out(eng, n, halves((R, K, V)[m // 8][:, m % 8, :]), both(n, TH))
            act_exp_before(eng)
            act_copy_out(eng, J_SHO, SHO[:].rearrange("p (e n) -> p e n", e=2), both(J_SHO)[0:9])
            eng.wait_ge(out_stored, 32)
            with eng.Fori(0, TILES - 1) as i:
                act_tile(eng, i)
            act_tile(eng, TILES - 1, last=True)
            act_copy_out(eng, J_STO, STO[:].rearrange("p (e n) -> p e n", e=2), both(J_STO)[0:HD])
            act_samples(eng)
            for k in range(KT):
                wait_emptied(eng, jg("mean", k))
                act(GQ[:, k, :], R[:, k, :], ACT.Square).then_inc(gn_squared, 1)
            for k in range(4):
                act_copy_out(eng, jg("gate", k), halves(GG[:, k, :]), both(jg("gate", k), TH))
            j = jg("var", 0)
            wait_filled(eng, j)
            act(halves(GR[:]), both(j, TH)[0:NH], ACT.Sqrt, bias=CC["eps"][0:NH, 1:2], scale=1.0 / HD)\
                .then_inc(emptied[j % 4], 2)
            for k in range(4, KT):
                act_copy_out(eng, jg("gate", k), halves(GG[:, k, :]), both(jg("gate", k), TH))
            act_split(eng, U_WO)
            for k in range(KT):
                eng.wait_ge(gn_gated, k + 1)
                act(XSH[1][:, k, :], R[:, k, :], ACT.Copy).then_inc(gn_hi, 1)
            for n in range(4):
                act_split(eng, U_WO + n + 1)
                for k in (2 * n - 2, 2 * n - 1) if n else ():
                    act_gained(eng, k, NFFN, lambda k: wait_emptied(eng, J_WO + k))
            for k in (6, 7):
                act_gained(eng, k, NFFN, lambda k: wait_emptied(eng, J_WO + k))
            act_root(eng, J_N1)
            with eng.Fori(0, CHUNKS - 1) as i:
                act_ffn(eng, 0, i, False)
            act_ffn(eng, 0, CHUNKS - 1, False)
            act_norm(eng, 2, J_N2, lambda k: wait_emptied(eng, J_N2 - KT + k))
            wait_filled(eng, J_PST)
            for k in range(KT):
                ins = act(samples(EXT[:, k, S0_:], 0, PBUF),
                          bank(J_PST, k // 4)[:, (k % 4) * 120:(k % 4 + 1) * 120].rearrange("p (b t) -> p b t", b=NB),
                          ACT.Copy)
                if k % 4 == 3:
                    ins.then_inc(emptied[J_PST % 4], 1)
            wait_emptied(eng, J_PST)
            for i, k in enumerate(POOL_ORDER):
                eng.wait_ge(hn_made, KT + i + 1)
                act(PCO[:, k], samples(EXT[:, k, S0_:], DS, PBUF), ACT.Copy).then_inc(pool_cols, 1)
                if i % 2:
                    pool_lead(eng, i - 1)
                    pool_lead(eng, i)

            def summed(k):
                wait_emptied(eng, jpw(k))
                wait_filled(eng, jpw(k | 1))

            act_split(eng, U_F1)
            for k in POOL_ORDER[0:4]:
                act_gained(eng, k, NFFN + 8, summed, DF)
            act_copy_out(eng, J_PO, PRO[0][0:PBUF, :].rearrange("p (e n) -> p e n", e=2), both(J_PO)[0:PBUF])
            act_copy_out(eng, J_PO + 1, PRO[1][0:120, :].rearrange("p (e n) -> p e n", e=2), both(J_PO + 1)[0:120])
            for k in POOL_ORDER[4:]:
                act_gained(eng, k, NFFN + 8, summed, DF)
            act_root(eng, J_N3)
            with eng.Fori(0, CHUNKS - 1) as i:
                act_ffn(eng, 1, i, False)
            act_ffn(eng, 1, CHUNKS - 1, True)
            for k in range(KT):
                wait_emptied(eng, J_N4 - KT + k)
                act(SQ[:, k, :], X[:, k, :], ACT.Square).then_inc(sq_made, 1)
                act(HN[:, k, :], X[:, k, :], ACT.Copy, scale=col(NFIN + k)).then_inc(xhi_made, 1)
            act_root(eng, J_N4)
            wait_emptied(eng, J_YT)
            for n in range(5):
                w = P if n < 4 else NS
                act_copy_out(eng, jy(n), YO[n][0:w, :].rearrange("p (e n) -> p e n", e=2), both(jy(n))[0:w], ACT.Copy,
                             YR[0:w, n:n + 1])


        def pool_lead(eng, i):
            k = POOL_ORDER[i]
            eng.wait_ge(pool_diff, i + 1)
            act(XSH[0][:, k, :], DF[:, k, :], ACT.Copy).then_inc(pool_hi, 1)

        def act_gained(eng, k, gcol, ready, sq=SQ):
            ready(k)
            act(sq[:, k, :], X[:, k, :], ACT.Square).then_inc(sq_made, 1)
            act(XSH[0][:, k, :], X[:, k, :], ACT.Copy, scale=col(gcol + k)).then_inc(xhi_made, 1)

        def act_root(eng, j):
            wait_filled(eng, j)
            act(halves(RS1[:]), both(j, TH), ACT.Sqrt, bias=CC["eps"][:, 0:1], scale=1.0 / D).then_inc(emptied[j % 4], 2)

        tt, ts, stt = nc.vector.tensor_tensor, nc.vector.tensor_scalar, nc.vector.scalar_tensor_tensor

        def dve_split(eng, u, i=0):
            eng.wait_ge(raw_loaded[u % 2], i * (16 * FFN_U // 2) + 16 * (u // 2 + 1))
            eng.wait_ge(whi_made, i * FFN_U + u + 1)
            w = unit_width(u)
            b = u % 2
            tt(WLO[b][:, :, 0:w], RAW[b][:, :, 0:w], WHI[b][:, :, 0:w].bitcast(F32), SUB).then_inc(wlo_made, 1)

        samples = lambda ap, lo, n: ap.rearrange("p (b t) -> p b t", b=NB)[:, :, lo:lo + n]

        def dve_gained_lo(eng, n, k, gcol):
            eng.wait_ge(xhi_made, xlo_at(n, k))
            stt(XSL[0][:, k, :], X[:, k, :], col(gcol + k), XSH[0][:, k, :].bitcast(F32), MUL, SUB).then_inc(xlo_made, 1)

        def dve_rstd(eng, n, j):
            wait_emptied(eng, j)
            nc.vector.reciprocal(RS1[:], RS1[:]).then_inc(rstd_made, 1)
            eng.wait_ge(rstd_made, n + 1)

        def dve_features(eng, A, n_tok, tok, rst, need, act_need, feature, wait_w, wait_a, norm2):
            bc = lambda c0: spread(PRM[:, c0:c0 + KT], n_tok)
            f = lambda ins: ins.then_inc(feature, 1)
            r_, k_ = R[:, :, tok], K[:, :, tok]
            f(tt(A["KQ"][:], k_, bc(KK_), MUL))
            need("KQ")
            f(tt(A["KSQ"][:], A["KQ"][:], A["KQ"][:], MUL))
            wait_w()
            f(ts(A["SG"][:], A["TW"][:], 0.5, 0.5, MUL, ADD))
            need("SG")
            f(nc.vector.tensor_tensor_scan(flat2(A["CS"]), rst, flat2(A["SG"]), 0.0, MUL, ADD))
            need("CS")
            f(tt(A["CX"][:], A["CS"][:], A["SG"][:], SUB))
            norm2()
            act_need("NR")
            f(nc.vector.reciprocal(A["NR"][:], A["NR"][:]))
            need("RI")
            f(tt(A["KK"][:], A["KQ"][:], A["NR"][:], MUL))
            need("KK")
            act_need("EX")
            f(stt(A["AT"][:], A["KK"][:], -1.0, A["EX"][:], MUL, MUL))
            wait_a()
            f(ts(A["AG"][:], A["TA"][:], 0.5, 0.5, MUL, ADD))
            need("AG")
            f(tt(A["BB"][:], A["KK"][:], A["AG"][:], MUL))
            need("BB")
            f(tt(A["BH"][:], A["BB"][:], A["EN"][:], MUL))
            f(ts(A["T1"][:], A["TA"][:], 0.5, 0.5, MUL, SUB))
            need("T1")
            f(tt(A["T1"][:], A["T1"][:], bc(KA_), MUL))
            need("T2")
            f(stt(A["KP"][:], A["T1"][:], 1.0, k_, ADD, MUL))
            need("KP")
            f(tt(A["KH"][:], A["KP"][:], A["EN"][:], MUL))
            f(tt(A["RT"][:], r_, A["EL"][:], MUL))

        def flat2(T3):
            return T3[:].rearrange("p a b -> p (a b)")

        def dve_features2(eng, A, n_tok, tok, chunk, need, feature):
            f = lambda ins: ins.then_inc(feature, 1)
            n = n_tok // chunk
            end = A["EL"][:].rearrange("p g (c t) -> p g c t", t=chunk)[:, :, :, chunk - 1:chunk]\
                .to_broadcast([P, KT, n, chunk])
            v4 = lambda T3: T3[:].rearrange("p g (c t) -> p g c t", t=chunk)
            f(tt(v4(A["BD"]), v4(A["BH"]), end, MUL))
            f(tt(v4(A["KD"]), v4(A["KH"]), end, MUL))
            f(tt(A["Z"][:], R[:, :, tok], A["KP"][:], MUL))
            need("Z")
            f(tt(A["Z"][:], A["Z"][:], spread(PRM[:, RK_:RK_ + KT], n_tok), MUL))

        def prep_steps(eng, i):
            tok0 = 0 if i is None else i * P + P
            tok = bass.ds(tok0, P)
            A = WT
            bc = lambda c0: spread(PRM[:, c0:c0 + KT], P)
            f = lambda ins: ins.then_inc(dve_prep, 1)
            need = lambda name: eng.wait_ge(dve_prep, prep_count(i, DVE_PREP, name))
            made = lambda name: eng.wait_ge(act_prep, prep_count(i, ACT_PREP, name))
            gc = lambda T3: T3[:].rearrange("p g (c t) -> p (g c) t", c=2)

            def KQ():
                f(tt(A["KQ"][:], K[:, :, tok], bc(KK_), MUL))

            def KSQ():
                need("KQ")
                f(tt(A["KSQ"][:], A["KQ"][:], A["KQ"][:], MUL))

            def SG():
                w_kept(eng, i, "wpre")
                f(ts(A["SG"][:], A["TW"][:], 0.5, 0.5, MUL, ADD))

            def CS():
                need("SG")
                f(nc.vector.tensor_tensor_scan(flat2(A["CS"]), RST[:, 0:KT * P], flat2(A["SG"]), 0.0, MUL, ADD))

            def CX():
                need("CS")
                f(tt(A["CX"][:], A["CS"][:], A["SG"][:], SUB))

            def T1():
                w_kept(eng, i, "apre")
                f(stt(A["T1"][:], A["TA"][:], -1.0, spread(HKA[:], P), ADD, MUL))

            def KP():
                need("T1")
                f(stt(A["KP"][:], A["T1"][:], 1.0, K[:, :, tok], ADD, MUL))

            def MAX_():
                j = jw(i, "norm2")
                w_filled(eng, i, "norm2")
                ts(NRM[:], bank(j, 0)[0:NH, 0:P], 1e-24, None, MAX).then_inc(emptied[j % 4], 2)

            def RI():
                made("NR")
                f(nc.vector.reciprocal(NRM[:], NRM[:]))

            def KK():
                for h in range(2):
                    w_filled(eng, i, "norm3", h)
                    pairs = slice(4 * h, 4 * h + 4)
                    tt(A["KK"][:, pairs, :], A["KQ"][:, pairs, :], bank(jw(i, "norm3"), h).rearrange("p (a b) -> p a b", a=4), MUL)\
                        .then_inc(emptied[jw(i, "norm3") % 4], 1)

            def BB():
                w_kept(eng, i, "norm3")
                made("EX")
                need("T1")
                f(stt(A["BB"][:], A["TA"][:], 1.0, A["KK"][:], ADD, MUL))

            def BH():
                need("BB")
                made("EN")
                f(stt(BKH[:, :, 0, :], gc(A["BB"]), 0.5, gc(A["EN"]), MUL, MUL))

            def KH():
                need("KP")
                f(tt(BKH[:, :, 1, :], gc(A["KP"]), gc(A["EN"]), MUL))

            end = gc(A["EL"])[:, :, HD - 1:HD].to_broadcast([P, 2 * KT, HD])

            def BD():
                need("BH")
                need("KH")
                made("EL")
                f(tt(BKD[:, :, 0, :], BKH[:, :, 0, :], end, MUL))

            def KD():
                f(tt(BKD[:, :, 1, :], BKH[:, :, 1, :], end, MUL))

            def Z():
                f(tt(A["Z"][:], R[:, :, tok], A["KP"][:], MUL))

            def ZR():
                need("Z")
                f(tt(A["Z"][:], A["Z"][:], bc(RK_), MUL))

            def AT():
                w_kept(eng, i, "norm3")
                f(stt(AR[:, :, 0, :], gc(A["KK"]), -1.0, gc(A["EX"]), MUL, MUL))

            def ELE_():
                f(nc.vector.tensor_copy(ELE[:], A["EL"][:].rearrange("p g (c t) -> p g c t", c=2)[:, :, :, HD - 1]))

            def RT():
                for c in range(2):
                    ins = tt(AR[:].rearrange("p (g c) x t -> p g c x t", c=2)[:, :, c, 1, :],
                             R[:, :, bass.ds(tok0 + c * HD, HD)], A["EL"][:, :, c * HD:(c + 1) * HD], MUL)
                f(ins)

            return dict(KQ=KQ, KSQ=KSQ, SG=SG, CS=CS, CX=CX, T1=T1, KP=KP, MAX=MAX_, RI=RI, KK=KK, BB=BB, BH=BH, KH=KH,
                        BD=BD, KD=KD, Z=Z, ZR=ZR, AT=AT, ELE=ELE_, RT=RT)

        def dve_tile(eng, i, last=False):
            steps = {} if last else prep_steps(eng, i)

            def prep(*names):
                if not last:
                    for name in names:
                        steps[name]()

            A = WT
            m3 = lambda T4, h: T4[:, h]
            b3 = lambda name, h: bank(jw(i, name), h).rearrange("p (a b) -> p a b", a=8)

            def added(name):
                for h in range(2):
                    w_filled(eng, i, name, h)
                    tt(m3(XT_, h), m3(XT_, h), b3(name, h), ADD).then_inc(emptied[jw(i, name) % 4], 1)

            over2 = lambda ap, a, b: ap.unsqueeze(1).unsqueeze(1).to_broadcast([ap.shape[0], a, b, ap.shape[1]])
            for q in range(4):
                j = jw(i, f"Q{q}")
                w_filled(eng, i, f"Q{q}")
                for dst, mask in ((A["P1T"], "U8"), (A["OT"], "UO")):
                    for c in range(2):
                        src = both(j)[0:HD].rearrange("s p (g c x t) -> s p g c x t", g=2, c=2, x=2)[:, :, :, c, 0, :]
                        tt(dst[c * HD:(c + 1) * HD, :, 2 * q:2 * q + 2, :], src, over2(CC[mask][0:HD], 2, 2), MUL)
                src = both(j).rearrange("s p (e x t) -> s p e x t", e=4, x=2)
                tt(NT[HD:P, :, 4 * q:4 * q + 4, :], src[HD:P, :, :, 0, :], over2(CC["US"][HD:P], 2, 4), MUL)
                tt(RBK[:, :, 4 * q:4 * q + 4, :], src[:, :, :, 1, :], over2(CC["UI"], 2, 4), MUL)\
                    .then_inc(emptied[j % 4], 2)
            for h in range(2):
                w_filled(eng, i, "M", h)
                tt(m3(A["P1"], h), b3("M", h), over(CC["L8"], 8), MUL).then_inc(emptied[jw(i, "M") % 4], 1)
            w_kept(eng, i, "Q3")
            for h in range(2):
                tt(m3(XT_, h), m3(A["P1T"], h), over(CC["I64"], 8), ADD).then_inc(dve_sum, 1)
            prep("KQ")
            w_kept(eng, i, "M")
            w_filled(eng, i, "M")
            prep("KSQ")
            w_sum(eng, i, "XT1b")
            added("XT2")
            eng.wait_ge(vc_made, i + 1)
            for h in range(2):
                w_filled(eng, i, "bonus", h)
                vv = V[:, 4 * h:4 * h + 4, bass.ds(i * P, P)]
                tt(vv, vv, bank(jw(i, "bonus"), h).rearrange("p (a b) -> p a b", a=4), MUL)\
                    .then_inc(emptied[jw(i, "bonus") % 4], 1)
            w_kept(eng, i, "XT2")
            added("XT3")
            prep("SG", "CS", "CX", "T1", "KP")
            w_kept(eng, i, "XT3")
            for h in range(2):
                j = jw(i, "T1" + "ab"[h])
                w_filled(eng, i, "T1" + "ab"[h])
                xt = FX[:, h].rearrange("p (b a) x n -> p b a x n", b=2)[:, :, :, 1, :]
                tt(xt, xt, both(j).rearrange("p b (a x) -> p b a x", a=4)[:, :, :, HD:P], ADD).then_inc(emptied[j % 4], 1)
            prep("MAX")
            for h in range(2):
                w_kept(eng, i, "T1" + "ab"[h], 0)
            added("T2")
            prep("RI")
            w_kept(eng, i, "T2")
            added("T3")
            for c in range(2):
                rows = slice(c * HD, (c + 1) * HD)
                j = jw(i, f"AS{c}")
                w_filled(eng, i, f"AS{c}")
                w_kept(eng, i, "NV")
                g = A["NV"][rows]
                tt(g, g, both(j)[rows].rearrange("p b (a n) -> p b a n", a=KT), ADD).then_inc(emptied[j % 4], 2)
                if c == 1:
                    w_kept(eng, i, "SY0")
                tt(STD[:], ST[:], spread(ELE[:, :, c], HD), MUL).then_inc(dve_sum, 1)
                if c == 0:
                    prep("KK", "BB", "BH", "KH")
                else:
                    prep("AT")
                w_sum(eng, i, f"STD{c}")
                w_filled(eng, i, f"SY{c}")
                tt(ST[:], STD[:], bank(jw(i, f"SY{c}"), 1).rearrange("p (a b) -> p a b", a=KT), ADD)\
                    .then_inc(emptied[jw(i, f"SY{c}") % 4], 1)
                if c == 0:
                    prep("BD", "KD", "Z", "ZR")
                else:
                    prep("ELE", "RT")
            w_kept(eng, i, "SY1")
            for h in range(2):
                w_filled(eng, i, "YU", h)
                rr = R[:, :, bass.ds(i * P + h * HD, HD)]
                tt(rr, rr, bank(jw(i, "YU"), h).rearrange("p (a b) -> p a b", a=KT), ADD)\
                    .then_inc(emptied[jw(i, "YU") % 4], 1)

        def dve_samples(eng):
            A = SM
            need = lambda name: s_dve(eng, name)
            f = lambda ins: ins.then_inc(smp_dve, 1)
            tok = slice(SEQ, T)
            s8 = lambda j: bank(j, 0)[:, 0:KT * NS].rearrange("p (a b) -> p a b", a=KT)
            eng.wait_ge(emptied[J_STO % 4], 2 * (J_STO // 4) + 2)

            def norm2():
                j = js("norm2")
                wait_filled(eng, j)
                ts(A["NR"][:], s8(j), 1e-24, None, MAX).then_inc(emptied[j % 4], 2)

            dve_features(eng, A, NS, tok, RST[:, KT * P:], need, lambda n: s_act(eng, n), smp_dve,
                         lambda: wait_emptied(eng, js("wpre")), lambda: wait_emptied(eng, js("apre")), norm2)
            small = lambda j, rows: both(j, KT * NS)[rows].rearrange("p e (a b) -> p e a b", a=KT)
            c4 = lambda name, rows: CC[name][rows].unsqueeze(1).to_broadcast([rows.stop - rows.start, KT, NS])
            bs, ks, bks = slice(0, NS), slice(NS, 2 * NS), slice(0, 2 * NS)
            j = js("Q")
            wait_filled(eng, j)
            for e in range(2):
                src = bank(j, e)[bks].rearrange("p (a x b) -> p a x b", a=KT, x=2)
                tt(A["P1T"][bs, e], src[bs, :, 0, :], c4("SU", bs), MUL)
                tt(A["NT"][ks, e], src[ks, :, 0, :], c4("SU", ks), MUL)
                tt(A["RBK"][:, e], src[:, :, 1, :], c4("SUI", bks), MUL).then_inc(emptied[j % 4], 1)
            j = js("M")
            wait_filled(eng, j)
            for e in range(2):
                tt(A["P1"][bs, e], small(j, bs)[:, e], c4("SL", bs), MUL).then_inc(emptied[j % 4], 1)
            dve_features2(eng, A, NS, tok, DS, need, smp_dve)
            wait_emptied(eng, js("Q"))
            for e in range(2):
                ins = tt(A["XT"][bs, e], A["P1T"][bs, e], c4("SI", bs), ADD)
            f(ins)
            need("XT1")
            wait_filled(eng, js("XT2"))
            for e in range(2):
                tt(A["XT"][bs, e], A["XT"][bs, e], small(js("XT2"), bs)[:, e], ADD).then_inc(emptied[js("XT2") % 4], 1)
            j = js("bonus")
            wait_filled(eng, j)
            tt(V[:, :, tok], V[:, :, tok], s8(j), MUL).then_inc(emptied[j % 4], 2)
            f(nc.vector.tensor_copy(A["DC"][:], A["EL"][:].rearrange("p g (b t) -> p g b t", t=DS)[:, :, :, DS - 1]))
            need("DC")
            j = js("GY")
            wait_emptied(eng, j, 0)
            kinds = bank(j, 0).rearrange("p (x a n) -> p x a n", x=2, a=KT)
            nc.vector.tensor_copy(R[:, :, tok], kinds[:, 1])
            tt(A["GT"][:], A["GT"][:], kinds[:, 0], ADD).then_inc(emptied[j % 4], 1)
            for q in range(4):
                st = S0T[:, 2 * q:2 * q + 2]
                decay = A["DC"][:, :, 2 * q:2 * q + 2].rearrange("p g b -> p b g").unsqueeze(3).to_broadcast([P, 2, KT, HD])
                f(tt(st, st, decay, MUL))
            wait_filled(eng, js("YU"))
            wait_emptied(eng, js("GY"))
            tt(R[:, :, tok], R[:, :, tok], s8(js("YU")), ADD).then_inc(emptied[js("YU") % 4], 2)
            for q in range(4):
                j = js(f"SS{q}")
                need(f"SW{q}")
                wait_filled(eng, j)
                for h in range(2):
                    st = S0T[:, 2 * q:2 * q + 2, 4 * h:4 * h + 4, :]
                    tt(st, st, bank(j, h).rearrange("p (a b v) -> p b a v", a=4, b=2), ADD).then_inc(emptied[j % 4], 1)

        def dve_ffn(eng, l, i, last):
            u0, j0 = ((U_F0, J_F0), (U_F1, J_F1))[l]
            h0 = KT * CHUNKS * l
            for q in range(8):
                if not (last and q == 7):
                    dve_split(eng, u0 + q + 1, i)
                for m in (2 * q, 2 * q + 1):
                    j = j0 + m
                    if q < 4:
                        eng.wait_ge(filled, i * (2 * FFN_J) + 2 * j + 2)
                        if m >= 2:
                            eng.wait_ge(square_made, i * KT + (h0 + m - 1))
                        stt(halves(RL[:, m % 2, :]), both(j, TH), 0.0, halves(RS1[:]), MAX, MUL)\
                            .then_inc(emptied[j % 4], 2)
                        if m >= 1:
                            dve_hidden_lo(eng, i, h0, m - 1)
                    else:
                        eng.wait_ge(filled, i * (2 * FFN_J) + 2 * j + 2)
                        tt(halves(X[:, m - 8, :]), halves(X[:, m - 8, :]), both(j, TH), ADD).then_inc(emptied[j % 4], 2)
                if q == 3:
                    dve_hidden_lo(eng, i, h0, 7)

        def dve_hidden_lo(eng, i, h0, m):
            eng.wait_ge(hhi_made, i * KT + (h0 + m + 1))
            tt(HL[:, m, :], QL[:, m % 2, :], HH[:, m, :].bitcast(F32), SUB).then_inc(hlo_made, 1)

        def run_dve(eng):
            nc.vector.memset(ST[:], 0.0).then_inc(pads_made, 1)
            nc.vector.memset(H[:, :, 0:1], 0.0).then_inc(pads_made, 1)
            wait_emptied(eng, J_PRM)
            nc.vector.tensor_copy(H[:, :, 513:553].rearrange("p k (b t) -> p k b t", b=NB)[:, :, :, 0],
                                  PRM2[:, SHF:SHF + 64].rearrange("p (b k) -> p k b", b=NB)).then_inc(pads_made, 1)
            ts(HKA[:], PRM[:, KA_:KA_ + KT], 0.5, None, MUL).then_inc(pads_made, 1)
            wait_emptied(eng, J_N0)
            nc.vector.reciprocal(RS0[:], RS0[:]).then_inc(rstd_made, 1)
            eng.wait_ge(rstd_made, 1)
            eng.wait_ge(pads_made, 3)

            def normed(k):
                stt(H[:, k, 1:513], X[:, k, 0:SEQ], col(NMIX + k), RS0[:, 0:SEQ], MUL, MUL)
                stt(samples(H[:, k, 513:553], 1, DS), samples(X[:, k, SEQ:T], 0, DS), col(NMIX + k),
                    samples(RS0[:, SEQ:T], 0, DS), MUL, MUL).then_inc(hn_made, 1)

            def shift_diff(k):
                eng.wait_ge(hn_made, k + 1)
                tt(DX[:, k, 0:SEQ], H[:, k, 0:SEQ], H[:, k, 1:513], SUB)
                tt(samples(DX[:, k, SEQ:T], 0, DS), samples(H[:, k, 513:553], 0, DS), samples(H[:, k, 513:553], 1, DS),
                   SUB).then_inc(dx_made, 1)

            def mixed(n):
                jx, k = n // 8, n % 8
                if n < 8:
                    if n + 2 < 8:
                        normed(n + 2)
                    if n + 1 < 8:
                        shift_diff(n + 1)
                    eng.wait_ge(dx_made, n + 1)
                if n >= 2:
                    eng.wait_ge(xlo_made, n - 1)
                m = col(MIX + 8 * XS_ORDER[jx] + k)
                stt(XF[:, n % 2, 0:SEQ], DX[:, k, 0:SEQ], m, H[:, k, 1:513], MUL, ADD)
                stt(samples(XF[:, n % 2, SEQ:T], 0, DS), samples(DX[:, k, SEQ:T], 0, DS), m,
                    samples(H[:, k, 513:553], 1, DS), MUL, ADD).then_inc(xf_made, 1)
                if n == 7:
                    nc.vector.memset(WH[LW:LW + 1, :], 1.0).then_inc(pads_made, 1)
                    nc.vector.memset(AH[LA:LA + 1, :], 1.0).then_inc(pads_made, 1)
                    nc.vector.tensor_copy(SHT[:, :, 0:1], H[:, :, 512:513])
                    nc.vector.tensor_copy(SHT[:, :, 1:9], samples_of_all(H)[:, :, :, DS]).then_inc(sht_made, 1)

            samples_of_all = lambda T3: T3[:, :, 513:553].rearrange("p k (b t) -> p k b t", b=NB)
            normed(0)
            normed(1)
            shift_diff(0)

            def mixed_lo(n):
                jx, k = n // 8, n % 8
                eng.wait_ge(xhi_made, n + 1)
                tt(XSL[jx % 2][:, k, :], XF[:, n % 2, :], XSH[jx % 2][:, k, :].bitcast(F32), SUB).then_inc(xlo_made, 1)

            first = prep_steps(eng, None)
            for what, n in timeline():
                if what == "split":
                    dve_split(eng, n)
                elif what == "first":
                    if n == "squares":
                        wait_emptied(eng, J_K + 7)
                    if n == "exps":
                        eng.wait_ge(resets_loaded, 16)
                    for name in {"squares": ("KQ", "KSQ"), "exps": ("SG", "CS", "CX"), "root": ("MAX", "RI")}.get(n, ()):
                        first[name]()
                elif what == "xs":
                    if n == 0:
                        mixed(0)
                    if n + 1 < 48:
                        mixed(n + 1)
                    mixed_lo(n)
                elif n in (J_G1, J_G1 + 1):
                    wait_emptied(eng, n)
                    g = GH[:, 0, :] if n == J_G1 else GH[0:LG - P, 1, :]
                    ts(g, g, 0.5, 0.5, MUL, ADD).then_inc(gsig_made, 1)
            first["KK"]()
            wait_filled(eng, jv("V7"))
            for name in FIRST[DVE_PREP][6:]:
                first[name]()
            with eng.Fori(0, TILES - 1) as i:
                dve_tile(eng, i)
            dve_tile(eng, TILES - 1, last=True)
            dve_samples(eng)
            for k in range(KT):
                j = jg("mean", k)
                wait_filled(eng, j)
                tt(halves(R[:, k, :]), halves(R[:, k, :]), both(j, TH), SUB).then_inc(emptied[j % 4], 2)
            dve_split(eng, U_WO)
            wait_emptied(eng, jg("var", 0))
            nc.vector.reciprocal(GR[:], GR[:]).then_inc(gn_rstd, 1)
            for n in range(KT + 2):
                if n < KT:
                    j = jg("spread", n)
                    if n == 0:
                        wait_emptied(eng, jg("mean", KT - 1))
                    wait_filled(eng, j)
                    stt(halves(R[:, n, :]), halves(R[:, n, :]), col(GNW + n), both(j, TH), MUL, MUL)\
                        .then_inc(emptied[j % 4], 2)
                if 1 <= n <= KT:
                    k = n - 1
                    wait_emptied(eng, jg("spread", k))
                    stt(R[:, k, :], R[:, k, :], col(GNB + k), V[:, k, :], ADD, ADD).then_inc(gn_step, 1)
                    if k == 0:
                        wait_emptied(eng, jg("gate", KT - 1))
                    eng.wait_ge(gn_step, k + 1)
                    tt(R[:, k, :], R[:, k, :], GG[:, k, :], MUL).then_inc(gn_gated, 1)
                if n >= 2:
                    eng.wait_ge(gn_hi, n - 1)
                    tt(XSL[1][:, n - 2, :], R[:, n - 2, :], XSH[1][:, n - 2, :].bitcast(F32), SUB).then_inc(gn_lo, 1)
            for n in range(4):
                dve_split(eng, U_WO + n + 1)
                for m in (2 * n, 2 * n + 1):
                    j = J_WO + m
                    wait_filled(eng, j)
                    tt(halves(X[:, m, :]), halves(X[:, m, :]), both(j, TH), ADD).then_inc(emptied[j % 4], 2)
                for k in (2 * n - 2, 2 * n - 1) if n else ():
                    dve_gained_lo(eng, 1, k, NFFN)
            for k in (6, 7):
                dve_gained_lo(eng, 1, k, NFFN)
            dve_rstd(eng, 1, J_N1)
            with eng.Fori(0, CHUNKS - 1) as i:
                dve_ffn(eng, 0, i, False)
            dve_ffn(eng, 0, CHUNKS - 1, False)
            wait_filled(eng, J_N2)
            nc.vector.memset(EXT[:, :, 0:PBUF], 0.0)
            dve_rstd(eng, 2, J_N2)
            wins = [0]

            def win(ins):
                ins.then_inc(pool_win, 1)
                wins[0] += 1
                eng.wait_ge(pool_win, wins[0])

            def pool_group(gi):
                g = GROUP_ORDER[gi]
                w = POOLS[g]
                for k in (2 * g, 2 * g + 1):
                    stt(EXT[:, k, PBUF:S0_], X[:, k, 0:SEQ], col(NMIX + 8 + k), RS1[:, 0:SEQ], MUL, MUL)
                    stt(samples(EXT[:, k, S0_:], PBUF, DS), samples(X[:, k, SEQ:T], 0, DS), col(NMIX + 8 + k),
                        samples(RS1[:, SEQ:T], 0, DS), MUL, MUL).then_inc(hn_made, 1)
                if gi == 0:
                    wait_emptied(eng, J_PST)
                else:
                    eng.wait_ge(pool_diff, 2 * gi)
                eng.wait_ge(hn_made, KT + 2 * gi + 2)
                src = EXT[:, 2 * g:2 * g + 2, :]
                step, b = 1, 0
                while step < w:
                    dst = WS[b][:]
                    win(tt(dst[:, :, 2 * step - 1:], src[:, :, 2 * step - 1:], src[:, :, step - 1:-step], ADD))
                    src, step, b = dst, 2 * step, 1 - b
                for kk in range(2):
                    k = 2 * g + kk
                    head = src[:, kk, PBUF:PBUF + 16]
                    win(tt(head, head, CC[f"corr{w}"], MUL))
                    stt(DF[:, k, 0:SEQ], src[:, kk, PBUF:S0_], 1.0 / w, EXT[:, k, PBUF:S0_], MUL, SUB)
                    stt(samples(DF[:, k, SEQ:T], 0, DS), samples(src[:, kk, S0_:], PBUF, DS), 1.0 / w,
                        samples(EXT[:, k, S0_:], PBUF, DS), MUL, SUB).then_inc(pool_diff, 1)

            def pool_rest(gi):
                for i in (2 * gi, 2 * gi + 1):
                    k = POOL_ORDER[i]
                    eng.wait_ge(pool_hi, i + 1)
                    tt(XSL[0][:, k, :], DF[:, k, :], XSH[0][:, k, :].bitcast(F32), SUB).then_inc(pool_lo, 1)

            def pool_out(gi):
                for m in POOL_ORDER[2 * gi:2 * gi + 2]:
                    j = jpw(m)
                    wait_filled(eng, j)
                    stt(halves(X[:, m, :]), both(j, TH), PRM2[:, PSC + m:PSC + m + 1], halves(X[:, m, :]), MUL, ADD)\
                        .then_inc(emptied[j % 4], 2)

            for gi in range(4):
                pool_group(gi)
                if gi >= 2:
                    pool_out(gi - 2)
                if gi >= 1:
                    pool_rest(gi - 1)
            pool_rest(3)
            pool_out(2)
            dve_split(eng, U_F1)
            pool_out(3)
            for k in POOL_ORDER:
                dve_gained_lo(eng, 3, k, NFFN + 8)
            dve_rstd(eng, 3, J_N3)
            with eng.Fori(0, CHUNKS - 1) as i:
                dve_ffn(eng, 1, i, False)
            dve_ffn(eng, 1, CHUNKS - 1, True)
            wait_filled(eng, J_YT)
            nc.vector.reciprocal(YR[:, 0:4], bank(J_YT, 0)[:, 0:4]).then_inc(emptied[J_YT % 4], 1)
            nc.vector.reciprocal(YR[0:NS, 4:5], bank(J_YT, 0)[0:NS, 4:5]).then_inc(emptied[J_YT % 4], 1)

        block = ctx.enter_context(nc.Block())

        @block.sync
        def _(sp):
            run_sp(sp)

        @block.tensor
        def _(pe):
            run_pe(pe)

        @block.scalar
        def _(eng):
            run_act(eng)

        @block.vector
        def _(eng):
            run_dve(eng)


OUTS = (("y_prompt", (1, SEQ, D)), ("y_sample", (NB, DS, D)), ("wkv_prompt", (1, 1, NH, HD, HD)),
        ("shift_prompt", (1, 1, D)), ("pool_prompt", (1, 1, PBUF, D)), ("wkv_sample", (1, NB, NH, HD, HD)),
        ("shift_sample", (1, NB, D)), ("pool_sample", (1, NB, PBUF, D)))
UNUSED = ("rwkv_v0", "rwkv_v1", "rwkv_v2")


def kernel(**inputs):
    import numpy as np
    import concourse.bacc as bacc
    from concourse import mybir
    from concourse.bass_utils import run_bass_kernel_spmd

    nc = bacc.Bacc("TRN2", target_bir_lowering=False, num_devices=1)
    table, _, resets, head_rows = constants()
    arrays = {n: np.ascontiguousarray(v) for n, v in inputs.items() if n not in UNUSED}
    arrays |= {"const_table": table, "resets": resets, "head_rows": head_rows}
    a = {n: nc.dram_tensor(f"in_{n}", v.shape, mybir.dt.from_np(v.dtype), kind="ExternalInput").ap()
         for n, v in arrays.items()}
    o = {n: nc.dram_tensor(f"out_{n}", s, mybir.dt.float32, kind="ExternalOutput").ap() for n, s in OUTS}
    build(nc, a, o)
    r = run_bass_kernel_spmd(nc, [{f"in_{n}": v for n, v in arrays.items()}], core_ids=[0])
    return tuple(r.results[0][f"out_{n}"] for n, _ in OUTS)
```

```python
from contextlib import ExitStack

import numpy as np
import concourse.bass as bass
from concourse import mybir

F32 = mybir.dt.float32
F32R = mybir.dt.float32r
ALU = mybir.AluOpType
ACT = mybir.ActivationFunctionType
MUL, ADD, SUB, MAX, BYP = ALU.mult, ALU.add, ALU.subtract, ALU.max, ALU.bypass

P = 128
D = 1024
KT = D // P
SEQ, NB, DS = 512, 8, 4
NS = NB * DS
T = SEQ + NS
TH = T // 2
HD, NH = 64, 16
DFF = 4 * D
UW = 256
POOLS = (2, 4, 8, 16)
PBUF = 15
GROUP_ORDER = (3, 2, 1, 0)
POOL_ORDER = [2 * g + e for g in GROUP_ORDER for e in range(2)]
LW, LA, LG = 64, 64, 160
DECAY = float(np.exp(-0.5))
NORM_EPS, GN_EPS = 1e-6, 64e-5

NMIX, NFFN, NFIN, MIX = 0, 16, 32, 40
KK_, KA_, RK_, GNW, GNB = 88, 96, 104, 112, 120
PSC, SHF = 0, 8
XS_TILES = 5 * KT

U_WA, U_G1, U_G1M, U_RKV, U_WO = 0, 1, 2, 3, 15
U_F0 = 19
U_POOL = U_F0 + 32
U_F1 = U_POOL + 1
FFN_U, FFN_J = 8, 16
CHUNKS = DFF // D

J_X, J_PRM, J_N0 = 0, 5, 6
J_WA, J_G1, J_R, J_K, J_V = 7, 8, 10, 18, 26
V_SEQ = ("V0", "V1", "V2", "V3", "wpre", "apre", "norm2", "V4", "V5", "norm3", "V6", "V7")
J_SHO = J_V + len(V_SEQ)
PREP_JOBS = ("wpre", "apre", "norm2", "norm3")
J_WKV = J_SHO + 1
WKV_JOBS = ("Q0", "Q1", "Q2", "Q3", "M", "tb0", "bonus", "P2", "tb1", "P2T", "tv0", "XT2", "tv1", "P4", "XT3", "X",
            "wpre", "apre", "F", "FT", "F2", "T1a", "T1b", "norm2", "T2", "F4", "NV", "T3", "AS0", "norm3", "U0",
            "SY0", "AS1", "U1", "SY1", "YU")
LAST_JOBS = [n for n in WKV_JOBS if n not in PREP_JOBS]
JP = len(WKV_JOBS)
assert JP % 4 == 0 and len(PREP_JOBS) == 4
TILES = SEQ // P
J_LAST = J_WKV + JP * (TILES - 1)
J_STO = J_LAST + len(LAST_JOBS)
SMP_JOBS = ("wpre", "apre", "norm2", "s0t0", "s0t1", "s0t2", "s0t3", "Q", "M", "P2", "tBK", "XT2", "tV", "bonus", "GY",
            "tG", "U", "YU", "SS0", "SS1", "TO0", "TO1", "SS2", "TO2", "TO3", "SS3", "TO4", "TO5", "TO6", "TO7")
J_SMP = J_STO + 1
J_GN = J_SMP + len(SMP_JOBS)
GN_JOBS = ([("mean", k) for k in range(KT)] + [("gate", k) for k in range(4)] + [("var", 0)]
           + [("gate", k) for k in range(4, KT)] + [("spread", k) for k in range(KT)])
J_WO = J_GN + len(GN_JOBS)
J_N1 = J_WO + KT
J_F0 = J_N1 + 1
J_N2 = J_F0 + FFN_J * CHUNKS
J_PST = J_N2 + 1
J_PW = J_PST + 1
J_PO = J_PW + 6
J_N3 = J_PW + KT + 2
J_F1 = J_N3 + 1
J_N4 = J_F1 + FFN_J * CHUNKS
J_Y = J_N4 + 1
J_YT = J_Y + 1

DVE_PREP = ("KQ", "KSQ", "SG", "CS", "CX", "T1", "KP", "RI", "BB", "BH", "KH", "BD", "KD", "Z", "ZR", "AT", "ELE", "RT")
ACT_PREP = ("EL", "EN", "EX", "NR")
FIRST = {DVE_PREP: ("KQ", "KSQ", "SG", "CS", "CX", "RI", "T1", "KP", "BB", "BH", "KH", "BD", "KD", "Z", "ZR", "AT",
                    "ELE", "RT"), ACT_PREP: ("EL", "EN", "NR", "EX")}
DVE_SUMS = ("XT1a", "XT1b", "STD0", "STD1")
DVE_FEATURES = ("KQ", "KSQ", "SG", "CS", "CX", "RI", "KK", "AT", "AG", "BB", "BH", "T1", "T2", "KP", "KH", "RT", "BD",
                "KD", "Z", "ZR")
ACT_FEATURES = ("NR", "EL", "EN", "EX")
SMP_ACT = ACT_FEATURES + ("UM0", "UM1", "UM2", "UM3")
SMP_DVE = DVE_FEATURES + ("XT1", "DC", "SW0", "SW1", "SW2", "SW3")


def constants():
    s = np.arange(P)[:, None]
    c = np.arange(HD)[None, :]
    r = s % HD
    same8 = (r // 8) == (c // 8)
    e = np.arange(P)[None, :]
    parts = {
        "ident": (s == e), "ones": np.ones((P, P)),
        "eps": np.broadcast_to(np.array([[NORM_EPS, GN_EPS]]), (P, 2)), "bones": (s // HD == e // HD),
        "bmean": (s // HD == e // HD) / HD,
        "U8": (c > r) & same8, "L8": (c < r) & same8, "UO": (c > r) & ~same8, "US": c > r, "UI": c >= r,
        "I64": c == r,
    }
    q = np.arange(NS)[None, :]
    sameb = (s % NS) // DS == q // DS
    parts |= {"SU": (q > s % NS) & sameb, "SL": (q < s % NS) & sameb, "SUI": (q >= s % NS) & sameb,
              "SI": q == s % NS, "SB": (s % NS) // DS == np.arange(NB)[None, :]}
    t = np.arange(16)[None, :]
    for w in POOLS:
        parts[f"corr{w}"] = np.broadcast_to(w / np.minimum(t + 1, w), (P, 16))
    parts["headsum"] = (np.arange(30)[None, :] - 14) == s // HD
    at, n = {}, 0
    for k, v in parts.items():
        at[k] = (n, v.shape[1])
        n += v.shape[1]
    table = np.concatenate([np.asarray(v, np.float32) for v in parts.values()], axis=1).astype(np.float32)
    resets = np.ones((1, KT * P + KT * NS), np.float32)
    resets[0, 0:KT * P:HD] = 0
    resets[0, KT * P::DS] = 0
    n = np.arange(NH)[:, None, None]
    headrow = (n // 2 == np.arange(KT)[None, :, None]) & (n % 2 == np.arange(P)[None, None, :] // HD)
    return table, at, resets, headrow.reshape(NH, KT * P).astype(np.float32)


def build(nc, a, o):
    table, CAT, _, _ = constants()
    ctx = ExitStack()
    with ctx:
        cursor = [(nc.sbuf_base + 31) // 32 * 32]

        def region(nbytes):
            off = cursor[0]
            cursor[0] += (nbytes + 31) // 32 * 32
            assert cursor[0] <= nc.sbuf_usable_end, (cursor[0], nc.sbuf_usable_end)
            return off

        def at(name, shape, off, dt=F32):
            return nc.alloc_sbuf_tensor_at(name, shape, dt, offset=off)

        def sem(name):
            return ctx.enter_context(nc.semaphore(name))

        FB = 4 * KT * T
        X = at("x_res", [P, KT, T], region(FB))
        CT = at("const_sb", [P, table.shape[1]], region(4 * table.shape[1]))
        PRM = at("params", [P, P], region(4 * P))
        PRM2 = at("params2", [P, 72], region(4 * 72))
        o_rst = region(4 * (KT * P + KT * NS))
        XF = at("xs_full", [P, 2, T], o_rst)
        RST = at("resets_sb", [P, KT * P + KT * NS], o_rst)
        o_raw, o_w = region(2 * 8192), region(4 * 8192)
        RAW = [at(f"w_raw{b}", [P, KT, UW], o_raw + 8192 * b) for b in range(2)]
        WHI = [at(f"w_hi{b}", [P, KT, UW], o_w + 8192 * b, F32R) for b in range(2)]
        WLO = [at(f"w_lo{b}", [P, KT, UW], o_w + 8192 * (2 + b), F32R) for b in range(2)]
        o_a, o_b, o_h, o_l = region(4 * FB), region(2 * FB), region(4 * KT * 553), region(4 * 4 * T)
        o_s = region(4096)
        XSH = [at(f"xs_hi{b}", [P, KT, T], o_a + 2 * FB * b, F32R) for b in range(2)]
        XSL = [at(f"xs_lo{b}", [P, KT, T], o_a + 2 * FB * b + FB, F32R) for b in range(2)]
        R = at("r_all", [P, KT, T], o_b)
        K = at("k_all", [P, KT, T], o_b + FB)
        H = at("h_shift", [P, KT, 553], o_h)
        V = at("v_all", [P, KT, T], o_h)
        WH = at("w_hidden", [P, T], o_l)
        AH = at("a_hidden", [P, T], o_l + 4 * T)
        GH = at("g_hidden", [P, 2, T], o_l + 8 * T)
        ST = at("state", [P, KT, HD], o_s)
        STD = at("state_decayed", [P, KT, HD], o_s + 2048)
        SHT = at("shift_cols", [P, KT, 9], o_s + 2048)
        XIN = at("x_rows", [P, 5, D], o_a)
        PR = at("param_rows", [P, P], o_w)
        PR2 = at("param_rows2", [72, P], o_w + 512)
        SQ = at("squares", [P, KT, T], o_b)
        SQR = at("row_squares", [P, 5, D], o_b)
        DG0 = at("rstd_diag", [P, 5, P], o_b + 20480)
        SS = at("square_sums", [P, 5], o_b + 24576)
        HN = at("normed", [P, KT, T], o_b + FB)
        DX = at("shift_diff", [P, KT, T], o_b + FB)
        RS0, RS1 = at("rstd0", [P, T], o_l), at("rstd1", [P, T], o_h)
        slots = [o_a + 4096 * n for n in range(17)]
        feat, TMs = slots[0:9], slots[9:13]
        rw = lambda n: o_raw + 4096 * n
        ww = lambda n: o_w + 4096 * n
        W2A, A2A = at("w2_aug", [P, D], slots[15]), at("a2_aug", [P, D], slots[16])
        AR = at("rates_recept", [P, 2 * KT, 2, HD], slots[0])
        BKH = at("b_k_hat", [P, 2 * KT, 2, HD], slots[9])
        BKD = at("b_k_decayed", [P, 2 * KT, 2, HD], slots[11])
        WT = {}
        slots += [ww(6), ww(7)]
        for name, n in (("TA", 9), ("KSQ", 10), ("TW", 11), ("SG", 11), ("CX", 11), ("BB", 11), ("CS", 12), ("EN", 12),
                        ("EL", 13), ("KQ", 14), ("KK", 14), ("VC", 2), ("T1", 17), ("KP", 17), ("Z", 17), ("EX", 18)):
            WT[name] = at("wkv_" + name, [P, KT, P], slots[n])
        for name, off in (("P1T", slots[3]), ("F", slots[3]), ("P1", slots[4]), ("F2T", slots[4]),
                          ("P2", slots[5]), ("F2", slots[5]), ("P2T", slots[6]), ("F4", slots[6]),
                          ("P4", ww(4)), ("X", ww(4)), ("OT", ww(5)), ("NV", slots[2])):
            WT[name] = at("wkv_" + name, [P, 2, KT, HD], off)
        FX = at("wkv_FT_XT", [P, 2, KT, 2, HD], slots[7])
        NT = at("wkv_NT", [P, 2, 2 * KT, HD], rw(0))
        HROWS = slice(96, 96 + NH)
        HR = at("head_rows", [P, KT, P], o_l)[HROWS]
        RBK = at("wkv_RBK", [P, 2, 2 * KT, HD], rw(2))
        UV = at("wkv_UV", [P, 2, D], ww(0))
        BKT = at("wkv_BKT", [P, 2, D], ww(2))
        o_x = region(64 + 512 + 32)
        HKA = at("half_k_a", [P, KT], o_x + 576)
        ELE = at("chunk_decay", [P, KT, 2], o_x)
        NRM = at("head_norms", [P, P], o_x + 64)[HROWS]
        SHO = at("shift_rows", [9, D], slots[2])
        STO = at("state_rows", [HD, D], ww(4))
        SM = {}
        unit = lambda n: feat[n // 4] + 1024 * (n % 4)
        for name, n in (("TW", 0), ("SG", 0), ("CX", 0), ("AG", 0), ("BB", 0), ("CS", 1), ("EL", 2), ("EN", 3), ("EX", 4),
                        ("TA", 5), ("T1", 5), ("KP", 5), ("KQ", 6), ("KK", 6), ("Z", 6), ("KSQ", 7), ("NR", 7),
                        ("GT", 14)):
            SM[name] = at("smp_" + name, [P, KT, NS], unit(n))
        for name, first, second, n in (("AR", "AT", "RT", 8), ("BKH", "BH", "KH", 10), ("BKD", "BD", "KD", 12)):
            SM[name] = at("smp_" + name, [P, KT, 2, NS], unit(n))
            SM[first], SM[second] = SM[name][:, :, 0, :], SM[name][:, :, 1, :]
        SM["DC"] = at("smp_DC", [P, KT, NB], unit(15))
        for n, name in enumerate(("P1T", "P1", "NT", "RBK", "XT", "P2")):
            SM[name] = at("smp_" + name, [2 * NS, 2, KT, NS], feat[4] + 2048 * n)
        SM["BKT"] = at("smp_BKT", [2 * NS, D], feat[7])
        SM["UV"] = at("smp_UV", [2 * NS, D], feat[8])
        SM["G"] = at("smp_G", [NS, D], TMs[0])
        UVM = [at(f"smp_uv_masked{n}", [2 * NS, 2, D], slots[10] + 8192 * n) for n in range(2)]
        S0L = at("smp_state_rows", [HD, NB, NH, HD], o_raw)
        S0T = at("smp_state", [P, NB, KT, HD], o_b + FB)
        SO = at("smp_state_out", [HD, NB, D], o_raw)
        G2A, G2B = at("g2_a", [P, D], o_a), at("g2_b", [LG - P, D], o_a + 4096)
        GG = at("gn_gate", [P, KT, T], o_a + 8192)
        GR = at("gn_rstd", [P, T], o_a + 8192 + FB)[HROWS]
        GQ = at("gn_squares", [P, KT, T], o_b + FB)
        WPL = at("pool_w_whole", [P, KT, UW], o_w + 8192 * (U_POOL % 2))
        EXT = at("pool_ext", [P, KT, PBUF + SEQ + NB * (PBUF + DS)], o_b)
        WS = [at(f"pool_sum{b}", [P, 2, PBUF + SEQ + NB * (PBUF + DS)], o_a + 2 * FB + 5440 * b) for b in range(2)]
        DF = at("pool_diff", [P, KT, T], o_a + 2 * FB + 11264)
        PSI = at("pool_state_rows", [P, D], o_l)
        PCO = at("pool_out_cols", [P, KT, NB, PBUF], o_l + 4096)
        PRO = [at(f"pool_out_rows{n}", [P, D], o_h + 4096 * (1 + n)) for n in range(2)]
        S0_ = PBUF + SEQ
        HH, HL = XSH[1], XSL[1]
        RL = at("relu_tmp", [P, 2, T], o_l)
        QL = at("square_tmp", [P, 2, T], o_l + 8 * T)
        YR = at("y_rstd", [P, 5], o_h + 4 * T)
        YO = [at(f"y_rows{n}", [P, D], o_a + 4096 * n) for n in range(5)]

        CC = {k: CT[:, n:n + w] for k, (n, w) in CAT.items()}
        ident, ones, bones, bmean = (CC[k] for k in ("ident", "ones", "bones", "bmean"))

        PS = ctx.enter_context(nc.psum_tensor("ps", [P, 8, 512], F32))

        def bank(j, half):
            return PS[:, 2 * (j % 4) + half, :]

        def both(j, n=512):
            return PS[:, 2 * (j % 4):2 * (j % 4) + 2, 0:n]

        def halves(ap):
            return ap.rearrange("p (a t) -> p a t", a=2)

        def col(n):
            return PRM[:, n:n + 1]

        def spread(ap, n):
            return ap.unsqueeze(2).to_broadcast([ap.shape[0], ap.shape[1], n])

        def over(ap, n):
            return ap.unsqueeze(1).to_broadcast([ap.shape[0], n, ap.shape[1]])

        filled = sem("psum_filled")
        emptied = [sem(f"psum_emptied{n}") for n in range(4)]
        raw_loaded = [sem(f"raw_loaded{b}") for b in range(2)]
        whi_made, wlo_made = sem("whi_made"), sem("wlo_made")
        const_loaded, prm_loaded, ss_made, diag_made = (sem(n) for n in (
            "const_loaded", "prm_loaded", "square_sums_made", "diag_made"))
        x_loaded = [sem(f"x_loaded{n}") for n in range(5)]
        pads_made = sem("pads_made")
        sq_summed = sem("sq_summed")
        sq_made, rstd_made, hn_made = sem("sq_made"), sem("rstd_made"), sem("hn_made")
        dx_made, xf_made, xhi_made, xlo_made = sem("dx_made"), sem("xf_made"), sem("xhi_made"), sem("xlo_made")
        gsig_made, a1_loaded, scaled_made, plain_used = (sem(n) for n in (
            "gsig_made", "a1_loaded", "scaled_made", "plain_used"))
        aug_loaded, resets_loaded, s0_loaded, g2_loaded, pst_loaded = (sem(n) for n in (
            "aug_loaded", "resets_loaded", "s0_loaded", "g2_loaded", "pst_loaded"))
        out_stored, sht_made = sem("out_stored"), sem("sht_made")
        headrow_loaded, vc_made = sem("headrow_loaded"), sem("vc_made")
        settled, ys_filled = sem("settled"), sem("ys_filled")
        square_made, hhi_made, hlo_made = sem("square_made"), sem("hhi_made"), sem("hlo_made")
        dve_prep, act_prep, dve_sum = sem("dve_prep"), sem("act_prep"), sem("dve_sum")
        smp_dve, smp_act = sem("smp_dve_feature"), sem("smp_act_feature")
        gn_squared, gn_rstd, gn_step, gn_gated, gn_hi, gn_lo = (sem(n) for n in (
            "gn_squared", "gn_rstd", "gn_step", "gn_gated", "gn_hi", "gn_lo"))
        pool_win, pool_diff = sem("pool_window"), sem("pool_diff")
        pool_cols = sem("pool_cols")

        def wait_filled(eng, j, half=1):
            eng.wait_ge(filled, 2 * j + half + 1)

        def wait_emptied(eng, j, half=1):
            eng.wait_ge(emptied[j % 4], 2 * (j // 4) + half + 1)

        def wait_free(pe, j, half=1):
            if j >= 4:
                wait_emptied(pe, j - 4, half)

        def jv(name):
            return J_V + V_SEQ.index(name)

        def spot(i, name):
            if i is None:
                return jv(name), 0
            if isinstance(i, int):
                return J_LAST + LAST_JOBS.index(name), 0
            return J_WKV + WKV_JOBS.index(name), i

        def jw(i, name):
            return spot(i, name)[0]

        def jg(what, k):
            return J_GN + GN_JOBS.index((what, k))

        def js(name):
            return J_SMP + SMP_JOBS.index(name)

        def w_filled(eng, i, name, half=1):
            j, n = spot(i, name)
            eng.wait_ge(filled, n * (2 * JP) + (2 * j + half + 1))

        def w_kept(eng, i, name, half=1):
            j, n = spot(i, name)
            eng.wait_ge(emptied[j % 4], n * (JP // 2) + (2 * (j // 4) + half + 1))

        def w_free(pe, i, name):
            j, n = spot(i, name)
            pe.wait_ge(emptied[j % 4], n * (JP // 2) + 2 * ((j - 4) // 4) + 2)

        def prep_count(i, names, name):
            return FIRST[names].index(name) + 1 if i is None else (i + 1) * len(names) + names.index(name) + 1

        def w_prep(eng, i, name):
            eng.wait_ge(dve_prep, i * len(DVE_PREP) + DVE_PREP.index(name) + 1)

        def w_sum(eng, i, name):
            eng.wait_ge(dve_sum, i * len(DVE_SUMS) + DVE_SUMS.index(name) + 1)

        def s_dve(eng, name):
            eng.wait_ge(smp_dve, SMP_DVE.index(name) + 1)

        def s_act(eng, name):
            eng.wait_ge(smp_act, SMP_ACT.index(name) + 1)

        SUMMED = {1: 4, 2: 6, 4: 6}

        def summed_by(n, k):
            return sum(SUMMED[m] - 1 for m in SUMMED if m < n) + k

        ORDER = {n: list(range(KT)) for n in (0, 1, 2, 4)} | {3: POOL_ORDER}

        def jy(n):
            return J_Y if n == 0 else J_YT + n

        def jpw(m):
            return J_PW + POOL_ORDER.index(m) + (2 if m in POOL_ORDER[6:] else 0)

        def last_job(u):
            if u < U_RKV:
                return (J_WA, J_G1 + 1, J_G1 + 1)[u]
            if u < U_WO:
                return J_R + 2 * (u - U_RKV) + 1 if u < U_RKV + 8 else jv(f"V{2 * (u - U_RKV) - 15}")
            if u < U_F0:
                return J_WO + 2 * (u - U_WO) + 1
            if u < U_POOL:
                return J_F0 + 2 * (u - U_F0) + 1
            return J_PW + KT + 1 if u == U_POOL else J_F1 + 2 * (u - U_F1) + 1

        w1_v = a["rwkv_w1"][0].rearrange("(k p) n -> p k n", p=P)
        a1_v = a["rwkv_a1"][0].rearrange("(k p) n -> p k n", p=P)
        g1_v = a["rwkv_g1"][0].rearrange("(k p) n -> p k n", p=P)
        rkv_v = a["rwkv_w_rkv"][0].rearrange("j (k p) n -> j p k n", p=P)
        wo_v = a["rwkv_w_o"][0].rearrange("(k p) n -> p k n", p=P)
        up_v = [a["ffn_w1"][l].rearrange("(k p) (c n) -> p k c n", p=P, n=D) for l in range(2)]
        dn_v = [a["ffn_w2"][l].rearrange("(c k p) n -> c p k n", p=P, k=KT) for l in range(2)]
        pool_v = a["pool_w"][0].rearrange("g (k p) n -> p (g k) n", p=P)

        def unit_width(u):
            return LG if u in (U_G1, U_G1M) else UW

        def sp_unit(sp, u, src, i=0):
            if u >= 2:
                sp.wait_ge(whi_made, i * FFN_U + u - 1)
                sp.wait_ge(wlo_made, i * FFN_U + u - 1)
            sp.dma_start(RAW[u % 2][:, :, 0:unit_width(u)], src).then_inc(raw_loaded[u % 2], 16)

        def store(sp, dst, src):
            sp.dma_start(dst, src).then_inc(out_stored, 16)
            stores[0] += 1

        stores = [0]

        def sp_ffn(sp, l, i):
            u0 = (U_F0, U_F1)[l]
            for q in range(4):
                sp_unit(sp, u0 + q, up_v[l][:, :, i, q * UW:(q + 1) * UW], i)
            for q in range(4):
                sp_unit(sp, u0 + 4 + q, dn_v[l][i, :, :, q * UW:(q + 1) * UW], i)

        def run_sp(sp):
            first = 2 * P + 2
            sp.dma_start(CT[:, 0:first], a["const_table"][:, 0:first]).then_inc(const_loaded, 16)
            xp = a["x_prompt"][0].rearrange("(a p) d -> a p d", p=P)
            for n in range(4):
                sp.dma_start(XIN[:, n, :], xp[n]).then_inc(x_loaded[n], 16)
            sp.dma_start(XIN[0:NS, 4, :], a["x_sample"].rearrange("b t d -> (b t) d")).then_inc(x_loaded[4], 16)
            rows = lambda ap: ap.rearrange("a (k p) -> (a k) p", p=P)
            for name, r0, n in (("norm_mix", NMIX, 2), ("norm_ffn", NFFN, 2), ("rwkv_k_k", KK_, 1), ("rwkv_k_a", KA_, 1),
                                ("rwkv_gn_w", GNW, 1), ("rwkv_gn_b", GNB, 1)):
                sp.dma_start(PR[r0:r0 + 8 * n, :], rows(a[name])).then_inc(prm_loaded, 16)
            sp.dma_start(PR[NFIN:NFIN + 8, :], a["norm_final"].rearrange("(k p) -> k p", p=P)).then_inc(prm_loaded, 16)
            sp.dma_start(PR[MIX:MIX + 48, :], rows(a["rwkv_mix"][0])).then_inc(prm_loaded, 16)
            sp.dma_start(PR[RK_:RK_ + 8, :], a["rwkv_r_k"][0].rearrange("(k e) d -> k (e d)", e=2)).then_inc(prm_loaded, 16)
            sp.dma_start(PR2[PSC:PSC + 8, :], rows(a["pool_scale"])).then_inc(prm_loaded, 16)
            sp.dma_start(PR2[SHF:SHF + 64, :], a["state_shift"][0].rearrange("b (k p) -> (b k) p", p=P)).then_inc(prm_loaded, 16)
            sp.dma_start(CT[:, first:], a["const_table"][:, first:]).then_inc(const_loaded, 16)
            sp.dma_start(RAW[0][:, :, 0:LW], w1_v).then_inc(raw_loaded[0], 16)
            sp.dma_start(RAW[0][:, :, LW:LW + LA], a1_v).then_inc(a1_loaded, 16)
            sp_unit(sp, U_G1, g1_v)
            sp_unit(sp, U_G1M, g1_v)
            def sp_rkv(n):
                sp_unit(sp, U_RKV + n, rkv_v[n // 4, :, :, (n % 4) * UW:(n % 4 + 1) * UW])

            for n in range(8):
                sp_rkv(n)
            sp.wait_ge(hn_made, KT)
            sp.dma_start(HR[:], a["head_rows"].rearrange("n (k p) -> n k p", k=KT)).then_inc(headrow_loaded, 16)
            sp.wait_ge(xlo_made, XS_TILES)
            sp.dma_start(RST[:], a["resets"].to_broadcast([P, KT * P + KT * NS])).then_inc(resets_loaded, 16)
            for n in (8, 9):
                sp_rkv(n)
            wait_filled(sp, J_K + 7)
            sp.dma_start(W2A[0:LW, :], a["rwkv_w2"][0]).then_inc(aug_loaded, 16)
            sp.dma_start(W2A[LW:LW + 1, :], a["rwkv_w0"]).then_inc(aug_loaded, 16)
            sp.dma_start(A2A[0:LA, :], a["rwkv_a2"][0]).then_inc(aug_loaded, 16)
            sp.dma_start(A2A[LA:LA + 1, :], a["rwkv_a0"]).then_inc(aug_loaded, 16)
            for n in (10, 11):
                sp_rkv(n)
            wait_emptied(sp, J_SHO)
            store(sp, o["shift_prompt"][0], SHO[0:1, :])
            store(sp, o["shift_sample"][0], SHO[1:9, :])
            wait_filled(sp, J_STO - 1)
            for b in range(NB):
                sp.dma_start(S0L[:, b], a["state_wkv"][0, b].rearrange("h v k -> v h k")).then_inc(s0_loaded, 16)
            wait_emptied(sp, J_STO)
            store(sp, o["wkv_prompt"][0, 0].rearrange("h v k -> v h k"), STO[:].rearrange("v (h k) -> v h k", k=HD))
            wait_emptied(sp, js("GY"))
            sp.dma_start(G2A[:], a["rwkv_g2"][0, 0:P]).then_inc(g2_loaded, 16)
            sp.dma_start(G2B[:], a["rwkv_g2"][0, P:LG]).then_inc(g2_loaded, 16)
            for b in range(NB):
                wait_emptied(sp, js(f"TO{b}"))
                store(sp, o["wkv_sample"][0, b].rearrange("h v k -> v h k"), SO[:, b].rearrange("v (h k) -> v h k", k=HD))
            sp.wait_ge(out_stored, 16 * stores[0])
            for n in range(4):
                sp_unit(sp, U_WO + n, wo_v[:, :, n * UW:(n + 1) * UW])
            with sp.Fori(0, CHUNKS) as i:
                sp_ffn(sp, 0, i)
            sp_unit(sp, U_POOL, pool_v)
            wait_filled(sp, J_N2)
            sp.dma_start(PSI[0:NB * PBUF, :], a["state_pool"][0].rearrange("b t d -> (b t) d")).then_inc(pst_loaded, 16)
            for n in range(2):
                sp_unit(sp, U_F1 + n, up_v[1][:, :, 0, n * UW:(n + 1) * UW])
            wait_emptied(sp, J_PO)
            store(sp, o["pool_prompt"][0, 0], PRO[0][0:PBUF, :])
            wait_emptied(sp, J_PO + 1)
            store(sp, o["pool_sample"][0].rearrange("b t d -> (b t) d"), PRO[1][0:NB * PBUF, :])
            for q in range(2, 4):
                sp_unit(sp, U_F1 + q, up_v[1][:, :, 0, q * UW:(q + 1) * UW])
            for q in range(4):
                sp_unit(sp, U_F1 + 4 + q, dn_v[1][0, :, :, q * UW:(q + 1) * UW])
            with sp.Fori(1, CHUNKS) as i:
                sp_ffn(sp, 1, i)
            for n in range(5):
                wait_emptied(sp, jy(n))
                if n < 4:
                    store(sp, o["y_prompt"][0, n * P:(n + 1) * P, :], YO[n][:])
                else:
                    store(sp, o["y_sample"].rearrange("b t d -> (b t) d"), YO[n][0:NS, :])
            sp.wait_ge(out_stored, 16 * stores[0])

        def pe_unit(pe, u, j0, xh, xl, mtiles, ready=None, i=0, ktiles=None, begins=True, ends=True):
            pe.wait_ge(whi_made, i * FFN_U + u + 1)
            pe.wait_ge(wlo_made, i * FFN_U + u + 1)
            wh, wl = WHI[u % 2], WLO[u % 2]
            for m, (c0, w) in enumerate(mtiles):
                j = j0 + m
                if begins:
                    pe.wait_ge(emptied[(j - 4) % 4], i * (FFN_J // 2) + 2 * ((j - 4) // 4) + 2)
                ks = ktiles[m] if ktiles else [(k, k) for k in range(KT)]
                for n, (kw, kx) in enumerate(ks):
                    if ready is not None:
                        ready(pe, m, kx)
                    for wt, xt in ((wh, xh), (wh, xl), (wl, xh)):
                        for h in range(2):
                            mm = nc.tensor.matmul(bank(j, h)[0:w, 0:TH], wt[:, kw, c0:c0 + w],
                                                  xt[:, kx, h * TH:(h + 1) * TH],
                                                  start=(begins and n == 0 and wt is wh and xt is xh),
                                                  stop=(ends and n == len(ks) - 1 and wt is wl),
                                                  skip_group_check=not (begins and ends))
                if ends:
                    mm.then_inc(filled, 2)
            return mm

        def pe_transposes(pe, j, items, n=P):
            wait_free(pe, j)
            for out, in_ in items:
                k = in_.shape[0]
                mm = nc.tensor.transpose(out, in_, ident[0:k, 0:k])
            mm.then_inc(filled, 2)

        def pe_norm(pe, n, j):
            wait_free(pe, j)
            sq = DF if n == 3 else SQ
            tiles = list(enumerate(ORDER[n]))
            if n in SUMMED:
                pe.wait_ge(sq_summed, summed_by(n, SUMMED[n] - 1))
                tiles = tiles[0:1] + tiles[SUMMED[n]:]
            for i, k in tiles:
                pe.wait_ge(sq_made, KT * (n - 1) + i + 1)
                for h in range(2):
                    mm = nc.tensor.matmul(bank(j, h)[:, 0:TH], ones, sq[:, k, h * TH:(h + 1) * TH],
                                          start=(i == 0), stop=(i == KT - 1))
            mm.then_inc(filled, 2)

        DIAGONAL = ((0, 0), (1, 1), (1, 0), (0, 1))

        def settle(pe):
            pe.sem_inc(settled, 1)


        def w_square(pe, i, name, L, Rt, needs=()):
            j = jw(i, name)
            for h in range(2):
                w_free(pe, i, name)
                for need in needs:
                    need(h)
                settle(pe)
                for g in range(KT):
                    for c in range(2):
                        rows = slice(c * HD, (c + 1) * HD)
                        rhs = Rt[rows, :] if Rt is CC["I64"] else Rt[rows, h, g, :]
                        mm = nc.tensor.matmul(bank(j, h)[rows, g * HD:(g + 1) * HD], L[rows, h, g, :], rhs,
                                              start=True, stop=True)
                mm.then_inc(filled, 1)

        XT_ = FX[:, :, :, 1, :]
        FT_ = FX[:, :, :, 0, :]

        def pe_lora(pe, i, name, tok):
            wa, hid = {"wpre": (W2A, WH), "apre": (A2A, AH)}[name]
            for h in range(2):
                w_free(pe, i, name)
                for g in range(4):
                    mm = nc.tensor.matmul(bank(jw(i, name), h)[:, g * P:(g + 1) * P],
                                          wa[0:LW + 1, (4 * h + g) * P:(4 * h + g + 1) * P], hid[0:LW + 1, tok],
                                          start=True, stop=True)
                mm.then_inc(filled, 1)

        def pe_headsums(pe, i):
            j = jw(i, "norm2")
            w_free(pe, i, "norm2")
            pe.wait_ge(dve_prep, prep_count(i, DVE_PREP, "KSQ"))
            c0 = CAT["headsum"][0] + 14
            for g in range(KT):
                mm = nc.tensor.matmul(bank(j, 0)[0:NH, 0:P], CT[:, c0 - 2 * g:c0 - 2 * g + NH], WT["KSQ"][:, g, :],
                                      start=(g == 0), stop=(g == KT - 1))
            mm.then_inc(filled, 2)

        def pe_headspread(pe, i):
            j = jw(i, "norm3")
            w_free(pe, i, "norm3")
            pe.wait_ge(dve_prep, prep_count(i, DVE_PREP, "RI"))
            for g in range(KT):
                mm = nc.tensor.matmul(bank(j, g // 4)[:, (g % 4) * P:(g % 4 + 1) * P], HR[:, g, :], NRM[:],
                                      start=True, stop=True)
                if g % 4 == 3:
                    mm.then_inc(filled, 1)

        def pe_tile(pe, i, last=False):
            if not last:
                nxt = bass.ds(i * P + P, P)
            kept = lambda name: (lambda h: w_kept(pe, i, name, h))
            w_prep(pe, i, "RT")
            for q in range(4):
                j = jw(i, f"Q{q}")
                w_free(pe, i, f"Q{q}")
                settle(pe)
                for gg in range(2):
                    for c in range(2):
                        for p in range(2):
                            gc, rows = 2 * (2 * q + gg) + c, slice(p * HD, (p + 1) * HD)
                            cols = slice((2 * gg + c) * P, (2 * gg + c + 1) * P)
                            mm = nc.tensor.matmul(bank(j, p)[:, cols], BKH[rows, gc].rearrange("p x n -> p (x n)"),
                                                  AR[rows, gc].rearrange("p x n -> p (x n)"), start=True, stop=True)
                mm.then_inc(filled, 2)
            j = jw(i, "M")
            w_free(pe, i, "M")
            settle(pe)
            for g in range(KT):
                for p, c in DIAGONAL:
                    rows = slice(p * HD, (p + 1) * HD)
                    mm = nc.tensor.matmul(bank(j, p)[c * HD:(c + 1) * HD, g * HD:(g + 1) * HD],
                                          AR[rows, 2 * g + c, 0, :], BKH[rows, 2 * g + c, 0, :], start=True, stop=True)
            mm.then_inc(filled, 2)
            def turn_bk(q):
                j = jw(i, f"tb{q}")
                w_free(pe, i, f"tb{q}")
                for c in range(2):
                    for g in range(4):
                        mm = nc.tensor.transpose(bank(j, c)[:, g * P:(g + 1) * P],
                                                 BKD[:, 2 * (4 * q + g) + c].rearrange("p x n -> p (x n)"), ident)
                mm.then_inc(filled, 2)

            def turn_v(q):
                j = jw(i, f"tv{q}")
                w_free(pe, i, f"tv{q}")
                settle(pe)
                for c in range(2):
                    for g in range(4):
                        mm = nc.tensor.matmul(bank(j, c)[HD:P, g * P:(g + 1) * P],
                                              WT["VC"][:, 4 * q + g, c * HD:(c + 1) * HD], ident, start=True, stop=True)
                mm.then_inc(filled, 2)

            turn_bk(0)
            for h in range(2):
                w_free(pe, i, "bonus")
                mm = nc.tensor.matmul(bank(jw(i, "bonus"), h), bones,
                                      WT["Z"][:, 4 * h:4 * h + 4, :].rearrange("p a b -> p (a b)"), start=True, stop=True)
                mm.then_inc(filled, 1)
            w_square(pe, i, "P2", WT["P1T"], WT["P1"], [kept("Q3"), kept("M")])
            turn_bk(1)
            w_square(pe, i, "P2T", WT["P1"], WT["P1T"])
            pe.wait_ge(vc_made, i + 1)
            turn_v(0)
            w_square(pe, i, "XT2", WT["P2"], XT_, [kept("P2"), lambda h: w_sum(pe, i, "XT1" + "ab"[h])])
            turn_v(1)
            w_square(pe, i, "P4", WT["P2T"], WT["P2"], [kept("P2T")])
            w_square(pe, i, "XT3", WT["P4"], XT_, [kept("P4"), kept("XT2")])
            w_square(pe, i, "X", XT_, CC["I64"], [kept("XT3")])
            if not last:
                pe_lora(pe, i, "wpre", nxt)
                pe_lora(pe, i, "apre", nxt)
            w_square(pe, i, "F", WT["OT"], WT["X"], [kept("X")])
            w_square(pe, i, "FT", WT["X"], WT["OT"])
            w_square(pe, i, "F2", FT_, WT["F"], [kept("F"), kept("FT")])
            for h in range(2):
                name = "T1" + "ab"[h]
                j = jw(i, name)
                w_free(pe, i, name)
                settle(pe)
                for g in range(KT):
                    for c in range(2):
                        rows = slice(c * HD, (c + 1) * HD)
                        mm = nc.tensor.matmul(bank(j, g // 4)[rows, (g % 4) * P:(g % 4 + 1) * P], WT["F"][rows, h, g, :],
                                              FX[rows, h, g].rearrange("p x n -> p (x n)"), start=True, stop=True)
                    if g % 4 == 3:
                        mm.then_inc(filled, 1)
            if not last:
                pe_headsums(pe, i)
            w_square(pe, i, "T2", WT["F2"], XT_, [kept("F2"), lambda h: w_kept(pe, i, "T1" + "ab"[h], 0)])
            w_square(pe, i, "F4", WT["F2T"], WT["F2"], [lambda h: w_kept(pe, i, "T1" + "ab"[h])])
            j = jw(i, "NV")
            w_free(pe, i, "NV")
            w_kept(pe, i, "tv1")
            settle(pe)
            for g in range(KT):
                for c in range(2):
                    for p in range(2):
                        mm = nc.tensor.matmul(bank(j, p)[c * HD:(c + 1) * HD, g * HD:(g + 1) * HD],
                                              NT[HD:P, p, 2 * g + c, :],
                                              UV[HD:P, c, (2 * g + p) * HD:(2 * g + p + 1) * HD], start=True, stop=True)
            mm.then_inc(filled, 2)
            w_square(pe, i, "T3", WT["F4"], XT_, [kept("F4"), kept("T2")])
            for c in range(2):
                rows = slice(c * HD, (c + 1) * HD)
                j = jw(i, f"AS{c}")
                w_free(pe, i, f"AS{c}")
                if c == 1:
                    w_kept(pe, i, "SY0")
                settle(pe)
                for g in range(KT):
                    for p in range(2):
                        ch = slice(p * HD, (p + 1) * HD)
                        mm = nc.tensor.matmul(bank(j, p)[rows, g * HD:(g + 1) * HD], AR[ch, 2 * g + c, 0, :],
                                              ST[ch, g, :], start=True, stop=True)
                mm.then_inc(filled, 2)
                if c == 0 and not last:
                    pe_headspread(pe, i)
                j = jw(i, f"SY{c}")
                w_free(pe, i, f"SY{c}")
                settle(pe)
                for n in range(NH):
                    g, p = n // 2, n % 2
                    ch = slice(p * HD, (p + 1) * HD)
                    mm = nc.tensor.matmul(bank(j, 0)[ch, g * HD:(g + 1) * HD], ST[ch, g, :], AR[ch, 2 * g + c, 1, :],
                                          start=True, stop=True)
                mm.then_inc(ys_filled, 1)
                j = jw(i, f"U{c}")
                w_free(pe, i, f"U{c}")
                w_kept(pe, i, f"AS{c}")
                w_kept(pe, i, "T3")
                settle(pe)
                for p in range(2):
                    for g in range(KT):
                        mm = nc.tensor.matmul(bank(j, p)[0:HD, g * HD:(g + 1) * HD], FX[rows, p, g, 1, :],
                                              WT["NV"][rows, p, g, :], start=True, stop=True)
                    mm.then_inc(filled, 1)
                j = jw(i, f"SY{c}")
                for p in range(2):
                    w_kept(pe, i, f"U{c}", p)
                    settle(pe)
                    for g in range(KT):
                        vals = slice((2 * g + p) * HD, (2 * g + p + 1) * HD)
                        mm = nc.tensor.matmul(bank(j, 1)[p * HD:(p + 1) * HD, g * HD:(g + 1) * HD],
                                              BKT[:, c, vals], UV[:, c, vals], start=True, stop=True)
                mm.then_inc(filled, 2)
            j = jw(i, "YU")
            w_free(pe, i, "YU")
            settle(pe)
            for g in range(KT):
                for c in range(2):
                    for p in range(2):
                        n = 2 * g + p
                        mm = nc.tensor.matmul(bank(j, c)[p * HD:(p + 1) * HD, g * HD:(g + 1) * HD],
                                              UV[:, c, n * HD:(n + 1) * HD], RBK[:, p, 2 * g + c, :], start=True, stop=True)
            mm.then_inc(filled, 2)

        def pe_samples(pe):
            t0 = SEQ
            for name, wa, hid in (("wpre", W2A, WH), ("apre", A2A, AH)):
                wait_free(pe, js(name))
                for g in range(KT):
                    mm = nc.tensor.matmul(bank(js(name), 0)[:, g * NS:(g + 1) * NS], wa[0:LW + 1, g * P:(g + 1) * P],
                                          hid[0:LW + 1, t0:t0 + NS], start=True, stop=True)
                mm.then_inc(filled, 2)

            def pairsum(name, src):
                wait_free(pe, js(name))
                nc.tensor.matmul(bank(js(name), 0)[:, 0:KT * NS], bones, src[:].rearrange("p a b -> p (a b)"),
                                 start=True, stop=True).then_inc(filled, 2)

            def square(name, L, Rt):
                wait_free(pe, js(name))
                for n in range(NH):
                    g, p = n // 2, n % 2
                    mm = nc.tensor.matmul(bank(js(name), p)[0:NS, g * NS:(g + 1) * NS], L[0:NS, p, g, :],
                                          Rt[0:NS, p, g, :], start=True, stop=True)
                mm.then_inc(filled, 2)

            s_dve(pe, "KSQ")
            pairsum("norm2", SM["KSQ"])
            for q in range(4):
                j = js(f"s0t{q}")
                if q == 0:
                    pe.wait_ge(s0_loaded, 16 * NB)
                pe_transposes(pe, j, [(bank(j, bb)[:, g * HD:(g + 1) * HD],
                                       S0L[:, 2 * q + bb, 2 * g:2 * g + 2, :].rearrange("v h k -> v (h k)"))
                                      for bb in range(2) for g in range(KT)])
            s_dve(pe, "RT")
            j = js("Q")
            wait_free(pe, j)
            for n in range(NH):
                g, p = n // 2, n % 2
                ch = slice(p * HD, (p + 1) * HD)
                mm = nc.tensor.matmul(bank(j, p)[0:2 * NS, g * 2 * NS:(g + 1) * 2 * NS],
                                      SM["BKH"][ch, g].rearrange("p x n -> p (x n)"),
                                      SM["AR"][ch, g].rearrange("p x n -> p (x n)"), start=True, stop=True)
            mm.then_inc(filled, 2)
            j = js("M")
            wait_free(pe, j)
            for n in range(NH):
                g, p = n // 2, n % 2
                ch = slice(p * HD, (p + 1) * HD)
                mm = nc.tensor.matmul(bank(j, p)[0:NS, g * NS:(g + 1) * NS], SM["AT"][ch, g, :], SM["BH"][ch, g, :],
                                      start=True, stop=True)
            mm.then_inc(filled, 2)
            wait_emptied(pe, js("Q"))
            wait_emptied(pe, js("M"))
            square("P2", SM["P1T"], SM["P1"])
            s_dve(pe, "KD")
            j = js("tBK")
            pe_transposes(pe, j, [(bank(j, g // 4)[0:2 * NS, (g % 4) * P:(g % 4 + 1) * P],
                                   SM["BKD"][:, g].rearrange("p x n -> p (x n)")) for g in range(KT)])
            wait_emptied(pe, js("P2"))
            s_dve(pe, "XT1")
            square("XT2", SM["P2"], SM["XT"])
            j = js("tV")
            wait_free(pe, j)
            for g in range(KT):
                mm = nc.tensor.matmul(bank(j, g // 4)[NS:2 * NS, (g % 4) * P:(g % 4 + 1) * P], V[:, g, SEQ:T], ident,
                                      start=True, stop=True)
            mm.then_inc(filled, 2)
            s_dve(pe, "ZR")
            pairsum("bonus", SM["Z"])
            j = js("GY")
            wait_free(pe, j)
            wait_emptied(pe, js("tV"))
            wait_emptied(pe, js("s0t3"))
            for n in range(NH):
                g, p = n // 2, n % 2
                mm = nc.tensor.matmul(bank(j, 1)[p * HD:(p + 1) * HD, g * NS:(g + 1) * NS],
                                      SM["UV"][NS:2 * NS, n * HD:(n + 1) * HD], SM["NT"][NS:2 * NS, p, g, :],
                                      start=True, stop=True)
            for g in range(KT):
                for b in range(NB):
                    for p in range(2):
                        ch = slice(p * HD, (p + 1) * HD)
                        out = bank(j, 0)[ch].rearrange("p (x a n) -> p x a n", x=2, a=KT)
                        mm = nc.tensor.matmul(out[:, :, g, b * DS:(b + 1) * DS], S0T[ch, b, g, :],
                                              SM["AR"][ch, g, :, b * DS:(b + 1) * DS], start=True, stop=True)
            mm.then_inc(filled, 2)
            wait_emptied(pe, j)
            j = js("tG")
            pe_transposes(pe, j, [(bank(j, g // 4)[0:NS, (g % 4) * P:(g % 4 + 1) * P], SM["GT"][:, g, :])
                                  for g in range(KT)])
            j = js("U")
            wait_free(pe, j)
            wait_emptied(pe, js("tG"))
            wait_emptied(pe, js("XT2"))
            for n in range(NH):
                g, p = n // 2, n % 2
                mm = nc.tensor.matmul(bank(j, p)[0:NS, g * HD:(g + 1) * HD], SM["XT"][0:NS, p, g, :],
                                      SM["G"][:, n * HD:(n + 1) * HD], start=True, stop=True)
            mm.then_inc(filled, 2)
            j = js("YU")
            wait_free(pe, j)
            wait_emptied(pe, js("U"))
            for n in range(NH):
                g, p = n // 2, n % 2
                mm = nc.tensor.matmul(bank(j, 0)[p * HD:(p + 1) * HD, g * NS:(g + 1) * NS],
                                      SM["UV"][:, n * HD:(n + 1) * HD], SM["RBK"][:, p, g, :], start=True, stop=True)
            mm.then_inc(filled, 2)

            def sums(q):
                j = js(f"SS{q}")
                wait_free(pe, j)
                s_act(pe, f"UM{q}")
                for n in range(NH):
                    g, p = n // 2, n % 2
                    vals = slice(n * HD, (n + 1) * HD)
                    mm = nc.tensor.matmul(bank(j, g // 4)[p * HD:(p + 1) * HD, (g % 4) * P:(g % 4 + 1) * P],
                                          SM["BKT"][:, vals], UVM[q % 2][:, :, vals], start=True, stop=True)
                mm.then_inc(filled, 2)

            def out_rows(b):
                j = js(f"TO{b}")
                wait_emptied(pe, js(f"SS{b // 2}"))
                pe_transposes(pe, j, [(bank(j, g // 4)[0:HD, (g % 4) * P:(g % 4 + 1) * P], S0T[:, b, g, :])
                                      for g in range(KT)])

            for q in range(4):
                sums(q)
                if q:
                    out_rows(2 * q - 2)
                    out_rows(2 * q - 1)
            out_rows(NB - 2)
            out_rows(NB - 1)

        def pe_ffn(pe, l, i):
            u0, j0 = ((U_F0, J_F0), (U_F1, J_F1))[l]
            nn = (1, 3)[l]
            first = lambda pe, m, k: pe.wait_ge(xlo_made, xlo_at(nn, k))
            for q in range(4):
                pe_unit(pe, u0 + q, j0 + 2 * q, XSH[0], XSL[0], ((0, P), (P, P)), first if q == 0 else None, i,
                        [[(k, k) for k in ORDER[nn]]] * 2)
            hid = lambda pe, m, k: pe.wait_ge(hlo_made, i * KT + (KT * CHUNKS * l + k + 1))
            for q in range(4):
                pe_unit(pe, u0 + 4 + q, j0 + 8 + 2 * q, HH, HL, ((0, P), (P, P)), hid if q == 0 else None, i)

        def xlo_at(n, k):
            return XS_TILES + KT * {1: 0, 3: 1}[n] + ORDER[n].index(k) + 1

        def run_pe(pe):
            pe.wait_ge(const_loaded, 16)
            for n in range(5):
                pe.wait_ge(x_loaded[n], 16)
                j, w = J_X + n, P if n < 4 else NS
                pe_transposes(pe, j, [(bank(j, k // 4)[:, (k % 4) * w:(k % 4 + 1) * w], XIN[0:w, n, k * P:(k + 1) * P])
                                      for k in range(KT)])
            pe.wait_ge(prm_loaded, 16 * 11)
            pe_transposes(pe, J_PRM, [(bank(J_PRM, 0)[:, 0:P], PR[:]), (bank(J_PRM, 1)[:, 0:72], PR2[:])])
            wait_free(pe, J_N0)
            pe.wait_ge(diag_made, 5)
            for n in range(5):
                w = P if n < 4 else NS
                mm = nc.tensor.matmul(bank(J_N0, n // 4)[:, (n % 4) * P:(n % 4) * P + w], ones[0:w, :], DG0[0:w, n, 0:w],
                                      start=True, stop=True)
            mm.then_inc(filled, 2)
            pe.wait_ge(const_loaded, 32)
            ready_h = lambda pe, m, k: pe.wait_ge(xlo_made, k + 1)
            ready_dx = lambda pe, m, k: pe.wait_ge(xlo_made, KT + k + 1)
            gate = ((0, P), (P, LG - P))
            pe_unit(pe, U_WA, J_WA, XSH[0], XSL[0], ((0, LW + LA),), ready_h, ends=False)
            pe_unit(pe, U_G1, J_G1, XSH[0], XSL[0], gate, ends=False).then_inc(plain_used, 1)
            pe_unit(pe, U_WA, J_WA, XSH[1], XSL[1], ((LW + LA, LW + LA),), ready_dx, begins=False)
            pe_unit(pe, U_G1M, J_G1, XSH[1], XSL[1], gate, begins=False)
            for n in range(12):
                jx = 2 + n // 4
                ready = lambda pe, m, k, jx=jx: pe.wait_ge(xlo_made, KT * jx + k + 1)
                pe_unit(pe, U_RKV + n, J_R + 2 * n if n < 8 else jv(f"V{2 * n - 16}"), XSH[jx % 2], XSL[jx % 2],
                        ((0, P), (P, P)), ready if n % 4 == 0 else None)
                if n == 9:
                    pe.wait_ge(aug_loaded, 64)
                    pe.wait_ge(pads_made, 6)
                    for name in ("wpre", "apre"):
                        pe_lora(pe, None, name, slice(0, P))
                    pe_headsums(pe, None)
                if n == 10:
                    pe.wait_ge(headrow_loaded, 16)
                    pe_headspread(pe, None)
            pe.wait_ge(sht_made, 1)
            pe_transposes(pe, J_SHO, [(bank(J_SHO, k // 4)[0:9, (k % 4) * P:(k % 4 + 1) * P], SHT[:, k, :])
                                      for k in range(KT)])
            pe.wait_ge(gsig_made, 2)
            with pe.Fori(0, TILES - 1) as i:
                pe_tile(pe, i)
            pe_tile(pe, TILES - 1, last=True)
            wait_emptied(pe, J_STO - 2)
            pe_transposes(pe, J_STO, [(bank(J_STO, g // 4)[0:HD, (g % 4) * P:(g % 4 + 1) * P], ST[:, g, :])
                                      for g in range(KT)])
            pe_samples(pe)
            c0 = CAT["headsum"][0] + 14
            for what, k in GN_JOBS:
                j = jg(what, k)
                wait_free(pe, j)
                if what == "var":
                    for kk in range(KT):
                        pe.wait_ge(gn_squared, kk + 1)
                        for h in range(2):
                            mm = nc.tensor.matmul(bank(j, h)[0:NH, 0:TH], CT[:, c0 - 2 * kk:c0 - 2 * kk + NH],
                                                  GQ[:, kk, h * TH:(h + 1) * TH], start=(kk == 0), stop=(kk == KT - 1))
                    mm.then_inc(filled, 2)
                    continue
                if (what, k) == ("gate", 0):
                    pe.wait_ge(g2_loaded, 32)
                if what == "spread":
                    pe.wait_ge(gn_rstd, 1)
                for h in range(2):
                    cols = slice(h * TH, (h + 1) * TH)
                    out = bank(j, h)[:, 0:TH]
                    if what == "mean":
                        mm = nc.tensor.matmul(out, bmean, R[:, k, cols], start=True, stop=True)
                    elif what == "spread":
                        mm = nc.tensor.matmul(out, HR[:, k, :], GR[:, cols], start=True, stop=True)
                    else:
                        nc.tensor.matmul(out, G2A[:, k * P:(k + 1) * P], GH[:, 0, cols], start=True, stop=False)
                        mm = nc.tensor.matmul(out, G2B[:, k * P:(k + 1) * P], GH[0:LG - P, 1, cols],
                                              start=False, stop=True)
                mm.then_inc(filled, 2)
            ready = lambda pe, m, k: pe.wait_ge(gn_lo, k + 1)
            for n in range(4):
                pe_unit(pe, U_WO + n, J_WO + 2 * n, XSH[1], XSL[1], ((0, P), (P, P)), ready if n == 0 else None)
            pe_norm(pe, 1, J_N1)
            with pe.Fori(0, CHUNKS) as i:
                pe_ffn(pe, 0, i)
            pe_norm(pe, 2, J_N2)
            pe.wait_ge(pst_loaded, 16)
            pe_transposes(pe, J_PST, [(bank(J_PST, k // 4)[:, (k % 4) * 120:(k % 4 + 1) * 120],
                                       PSI[0:120, k * P:(k + 1) * P]) for k in range(KT)])

            def pool_products(first, n):
                pe.wait_ge(whi_made, U_POOL + 1)
                pe.wait_ge(wlo_made, U_POOL + 1)
                for i in range(first, first + n):
                    m = POOL_ORDER[i]
                    j, c0 = jpw(m), P * (m % 2)
                    wait_free(pe, j)
                    for k in (m & ~1, m | 1):
                        pe.wait_ge(pool_diff, POOL_ORDER.index(k) + 1)
                        for h in range(2):
                            mm = nc.tensor.matmul(bank(j, h)[:, 0:TH], WPL[:, k, c0:c0 + P],
                                                  DF[:, k, h * TH:(h + 1) * TH], start=(k % 2 == 0), stop=(k % 2 == 1))
                    mm.then_inc(filled, 2)

            pool_products(0, 6)
            pe.wait_ge(hn_made, 2 * KT)
            pe_transposes(pe, J_PO, [(bank(J_PO, k // 4)[0:PBUF, (k % 4) * P:(k % 4 + 1) * P],
                                      EXT[:, k, SEQ:SEQ + PBUF]) for k in range(KT)])
            pe.wait_ge(pool_cols, KT)
            pe_transposes(pe, J_PO + 1, [(bank(J_PO + 1, k // 4)[0:120, (k % 4) * P:(k % 4 + 1) * P],
                                          PCO[:, k].rearrange("p b t -> p (b t)")) for k in range(KT)])
            pool_products(6, 2)
            pe_norm(pe, 3, J_N3)
            with pe.Fori(0, CHUNKS) as i:
                pe_ffn(pe, 1, i)
            pe_norm(pe, 4, J_N4)
            pe.wait_ge(xhi_made, XS_TILES + 3 * KT)
            for n in range(5):
                j, w = jy(n), P if n < 4 else NS
                pe_transposes(pe, j, [(bank(j, k // 4)[0:w, (k % 4) * P:(k % 4 + 1) * P], HN[:, k, n * P:n * P + w])
                                      for k in range(KT)])
                if n == 0:
                    wait_emptied(pe, J_N4)
                    wait_free(pe, J_YT)
                    for i in range(5):
                        w = P if i < 4 else NS
                        mm = nc.tensor.matmul(bank(J_YT, 0)[0:w, i:i + 1], RS1[0:1, i * P:i * P + w], ones[0:1, 0:1],
                                              start=True, stop=True)
                    mm.then_inc(filled, 2)

        def timeline():
            xs = lambda a, b: [("xs", n) for n in range(a, b)]
            steps = (xs(0, 6) + [("split", U_G1)] + xs(6, 20)
                     + [("split", U_G1M), ("out", J_WA), ("split", U_RKV)] + xs(20, 24) + [("out", J_G1), ("out", J_G1 + 1)])
            for n in range(12):
                if n < 11:
                    steps += [("split", U_RKV + n + 1)]
                if n < 4:
                    steps += xs(24 + 2 * n, 26 + 2 * n)
                elif n < 6:
                    steps += xs(16 + 4 * n, 20 + 4 * n)
                if n == 5:
                    steps += [("out", J_K), ("out", J_K + 1)]
                if n == 10:
                    steps += [("first", "exps"), ("first", "root")]
                if n >= 8:
                    steps += [("out", jv(f"V{2 * n - 16}")), ("out", jv(f"V{2 * n - 15}"))]
                elif n != 4:
                    steps += [("out", J_R + 2 * n), ("out", J_R + 2 * n + 1)]
                if n in (8, 9, 10):
                    steps += [("first", ("squares", "lora", "late")[n - 8])]
            return steps

        def wait_split(eng, u, i=0):
            eng.wait_ge(raw_loaded[u % 2], i * (16 * FFN_U // 2) + 16 * (u // 2 + 1))
            if u == U_RKV:
                eng.wait_ge(plain_used, 1)
            elif u >= 2:
                j = {U_F0 + 1: J_F0 - 1, U_F1 + 1: J_F1 - 1}.get(u, last_job(u - 2))
                eng.wait_ge(filled, i * (2 * FFN_J) + 2 * j + 2)

        act = nc.scalar.activation

        def act_split(eng, u, i=0):
            w = unit_width(u)
            if u in (U_WA, U_G1M):
                eng.wait_ge(scaled_made, u // 2 + 1)
            wait_split(eng, u, i)
            if isinstance(i, int) and u + i * FFN_U == U_POOL:
                act(WPL[:, 0:4], RAW[u % 2][:, 0:4], ACT.Copy).then_inc(whi_made, 1)
                return
            act(WHI[u % 2][:, :, 0:w], RAW[u % 2][:, :, 0:w], ACT.Copy).then_inc(whi_made, 1)

        def act_copy_out(eng, j, dst, src, func=ACT.Copy, scale=1.0):
            wait_filled(eng, j)
            act(dst, src, func, scale=scale).then_inc(emptied[j % 4], 2)

        def act_lora(eng, i, name):
            j = jw(i, name)
            dst = WT[{"wpre": "TW", "apre": "TA"}[name]]
            for h in range(2):
                w_filled(eng, i, name, h)
                act(dst[:, 4 * h:4 * h + 4, :].rearrange("p a b -> p (a b)"), bank(j, h), ACT.Tanh, scale=0.5)\
                    .then_inc(emptied[j % 4], 1)

        def act_exps(eng, i):
            eng.wait_ge(dve_prep, prep_count(i, DVE_PREP, "CS"))
            act(WT["EL"][:], WT["CS"][:], ACT.Exp, scale=-DECAY).then_inc(act_prep, 1)
            eng.wait_ge(dve_prep, prep_count(i, DVE_PREP, "CX"))
            act(WT["EN"][:], WT["CS"][:], ACT.Exp, scale=DECAY).then_inc(act_prep, 1)

        def act_exp_before(eng):
            act(WT["EX"][:], WT["CX"][:], ACT.Exp, scale=-DECAY).then_inc(act_prep, 1)

        def act_root_heads(eng, i):
            w_kept(eng, i, "norm2")
            act(NRM[:], NRM[:], ACT.Sqrt).then_inc(act_prep, 1)

        def act_tile(eng, i, last=False):
            tok0 = i * P
            act(WT["VC"][:], V[:, :, bass.ds(tok0, P)], ACT.Copy).then_inc(vc_made, 1)

            def mats(name, T4=None):
                T4 = WT[name][:] if T4 is None else T4
                j = jw(i, name)
                for h in range(2):
                    w_filled(eng, i, name, h)
                    act(T4[:, h], bank(j, h).rearrange("p (a b) -> p a b", a=KT), ACT.Copy).then_inc(emptied[j % 4], 1)

            def turned(name, dst, rows=slice(0, P)):
                j = jw(i, name)
                w_filled(eng, i, name)
                act(dst, both(j)[rows], ACT.Copy).then_inc(emptied[j % 4], 2)

            turned("tb0", BKT[:, :, 0:512])
            mats("P2")
            turned("tb1", BKT[:, :, 512:1024])
            mats("P2T")
            turned("tv0", UV[HD:P, :, 0:512], slice(HD, P))
            turned("tv1", UV[HD:P, :, 512:1024], slice(HD, P))
            mats("P4")
            mats("X")
            if not last:
                act_lora(eng, i, "wpre")
                act_lora(eng, i, "apre")
            mats("F")
            mats("FT", FT_)
            if not last:
                act_exps(eng, i)
                act_exp_before(eng)
            mats("F2")
            for h in range(2):
                j = jw(i, "T1" + "ab"[h])
                w_kept(eng, i, "T1" + "ab"[h], 0)
                act(WT["F2T"][:, h].rearrange("p (b a) n -> p b a n", b=2),
                    both(j).rearrange("p b (a x) -> p b a x", a=4)[:, :, :, 0:HD], ACT.Copy).then_inc(emptied[j % 4], 1)
            mats("F4")
            mats("NV")
            if not last:
                act_root_heads(eng, i)
            for c in range(2):
                eng.wait_ge(ys_filled, 2 * i + c + 1)
                act(R[:, :, bass.ds(tok0 + c * HD, HD)],
                    bank(jw(i, f"SY{c}"), 0).rearrange("p (a b) -> p a b", a=KT), ACT.Copy)\
                    .then_inc(emptied[jw(i, f"SY{c}") % 4], 1)
                j = jw(i, f"U{c}")
                for p in range(2):
                    w_filled(eng, i, f"U{c}", p)
                    act(UV[0:HD, c].rearrange("s (g p v) -> s p g v", g=KT, p=2)[:, p],
                        bank(j, p)[0:HD].rearrange("s (g v) -> s g v", g=KT), ACT.Copy).then_inc(emptied[j % 4], 1)

        def act_samples(eng):
            s8 = lambda j: bank(j, 0)[:, 0:KT * NS].rearrange("p (a b) -> p a b", a=KT)
            act_copy_out(eng, js("wpre"), SM["TW"][:], s8(js("wpre")), ACT.Tanh, 0.5)
            act_copy_out(eng, js("apre"), SM["TA"][:], s8(js("apre")), ACT.Tanh, 0.5)
            wait_emptied(eng, js("norm2"))
            act(SM["NR"][:], SM["NR"][:], ACT.Sqrt).then_inc(smp_act, 1)
            s_dve(eng, "CS")
            act(SM["EL"][:], SM["CS"][:], ACT.Exp, scale=-DECAY).then_inc(smp_act, 1)
            act(SM["EN"][:], SM["CS"][:], ACT.Exp, scale=DECAY).then_inc(smp_act, 1)
            s_dve(eng, "CX")
            act(SM["EX"][:], SM["CX"][:], ACT.Exp, scale=-DECAY).then_inc(smp_act, 1)
            for q in range(4):
                if q == 0:
                    s_dve(eng, "KP")
                act_copy_out(eng, js(f"s0t{q}"), S0T[:, 2 * q:2 * q + 2].rearrange("p b g v -> p b (g v)"), both(js(f"s0t{q}")))
            rows2 = lambda T2: T2.rearrange("p (e n) -> p e n", e=2)
            j = js("P2")
            act_copy_out(eng, j, SM["P2"][0:NS].rearrange("p e a b -> p e (a b)"), both(j, KT * NS)[0:NS])
            act_copy_out(eng, js("tBK"), rows2(SM["BKT"][:]), both(js("tBK"))[0:2 * NS])
            act_copy_out(eng, js("tV"), rows2(SM["UV"][NS:2 * NS]), both(js("tV"))[NS:2 * NS])
            j = js("GY")
            wait_filled(eng, j)
            act(SM["GT"][:], bank(j, 1)[:, 0:KT * NS].rearrange("p (a b) -> p a b", a=KT), ACT.Copy).then_inc(emptied[j % 4], 1)
            act_copy_out(eng, js("tG"), rows2(SM["G"][:]), both(js("tG"))[0:NS])
            j = js("U")
            act_copy_out(eng, j, SM["UV"][0:NS].rearrange("s (g p v) -> s p g v", g=KT, p=2),
                         both(j)[0:NS].rearrange("s p (g v) -> s p g v", g=KT))

            def masked_uv(q):
                if q == 0:
                    wait_emptied(eng, js("U"))
                if q >= 2:
                    wait_filled(eng, js(f"SS{q - 2}"))
                for bb in range(2):
                    ins = act(UVM[q % 2][:, bb, :], SM["UV"][:], ACT.Copy, scale=CC["SB"][0:2 * NS, 2 * q + bb:2 * q + bb + 1])
                ins.then_inc(smp_act, 1)

            for q in range(4):
                masked_uv(q)
            for b in range(NB):
                act_copy_out(eng, js(f"TO{b}"), rows2(SO[:, b]), both(js(f"TO{b}"))[0:HD])

        def act_ffn(eng, l, i, last, final=None):
            u0, j0 = ((U_F0, J_F0), (U_F1, J_F1))[l]
            h0 = KT * CHUNKS * l
            for q in range(8):
                if not (last and q == 7):
                    act_split(eng, u0 + q + 1, i)
                if final and q > 4:
                    final(2 * q - 10)
                    final(2 * q - 9)
                for m in (2 * q, 2 * q + 1):
                    if q < 4:
                        j = j0 + m
                        eng.wait_ge(emptied[j % 4], i * (FFN_J // 2) + 2 * (j // 4) + 2)
                        if m >= 2:
                            eng.wait_ge(hlo_made, i * KT + (h0 + m - 1))
                        act(QL[:, m % 2, :], RL[:, m % 2, :], ACT.Square).then_inc(square_made, 1)
                        if m >= 1:
                            act_hidden_hi(eng, i, h0, m - 1)
                if q == 3:
                    act_hidden_hi(eng, i, h0, 7)

        def act_hidden_hi(eng, i, h0, m):
            eng.wait_ge(square_made, i * KT + (h0 + m + 1))
            act(HH[:, m, :], QL[:, m % 2, :], ACT.Copy).then_inc(hhi_made, 1)

        def run_act(eng):
            eng.wait_ge(const_loaded, 16)
            for n in range(5):
                w = P if n < 4 else NS
                eng.wait_ge(x_loaded[n], 16)
                act(SQR[0:w, n, :], XIN[0:w, n, :], ACT.Square, accum_out=SS[0:w, n:n + 1]).then_inc(ss_made, 1)
            wait_filled(eng, J_PRM)
            act(PRM[:], bank(J_PRM, 0)[:, 0:P], ACT.Copy).then_inc(emptied[J_PRM % 4], 1)
            act(PRM2[:], bank(J_PRM, 1)[:, 0:72], ACT.Copy).then_inc(emptied[J_PRM % 4], 1)
            eng.wait_ge(ss_made, 5)
            act(SS[:, 0:4], SS[:, 0:4], ACT.Sqrt, bias=CC["eps"][:, 0:1], scale=1.0 / D)
            act(SS[0:NS, 4:5], SS[0:NS, 4:5], ACT.Sqrt, bias=CC["eps"][0:NS, 0:1], scale=1.0 / D).then_inc(ss_made, 1)
            act_split(eng, U_WA)
            wait_filled(eng, J_N0)
            act(RS0[:, 0:SEQ], bank(J_N0, 0), ACT.Copy).then_inc(emptied[J_N0 % 4], 1)
            act(RS0[:, SEQ:T], bank(J_N0, 1)[:, 0:NS], ACT.Copy).then_inc(emptied[J_N0 % 4], 1)

            def shifted_hi(n):
                jx, k = n // 8, n % 8
                if k == 0 and jx == 2:
                    eng.wait_ge(plain_used, 1)
                elif k == 0 and jx > 2:
                    wait_filled(eng, (J_G1 + 1, J_R + 7)[jx - 3])
                dst = XSH[jx % 2][:, k, :]
                if jx == 0:
                    eng.wait_ge(hn_made, k + 1)
                    act(dst[:, 0:SEQ], H[:, k, 1:513], ACT.Copy)
                    act(samples(dst[:, SEQ:T], 0, DS), samples(H[:, k, 513:553], 1, DS), ACT.Copy).then_inc(xhi_made, 1)
                    return
                if jx == 1:
                    eng.wait_ge(dx_made, k + 1)
                else:
                    eng.wait_ge(xf_made, n - 2 * KT + 1)
                act(dst, DX[:, k, :] if jx == 1 else XF[:, n % 2, :], ACT.Copy).then_inc(xhi_made, 1)

            for what, n in timeline():
                if what == "split":
                    act_split(eng, n)
                elif what == "xs":
                    shifted_hi(n)
                elif what == "first":
                    if n == "lora":
                        act_lora(eng, None, "wpre")
                        act_lora(eng, None, "apre")
                    elif n == "exps":
                        act_exps(eng, None)
                    elif n == "root":
                        act_root_heads(eng, None)
                    elif n == "late":
                        act_exp_before(eng)
                elif n == J_WA:
                    wait_filled(eng, n)
                    act(halves(WH[0:LW, :]), both(n, TH)[0:LW], ACT.Tanh).then_inc(emptied[n % 4], 1)
                    act(halves(AH[0:LA, :]), both(n, TH)[LW:LW + LA], ACT.Copy).then_inc(emptied[n % 4], 1)
                elif n == J_G1:
                    act_copy_out(eng, n, halves(GH[:, 0, :]), both(n, TH), ACT.Tanh, 0.5)
                elif n == J_G1 + 1:
                    act_copy_out(eng, n, halves(GH[0:LG - P, 1, :]), both(n, TH)[0:LG - P], ACT.Tanh, 0.5)
                else:
                    m = n - J_R if n < J_V else 16 + int(V_SEQ[n - J_V][1])
                    if m == 8:
                        eng.wait_ge(xf_made, 3 * KT)
                    if m == 16:
                        eng.wait_ge(sht_made, 1)
                    act_copy_out(eng, n, halves((R, K, V)[m // 8][:, m % 8, :]), both(n, TH))
            act_copy_out(eng, J_SHO, SHO[:].rearrange("p (e n) -> p e n", e=2), both(J_SHO)[0:9])
            eng.wait_ge(out_stored, 32)
            with eng.Fori(0, TILES - 1) as i:
                act_tile(eng, i)
            act_tile(eng, TILES - 1, last=True)
            act_copy_out(eng, J_STO, STO[:].rearrange("p (e n) -> p e n", e=2), both(J_STO)[0:HD])
            act_samples(eng)
            for k in range(KT):
                wait_emptied(eng, jg("mean", k))
                act(GQ[:, k, :], R[:, k, :], ACT.Square).then_inc(gn_squared, 1)
            for k in range(4):
                act_copy_out(eng, jg("gate", k), halves(GG[:, k, :]), both(jg("gate", k), TH))
            act_split(eng, U_WO)
            j = jg("var", 0)
            wait_filled(eng, j)
            act(halves(GR[:]), both(j, TH)[0:NH], ACT.Sqrt, bias=CC["eps"][0:NH, 1:2], scale=1.0 / HD)\
                .then_inc(emptied[j % 4], 2)
            for k in range(4, KT):
                act_copy_out(eng, jg("gate", k), halves(GG[:, k, :]), both(jg("gate", k), TH))
            for k in range(KT):
                eng.wait_ge(gn_gated, k + 1)
                act(XSH[1][:, k, :], R[:, k, :], ACT.Copy).then_inc(gn_hi, 1)
            for n in range(4):
                act_split(eng, U_WO + n + 1)
                for k in (2 * n - 2, 2 * n - 1) if n else ():
                    act_gained(eng, k, NFFN, lambda k: wait_emptied(eng, J_WO + k))
            for k in (6, 7):
                act_gained(eng, k, NFFN, lambda k: wait_emptied(eng, J_WO + k))
            act_root(eng, J_N1)
            with eng.Fori(0, CHUNKS - 1) as i:
                act_ffn(eng, 0, i, False)

            def final_ffn0(k):
                wait_emptied(eng, J_N2 - KT + k)
                act(SQ[:, k, :], X[:, k, :], ACT.Square).then_inc(sq_made, 1)

            act_ffn(eng, 0, CHUNKS - 1, False, final_ffn0)
            final_ffn0(6)
            final_ffn0(7)
            act_root(eng, J_N2)
            wait_filled(eng, J_PST)
            for k in range(KT):
                ins = act(samples(EXT[:, k, S0_:], 0, PBUF),
                          bank(J_PST, k // 4)[:, (k % 4) * 120:(k % 4 + 1) * 120].rearrange("p (b t) -> p b t", b=NB),
                          ACT.Copy)
                if k % 4 == 3:
                    ins.then_inc(emptied[J_PST % 4], 1)
            wait_emptied(eng, J_PST)
            for i, k in enumerate(POOL_ORDER):
                eng.wait_ge(hn_made, KT + i + 1)
                act(PCO[:, k], samples(EXT[:, k, S0_:], DS, PBUF), ACT.Copy).then_inc(pool_cols, 1)

            def summed(k):
                wait_emptied(eng, jpw(k))
                wait_filled(eng, jpw(k | 1))

            act_split(eng, U_F1)
            for k in POOL_ORDER[0:4]:
                act_gained(eng, k, NFFN + 8, summed, DF)
            act_copy_out(eng, J_PO, PRO[0][0:PBUF, :].rearrange("p (e n) -> p e n", e=2), both(J_PO)[0:PBUF])
            act_copy_out(eng, J_PO + 1, PRO[1][0:120, :].rearrange("p (e n) -> p e n", e=2), both(J_PO + 1)[0:120])
            for k in POOL_ORDER[4:]:
                act_gained(eng, k, NFFN + 8, summed, DF)
            act_root(eng, J_N3)
            with eng.Fori(0, CHUNKS - 1) as i:
                act_ffn(eng, 1, i, False)

            def final_ffn1(k):
                wait_emptied(eng, J_N4 - KT + k)
                act(SQ[:, k, :], X[:, k, :], ACT.Square).then_inc(sq_made, 1)
                act(HN[:, k, :], X[:, k, :], ACT.Copy, scale=col(NFIN + k)).then_inc(xhi_made, 1)

            act_ffn(eng, 1, CHUNKS - 1, True, final_ffn1)
            final_ffn1(6)
            final_ffn1(7)
            act_root(eng, J_N4)
            wait_emptied(eng, J_YT)
            for n in range(5):
                w = P if n < 4 else NS
                act_copy_out(eng, jy(n), YO[n][0:w, :].rearrange("p (e n) -> p e n", e=2), both(jy(n))[0:w], ACT.Copy,
                             YR[0:w, n:n + 1])


        def act_gained(eng, k, gcol, ready, sq=SQ):
            ready(k)
            act(sq[:, k, :], X[:, k, :], ACT.Square).then_inc(sq_made, 1)
            act(XSH[0][:, k, :], X[:, k, :], ACT.Copy, scale=col(gcol + k)).then_inc(xhi_made, 1)

        def act_root(eng, j):
            wait_filled(eng, j)
            act(halves(RS1[:]), both(j, TH), ACT.Sqrt, bias=CC["eps"][:, 0:1], scale=1.0 / D).then_inc(emptied[j % 4], 2)

        tt, ts, stt = nc.vector.tensor_tensor, nc.vector.tensor_scalar, nc.vector.scalar_tensor_tensor

        def dve_split(eng, u, i=0):
            eng.wait_ge(raw_loaded[u % 2], i * (16 * FFN_U // 2) + 16 * (u // 2 + 1))
            w = unit_width(u)
            b = u % 2
            if u == U_G1M:
                tt(RAW[0][:, :, 0:w], RAW[0][:, :, 0:w], spread(PRM[:, MIX + 40:MIX + 40 + KT], w), MUL)\
                    .then_inc(scaled_made, 1)
            eng.wait_ge(whi_made, i * FFN_U + u + 1)
            if isinstance(i, int) and u + i * FFN_U == U_POOL:
                wait_split(eng, u, i)
                nc.vector.tensor_copy(WPL[:, 4:8], RAW[b][:, 4:8]).then_inc(wlo_made, 1)
                return
            tt(WLO[b][:, :, 0:w], RAW[b][:, :, 0:w], WHI[b][:, :, 0:w].bitcast(F32), SUB).then_inc(wlo_made, 1)

        samples = lambda ap, lo, n: ap.rearrange("p (b t) -> p b t", b=NB)[:, :, lo:lo + n]

        def dve_gained_lo(eng, n, k, gcol):
            eng.wait_ge(xhi_made, xlo_at(n, k))
            stt(XSL[0][:, k, :], X[:, k, :], col(gcol + k), XSH[0][:, k, :].bitcast(F32), MUL, SUB).then_inc(xlo_made, 1)

        def dve_add_square(eng, n, k):
            if k not in range(1, SUMMED[n]):
                return
            eng.wait_ge(sq_made, KT * (n - 1) + k + 1)
            if k > 1:
                eng.wait_ge(sq_summed, summed_by(n, k - 1))
            tt(SQ[:, 0, :], SQ[:, 0, :], SQ[:, k, :], ADD).then_inc(sq_summed, 1)

        def dve_rstd(eng, n, j):
            wait_emptied(eng, j)
            nc.vector.reciprocal(RS1[:], RS1[:]).then_inc(rstd_made, 1)
            eng.wait_ge(rstd_made, n + 1)

        def dve_features(eng, A, n_tok, tok, rst, need, act_need, feature, wait_w, wait_a, norm2):
            bc = lambda c0: spread(PRM[:, c0:c0 + KT], n_tok)
            f = lambda ins: ins.then_inc(feature, 1)
            r_, k_ = R[:, :, tok], K[:, :, tok]
            f(tt(A["KQ"][:], k_, bc(KK_), MUL))
            need("KQ")
            f(tt(A["KSQ"][:], A["KQ"][:], A["KQ"][:], MUL))
            wait_w()
            f(ts(A["SG"][:], A["TW"][:], 0.5, 0.5, MUL, ADD))
            need("SG")
            f(nc.vector.tensor_tensor_scan(flat2(A["CS"]), rst, flat2(A["SG"]), 0.0, MUL, ADD))
            need("CS")
            f(tt(A["CX"][:], A["CS"][:], A["SG"][:], SUB))
            norm2()
            act_need("NR")
            f(nc.vector.reciprocal(A["NR"][:], A["NR"][:]))
            need("RI")
            f(tt(A["KK"][:], A["KQ"][:], A["NR"][:], MUL))
            need("KK")
            act_need("EX")
            f(stt(A["AT"][:], A["KK"][:], -1.0, A["EX"][:], MUL, MUL))
            wait_a()
            f(ts(A["AG"][:], A["TA"][:], 0.5, 0.5, MUL, ADD))
            need("AG")
            f(tt(A["BB"][:], A["KK"][:], A["AG"][:], MUL))
            need("BB")
            f(tt(A["BH"][:], A["BB"][:], A["EN"][:], MUL))
            f(ts(A["T1"][:], A["TA"][:], 0.5, 0.5, MUL, SUB))
            need("T1")
            f(tt(A["T1"][:], A["T1"][:], bc(KA_), MUL))
            need("T2")
            f(stt(A["KP"][:], A["T1"][:], 1.0, k_, ADD, MUL))
            need("KP")
            f(tt(A["KH"][:], A["KP"][:], A["EN"][:], MUL))
            f(tt(A["RT"][:], r_, A["EL"][:], MUL))

        def flat2(T3):
            return T3[:].rearrange("p a b -> p (a b)")

        def dve_features2(eng, A, n_tok, tok, chunk, need, feature):
            f = lambda ins: ins.then_inc(feature, 1)
            n = n_tok // chunk
            end = A["EL"][:].rearrange("p g (c t) -> p g c t", t=chunk)[:, :, :, chunk - 1:chunk]\
                .to_broadcast([P, KT, n, chunk])
            v4 = lambda T3: T3[:].rearrange("p g (c t) -> p g c t", t=chunk)
            f(tt(v4(A["BD"]), v4(A["BH"]), end, MUL))
            f(tt(v4(A["KD"]), v4(A["KH"]), end, MUL))
            f(tt(A["Z"][:], R[:, :, tok], A["KP"][:], MUL))
            need("Z")
            f(tt(A["Z"][:], A["Z"][:], spread(PRM[:, RK_:RK_ + KT], n_tok), MUL))

        def prep_steps(eng, i):
            tok0 = 0 if i is None else i * P + P
            tok = bass.ds(tok0, P)
            A = WT
            bc = lambda c0: spread(PRM[:, c0:c0 + KT], P)
            f = lambda ins: ins.then_inc(dve_prep, 1)
            need = lambda name: eng.wait_ge(dve_prep, prep_count(i, DVE_PREP, name))
            made = lambda name: eng.wait_ge(act_prep, prep_count(i, ACT_PREP, name))
            gc = lambda T3: T3[:].rearrange("p g (c t) -> p (g c) t", c=2)

            def KQ():
                f(tt(A["KQ"][:], K[:, :, tok], bc(KK_), MUL))

            def KSQ():
                need("KQ")
                f(tt(A["KSQ"][:], A["KQ"][:], A["KQ"][:], MUL))

            def SG():
                w_kept(eng, i, "wpre")
                f(ts(A["SG"][:], A["TW"][:], 0.5, 0.5, MUL, ADD))

            def CS():
                need("SG")
                f(nc.vector.tensor_tensor_scan(flat2(A["CS"]), RST[:, 0:KT * P], flat2(A["SG"]), 0.0, MUL, ADD))

            def CX():
                need("CS")
                f(tt(A["CX"][:], A["CS"][:], A["SG"][:], SUB))

            def T1():
                w_kept(eng, i, "apre")
                f(stt(A["T1"][:], A["TA"][:], -1.0, spread(HKA[:], P), ADD, MUL))

            def KP():
                need("T1")
                f(stt(A["KP"][:], A["T1"][:], 1.0, K[:, :, tok], ADD, MUL))

            def MAX_():
                j = jw(i, "norm2")
                w_filled(eng, i, "norm2")
                ts(NRM[:], bank(j, 0)[0:NH, 0:P], 1e-24, None, MAX).then_inc(emptied[j % 4], 2)

            def RI():
                made("NR")
                f(nc.vector.reciprocal(NRM[:], NRM[:]))

            def KK():
                for h in range(2):
                    w_filled(eng, i, "norm3", h)
                    pairs = slice(4 * h, 4 * h + 4)
                    tt(A["KK"][:, pairs, :], A["KQ"][:, pairs, :], bank(jw(i, "norm3"), h).rearrange("p (a b) -> p a b", a=4), MUL)\
                        .then_inc(emptied[jw(i, "norm3") % 4], 1)

            def BB():
                w_kept(eng, i, "norm3")
                made("EX")
                need("T1")
                f(stt(A["BB"][:], A["TA"][:], 1.0, A["KK"][:], ADD, MUL))

            def BH():
                need("BB")
                made("EN")
                f(stt(BKH[:, :, 0, :], gc(A["BB"]), 0.5, gc(A["EN"]), MUL, MUL))

            def KH():
                need("KP")
                f(tt(BKH[:, :, 1, :], gc(A["KP"]), gc(A["EN"]), MUL))

            end = gc(A["EL"])[:, :, HD - 1:HD].to_broadcast([P, 2 * KT, HD])

            def BD():
                need("BH")
                need("KH")
                made("EL")
                f(tt(BKD[:, :, 0, :], BKH[:, :, 0, :], end, MUL))

            def KD():
                f(tt(BKD[:, :, 1, :], BKH[:, :, 1, :], end, MUL))

            def Z():
                f(tt(A["Z"][:], R[:, :, tok], A["KP"][:], MUL))

            def ZR():
                need("Z")
                f(tt(A["Z"][:], A["Z"][:], bc(RK_), MUL))

            def AT():
                w_kept(eng, i, "norm3")
                f(stt(AR[:, :, 0, :], gc(A["KK"]), -1.0, gc(A["EX"]), MUL, MUL))

            def ELE_():
                f(nc.vector.tensor_copy(ELE[:], A["EL"][:].rearrange("p g (c t) -> p g c t", c=2)[:, :, :, HD - 1]))

            def RT():
                for c in range(2):
                    ins = tt(AR[:].rearrange("p (g c) x t -> p g c x t", c=2)[:, :, c, 1, :],
                             R[:, :, bass.ds(tok0 + c * HD, HD)], A["EL"][:, :, c * HD:(c + 1) * HD], MUL)
                f(ins)

            return dict(KQ=KQ, KSQ=KSQ, SG=SG, CS=CS, CX=CX, T1=T1, KP=KP, MAX=MAX_, RI=RI, KK=KK, BB=BB, BH=BH, KH=KH,
                        BD=BD, KD=KD, Z=Z, ZR=ZR, AT=AT, ELE=ELE_, RT=RT)

        def dve_tile(eng, i, last=False):
            steps = {} if last else prep_steps(eng, i)

            def prep(*names):
                if not last:
                    for name in names:
                        steps[name]()

            A = WT
            m3 = lambda T4, h: T4[:, h]
            b3 = lambda name, h: bank(jw(i, name), h).rearrange("p (a b) -> p a b", a=8)

            def added(name):
                for h in range(2):
                    w_filled(eng, i, name, h)
                    tt(m3(XT_, h), m3(XT_, h), b3(name, h), ADD).then_inc(emptied[jw(i, name) % 4], 1)

            over2 = lambda ap, a, b: ap.unsqueeze(1).unsqueeze(1).to_broadcast([ap.shape[0], a, b, ap.shape[1]])
            for q in range(4):
                j = jw(i, f"Q{q}")
                w_filled(eng, i, f"Q{q}")
                for dst, mask in ((A["P1T"], "U8"), (A["OT"], "UO")):
                    for c in range(2):
                        src = both(j)[0:HD].rearrange("s p (g c x t) -> s p g c x t", g=2, c=2, x=2)[:, :, :, c, 0, :]
                        tt(dst[c * HD:(c + 1) * HD, :, 2 * q:2 * q + 2, :], src, over2(CC[mask][0:HD], 2, 2), MUL)
                src = both(j).rearrange("s p (e x t) -> s p e x t", e=4, x=2)
                tt(NT[HD:P, :, 4 * q:4 * q + 4, :], src[HD:P, :, :, 0, :], over2(CC["US"][HD:P], 2, 4), MUL)
                tt(RBK[:, :, 4 * q:4 * q + 4, :], src[:, :, :, 1, :], over2(CC["UI"], 2, 4), MUL)\
                    .then_inc(emptied[j % 4], 2)
            for h in range(2):
                w_filled(eng, i, "M", h)
                tt(m3(A["P1"], h), b3("M", h), over(CC["L8"], 8), MUL).then_inc(emptied[jw(i, "M") % 4], 1)
            w_kept(eng, i, "Q3")
            for h in range(2):
                tt(m3(XT_, h), m3(A["P1T"], h), over(CC["I64"], 8), ADD).then_inc(dve_sum, 1)
            eng.wait_ge(vc_made, i + 1)
            for h in range(2):
                w_filled(eng, i, "bonus", h)
                vv = V[:, 4 * h:4 * h + 4, bass.ds(i * P, P)]
                tt(vv, vv, bank(jw(i, "bonus"), h).rearrange("p (a b) -> p a b", a=4), MUL)\
                    .then_inc(emptied[jw(i, "bonus") % 4], 1)
            prep("KQ")
            w_kept(eng, i, "M")
            w_filled(eng, i, "M")
            prep("KSQ")
            w_sum(eng, i, "XT1b")
            added("XT2")
            w_kept(eng, i, "XT2")
            added("XT3")
            prep("SG", "CS", "CX", "T1", "KP")
            w_kept(eng, i, "XT3")
            for h in range(2):
                j = jw(i, "T1" + "ab"[h])
                w_filled(eng, i, "T1" + "ab"[h])
                xt = FX[:, h].rearrange("p (b a) x n -> p b a x n", b=2)[:, :, :, 1, :]
                tt(xt, xt, both(j).rearrange("p b (a x) -> p b a x", a=4)[:, :, :, HD:P], ADD).then_inc(emptied[j % 4], 1)
            prep("MAX")
            for h in range(2):
                w_kept(eng, i, "T1" + "ab"[h], 0)
            added("T2")
            prep("RI")
            w_kept(eng, i, "T2")
            added("T3")
            for c in range(2):
                rows = slice(c * HD, (c + 1) * HD)
                j = jw(i, f"AS{c}")
                w_filled(eng, i, f"AS{c}")
                w_kept(eng, i, "NV")
                g = A["NV"][rows]
                tt(g, g, both(j)[rows].rearrange("p b (a n) -> p b a n", a=KT), ADD).then_inc(emptied[j % 4], 2)
                if c == 1:
                    w_kept(eng, i, "SY0")
                tt(STD[:], ST[:], spread(ELE[:, :, c], HD), MUL).then_inc(dve_sum, 1)
                if c == 0:
                    prep("KK", "BB", "BH", "KH")
                else:
                    prep("AT")
                w_sum(eng, i, f"STD{c}")
                w_filled(eng, i, f"SY{c}")
                tt(ST[:], STD[:], bank(jw(i, f"SY{c}"), 1).rearrange("p (a b) -> p a b", a=KT), ADD)\
                    .then_inc(emptied[jw(i, f"SY{c}") % 4], 1)
                if c == 0:
                    prep("BD", "KD", "Z", "ZR")
                else:
                    prep("ELE", "RT")
            w_kept(eng, i, "SY1")
            for h in range(2):
                w_filled(eng, i, "YU", h)
                rr = R[:, :, bass.ds(i * P + h * HD, HD)]
                tt(rr, rr, bank(jw(i, "YU"), h).rearrange("p (a b) -> p a b", a=KT), ADD)\
                    .then_inc(emptied[jw(i, "YU") % 4], 1)

        def dve_samples(eng):
            A = SM
            need = lambda name: s_dve(eng, name)
            f = lambda ins: ins.then_inc(smp_dve, 1)
            tok = slice(SEQ, T)
            s8 = lambda j: bank(j, 0)[:, 0:KT * NS].rearrange("p (a b) -> p a b", a=KT)
            eng.wait_ge(emptied[J_STO % 4], 2 * (J_STO // 4) + 2)

            def norm2():
                j = js("norm2")
                wait_filled(eng, j)
                ts(A["NR"][:], s8(j), 1e-24, None, MAX).then_inc(emptied[j % 4], 2)

            dve_features(eng, A, NS, tok, RST[:, KT * P:], need, lambda n: s_act(eng, n), smp_dve,
                         lambda: wait_emptied(eng, js("wpre")), lambda: wait_emptied(eng, js("apre")), norm2)
            small = lambda j, rows: both(j, KT * NS)[rows].rearrange("p e (a b) -> p e a b", a=KT)
            c4 = lambda name, rows: CC[name][rows].unsqueeze(1).to_broadcast([rows.stop - rows.start, KT, NS])
            bs, ks, bks = slice(0, NS), slice(NS, 2 * NS), slice(0, 2 * NS)
            j = js("Q")
            wait_filled(eng, j)
            for e in range(2):
                src = bank(j, e)[bks].rearrange("p (a x b) -> p a x b", a=KT, x=2)
                tt(A["P1T"][bs, e], src[bs, :, 0, :], c4("SU", bs), MUL)
                tt(A["NT"][ks, e], src[ks, :, 0, :], c4("SU", ks), MUL)
                tt(A["RBK"][:, e], src[:, :, 1, :], c4("SUI", bks), MUL).then_inc(emptied[j % 4], 1)
            j = js("M")
            wait_filled(eng, j)
            for e in range(2):
                tt(A["P1"][bs, e], small(j, bs)[:, e], c4("SL", bs), MUL).then_inc(emptied[j % 4], 1)
            dve_features2(eng, A, NS, tok, DS, need, smp_dve)
            wait_emptied(eng, js("Q"))
            for e in range(2):
                ins = tt(A["XT"][bs, e], A["P1T"][bs, e], c4("SI", bs), ADD)
            f(ins)
            need("XT1")
            wait_filled(eng, js("XT2"))
            for e in range(2):
                tt(A["XT"][bs, e], A["XT"][bs, e], small(js("XT2"), bs)[:, e], ADD).then_inc(emptied[js("XT2") % 4], 1)
            j = js("bonus")
            wait_filled(eng, j)
            tt(V[:, :, tok], V[:, :, tok], s8(j), MUL).then_inc(emptied[j % 4], 2)
            f(nc.vector.tensor_copy(A["DC"][:], A["EL"][:].rearrange("p g (b t) -> p g b t", t=DS)[:, :, :, DS - 1]))
            need("DC")
            j = js("GY")
            wait_emptied(eng, j, 0)
            kinds = bank(j, 0).rearrange("p (x a n) -> p x a n", x=2, a=KT)
            nc.vector.tensor_copy(R[:, :, tok], kinds[:, 1])
            tt(A["GT"][:], A["GT"][:], kinds[:, 0], ADD).then_inc(emptied[j % 4], 1)
            for q in range(4):
                st = S0T[:, 2 * q:2 * q + 2]
                decay = A["DC"][:, :, 2 * q:2 * q + 2].rearrange("p g b -> p b g").unsqueeze(3).to_broadcast([P, 2, KT, HD])
                f(tt(st, st, decay, MUL))
            wait_filled(eng, js("YU"))
            wait_emptied(eng, js("GY"))
            tt(R[:, :, tok], R[:, :, tok], s8(js("YU")), ADD).then_inc(emptied[js("YU") % 4], 2)
            for q in range(4):
                j = js(f"SS{q}")
                need(f"SW{q}")
                wait_filled(eng, j)
                for h in range(2):
                    st = S0T[:, 2 * q:2 * q + 2, 4 * h:4 * h + 4, :]
                    tt(st, st, bank(j, h).rearrange("p (a b v) -> p b a v", a=4, b=2), ADD).then_inc(emptied[j % 4], 1)

        def dve_ffn(eng, l, i, last, norm=None):
            u0, j0 = ((U_F0, J_F0), (U_F1, J_F1))[l]
            h0 = KT * CHUNKS * l
            for q in range(8):
                if not (last and q == 7):
                    dve_split(eng, u0 + q + 1, i)
                if norm and q > 4:
                    for k in (2 * q - 10, 2 * q - 9):
                        dve_add_square(eng, norm, k)
                for m in (2 * q, 2 * q + 1):
                    j = j0 + m
                    if q < 4:
                        eng.wait_ge(filled, i * (2 * FFN_J) + 2 * j + 2)
                        if m >= 2:
                            eng.wait_ge(square_made, i * KT + (h0 + m - 1))
                        stt(halves(RL[:, m % 2, :]), both(j, TH), 0.0, halves(RS1[:]), MAX, MUL)\
                            .then_inc(emptied[j % 4], 2)
                        if m >= 1:
                            dve_hidden_lo(eng, i, h0, m - 1)
                    else:
                        eng.wait_ge(filled, i * (2 * FFN_J) + 2 * j + 2)
                        tt(halves(X[:, m - 8, :]), halves(X[:, m - 8, :]), both(j, TH), ADD).then_inc(emptied[j % 4], 2)
                if q == 3:
                    dve_hidden_lo(eng, i, h0, 7)

        def dve_hidden_lo(eng, i, h0, m):
            eng.wait_ge(hhi_made, i * KT + (h0 + m + 1))
            tt(HL[:, m, :], QL[:, m % 2, :], HH[:, m, :].bitcast(F32), SUB).then_inc(hlo_made, 1)

        def run_dve(eng):
            nc.vector.memset(ST[:], 0.0).then_inc(pads_made, 1)
            nc.vector.memset(H[:, :, 0:1], 0.0).then_inc(pads_made, 1)
            for n in range(5):
                j, w = J_X + n, P if n < 4 else NS
                wait_filled(eng, j)
                for h in range(2):
                    nc.vector.tensor_copy(X[:, 4 * h:4 * h + 4, n * P:n * P + w],
                                          bank(j, h)[:, 0:4 * w].rearrange("p (a b) -> p a b", a=4))\
                        .then_inc(emptied[j % 4], 1)
            wait_emptied(eng, J_PRM)
            nc.vector.tensor_copy(H[:, :, 513:553].rearrange("p k (b t) -> p k b t", b=NB)[:, :, :, 0],
                                  PRM2[:, SHF:SHF + 64].rearrange("p (b k) -> p k b", b=NB)).then_inc(pads_made, 1)
            ts(HKA[:], PRM[:, KA_:KA_ + KT], 0.5, None, MUL).then_inc(pads_made, 1)
            eng.wait_ge(ss_made, 6)
            nc.vector.reciprocal(SS[:, 0:4], SS[:, 0:4])
            nc.vector.reciprocal(SS[0:NS, 4:5], SS[0:NS, 4:5]).then_inc(rstd_made, 1)
            eng.wait_ge(rstd_made, 1)
            for n in range(5):
                w = P if n < 4 else NS
                ts(DG0[0:w, n, 0:w], ident[0:w, 0:w], SS[0:w, n:n + 1], None, MUL).then_inc(diag_made, 1)
            eng.wait_ge(raw_loaded[0], 16)
            eng.wait_ge(a1_loaded, 16)
            for c0, n in ((0, 3), (LW, 4)):
                ins = tt(RAW[0][:, :, LW + LA + c0:LW + LA + c0 + LW], RAW[0][:, :, c0:c0 + LW],
                         spread(PRM[:, MIX + 8 * n:MIX + 8 * n + KT], LW), MUL)
            ins.then_inc(scaled_made, 1)
            dve_split(eng, U_WA)
            wait_emptied(eng, J_N0)
            for n in range(5):
                wait_emptied(eng, J_X + n)
            eng.wait_ge(pads_made, 3)

            def normed(k):
                stt(H[:, k, 1:513], X[:, k, 0:SEQ], col(NMIX + k), RS0[:, 0:SEQ], MUL, MUL)
                stt(samples(H[:, k, 513:553], 1, DS), samples(X[:, k, SEQ:T], 0, DS), col(NMIX + k),
                    samples(RS0[:, SEQ:T], 0, DS), MUL, MUL).then_inc(hn_made, 1)

            def shift_diff(k):
                if k == 0:
                    eng.wait_ge(hn_made, KT)
                tt(DX[:, k, 0:SEQ], H[:, k, 0:SEQ], H[:, k, 1:513], SUB)
                tt(samples(DX[:, k, SEQ:T], 0, DS), samples(H[:, k, 513:553], 0, DS), samples(H[:, k, 513:553], 1, DS),
                   SUB).then_inc(dx_made, 1)

            def mixed(n):
                jx, k = n // 8, n % 8
                if n >= 2 * KT + 2:
                    eng.wait_ge(xlo_made, n - 1)
                m = col(MIX + 8 * (jx - 2) + k)
                stt(XF[:, n % 2, 0:SEQ], DX[:, k, 0:SEQ], m, H[:, k, 1:513], MUL, ADD)
                stt(samples(XF[:, n % 2, SEQ:T], 0, DS), samples(DX[:, k, SEQ:T], 0, DS), m,
                    samples(H[:, k, 513:553], 1, DS), MUL, ADD).then_inc(xf_made, 1)

            def ahead(n):
                if n < KT:
                    normed(n)
                elif n < 2 * KT:
                    shift_diff(n - KT)
                elif n < XS_TILES:
                    if n == 2 * KT:
                        eng.wait_ge(dx_made, KT)
                    mixed(n)

            def xs_lo(n):
                jx, k = n // 8, n % 8
                eng.wait_ge(xhi_made, n + 1)
                hi, lo = XSH[jx % 2][:, k, :].bitcast(F32), XSL[jx % 2][:, k, :]
                if jx == 0:
                    tt(lo[:, 0:SEQ], H[:, k, 1:513], hi[:, 0:SEQ], SUB)
                    tt(samples(lo[:, SEQ:T], 0, DS), samples(H[:, k, 513:553], 1, DS), samples(hi[:, SEQ:T], 0, DS),
                       SUB).then_inc(xlo_made, 1)
                else:
                    tt(lo, DX[:, k, :] if jx == 1 else XF[:, n % 2, :], hi, SUB).then_inc(xlo_made, 1)
                if n == KT - 1:
                    nc.vector.memset(WH[LW:LW + 1, :], 1.0).then_inc(pads_made, 1)
                    nc.vector.memset(AH[LA:LA + 1, :], 1.0).then_inc(pads_made, 1)
                    nc.vector.tensor_copy(SHT[:, :, 0:1], H[:, :, 512:513])
                    nc.vector.tensor_copy(SHT[:, :, 1:9], H[:, :, 513:553].rearrange("p k (b t) -> p k b t", b=NB)
                                          [:, :, :, DS]).then_inc(sht_made, 1)

            ahead(0)
            first = prep_steps(eng, None)
            for what, n in timeline():
                if what == "split":
                    dve_split(eng, n)
                elif what == "first":
                    if n == "squares":
                        wait_emptied(eng, J_K + 7)
                    if n == "exps":
                        eng.wait_ge(resets_loaded, 16)
                    if n == "late":
                        first["KK"]()
                        wait_filled(eng, jv("V5"))
                    late = FIRST[DVE_PREP][6:-3]
                    for name in {"late": late, "squares": ("KQ", "KSQ"), "exps": ("SG", "CS", "CX"), "root": ("MAX", "RI")}.get(n, ()):
                        first[name]()
                elif what == "xs":
                    ahead(n + 1)
                    xs_lo(n)
                elif n in (J_G1, J_G1 + 1):
                    wait_emptied(eng, n)
                    g = GH[:, 0, :] if n == J_G1 else GH[0:LG - P, 1, :]
                    ts(g, g, 0.5, 0.5, MUL, ADD).then_inc(gsig_made, 1)
            wait_filled(eng, jv("V7"))
            for name in FIRST[DVE_PREP][-3:]:
                first[name]()
            with eng.Fori(0, TILES - 1) as i:
                dve_tile(eng, i)
            dve_tile(eng, TILES - 1, last=True)
            dve_samples(eng)
            for k in range(KT):
                j = jg("mean", k)
                wait_filled(eng, j)
                tt(halves(R[:, k, :]), halves(R[:, k, :]), both(j, TH), SUB).then_inc(emptied[j % 4], 2)
            dve_split(eng, U_WO)
            wait_emptied(eng, jg("var", 0))
            nc.vector.reciprocal(GR[:], GR[:]).then_inc(gn_rstd, 1)
            for n in range(KT + 2):
                if n < KT:
                    j = jg("spread", n)
                    if n == 0:
                        wait_emptied(eng, jg("mean", KT - 1))
                    wait_filled(eng, j)
                    stt(halves(R[:, n, :]), halves(R[:, n, :]), col(GNW + n), both(j, TH), MUL, MUL)\
                        .then_inc(emptied[j % 4], 2)
                if 1 <= n <= KT:
                    k = n - 1
                    wait_emptied(eng, jg("spread", k))
                    stt(R[:, k, :], R[:, k, :], col(GNB + k), V[:, k, :], ADD, ADD).then_inc(gn_step, 1)
                    if k == 0:
                        wait_emptied(eng, jg("gate", KT - 1))
                    eng.wait_ge(gn_step, k + 1)
                    tt(R[:, k, :], R[:, k, :], GG[:, k, :], MUL).then_inc(gn_gated, 1)
                if n >= 2:
                    eng.wait_ge(gn_hi, n - 1)
                    tt(XSL[1][:, n - 2, :], R[:, n - 2, :], XSH[1][:, n - 2, :].bitcast(F32), SUB).then_inc(gn_lo, 1)
            for n in range(4):
                dve_split(eng, U_WO + n + 1)
                for m in (2 * n, 2 * n + 1):
                    j = J_WO + m
                    wait_filled(eng, j)
                    tt(halves(X[:, m, :]), halves(X[:, m, :]), both(j, TH), ADD).then_inc(emptied[j % 4], 2)
                for k in (2 * n - 2, 2 * n - 1) if n else ():
                    dve_gained_lo(eng, 1, k, NFFN)
                    dve_add_square(eng, 1, k)
            for k in (6, 7):
                dve_gained_lo(eng, 1, k, NFFN)
            dve_rstd(eng, 1, J_N1)
            with eng.Fori(0, CHUNKS - 1) as i:
                dve_ffn(eng, 0, i, False)
            dve_ffn(eng, 0, CHUNKS - 1, False, 2)
            wait_filled(eng, J_N2)
            nc.vector.memset(EXT[:, :, 0:PBUF], 0.0)
            dve_rstd(eng, 2, J_N2)
            wins = [0]

            def win(ins):
                ins.then_inc(pool_win, 1)
                wins[0] += 1
                eng.wait_ge(pool_win, wins[0])

            def pool_group(gi):
                g = GROUP_ORDER[gi]
                w = POOLS[g]
                for k in (2 * g, 2 * g + 1):
                    stt(EXT[:, k, PBUF:S0_], X[:, k, 0:SEQ], col(NMIX + 8 + k), RS1[:, 0:SEQ], MUL, MUL)
                    stt(samples(EXT[:, k, S0_:], PBUF, DS), samples(X[:, k, SEQ:T], 0, DS), col(NMIX + 8 + k),
                        samples(RS1[:, SEQ:T], 0, DS), MUL, MUL).then_inc(hn_made, 1)
                if gi == 0:
                    wait_emptied(eng, J_PST)
                else:
                    eng.wait_ge(pool_diff, 2 * gi)
                eng.wait_ge(hn_made, KT + 2 * gi + 2)
                src = EXT[:, 2 * g:2 * g + 2, :]
                step, b = 1, 0
                while step < w:
                    dst = WS[b][:]
                    win(tt(dst[:, :, 2 * step - 1:], src[:, :, 2 * step - 1:], src[:, :, step - 1:-step], ADD))
                    src, step, b = dst, 2 * step, 1 - b
                for kk in range(2):
                    k = 2 * g + kk
                    head = src[:, kk, PBUF:PBUF + 16]
                    win(tt(head, head, CC[f"corr{w}"], MUL))
                    stt(DF[:, k, 0:SEQ], src[:, kk, PBUF:S0_], 1.0 / w, EXT[:, k, PBUF:S0_], MUL, SUB)
                    stt(samples(DF[:, k, SEQ:T], 0, DS), samples(src[:, kk, S0_:], PBUF, DS), 1.0 / w,
                        samples(EXT[:, k, S0_:], PBUF, DS), MUL, SUB).then_inc(pool_diff, 1)

            def pool_out(gi):
                for m in POOL_ORDER[2 * gi:2 * gi + 2]:
                    j = jpw(m)
                    wait_filled(eng, j)
                    stt(halves(X[:, m, :]), both(j, TH), PRM2[:, PSC + m:PSC + m + 1], halves(X[:, m, :]), MUL, ADD)\
                        .then_inc(emptied[j % 4], 2)

            for gi in range(4):
                pool_group(gi)
                if gi >= 2:
                    pool_out(gi - 2)
            pool_out(2)
            dve_split(eng, U_F1)
            pool_out(3)
            for k in POOL_ORDER:
                dve_gained_lo(eng, 3, k, NFFN + 8)
            dve_rstd(eng, 3, J_N3)
            with eng.Fori(0, CHUNKS - 1) as i:
                dve_ffn(eng, 1, i, False)
            dve_ffn(eng, 1, CHUNKS - 1, True, 4)
            wait_filled(eng, J_YT)
            nc.vector.reciprocal(YR[:, 0:4], bank(J_YT, 0)[:, 0:4]).then_inc(emptied[J_YT % 4], 1)
            nc.vector.reciprocal(YR[0:NS, 4:5], bank(J_YT, 0)[0:NS, 4:5]).then_inc(emptied[J_YT % 4], 1)

        block = ctx.enter_context(nc.Block())

        @block.sync
        def _(sp):
            run_sp(sp)

        @block.tensor
        def _(pe):
            run_pe(pe)

        @block.scalar
        def _(eng):
            run_act(eng)

        @block.vector
        def _(eng):
            run_dve(eng)


OUTS = (("y_prompt", (1, SEQ, D)), ("y_sample", (NB, DS, D)), ("wkv_prompt", (1, 1, NH, HD, HD)),
        ("shift_prompt", (1, 1, D)), ("pool_prompt", (1, 1, PBUF, D)), ("wkv_sample", (1, NB, NH, HD, HD)),
        ("shift_sample", (1, NB, D)), ("pool_sample", (1, NB, PBUF, D)))
UNUSED = ("rwkv_v0", "rwkv_v1", "rwkv_v2")


def kernel(**inputs):
    import numpy as np
    import concourse.bacc as bacc
    from concourse import mybir
    from concourse.bass_utils import run_bass_kernel_spmd

    nc = bacc.Bacc("TRN2", target_bir_lowering=False, num_devices=1)
    table, _, resets, head_rows = constants()
    arrays = {n: np.ascontiguousarray(v) for n, v in inputs.items() if n not in UNUSED}
    arrays |= {"const_table": table, "resets": resets, "head_rows": head_rows}
    a = {n: nc.dram_tensor(f"in_{n}", v.shape, mybir.dt.from_np(v.dtype), kind="ExternalInput").ap()
         for n, v in arrays.items()}
    o = {n: nc.dram_tensor(f"out_{n}", s, mybir.dt.float32, kind="ExternalOutput").ap() for n, s in OUTS}
    build(nc, a, o)
    r = run_bass_kernel_spmd(nc, [{f"in_{n}": v for n, v in arrays.items()}], core_ids=[0])
    return tuple(r.results[0][f"out_{n}"] for n, _ in OUTS)
```
